# Optimizing a Trainium2 kernel written in Bass

```python
import math
import jax, jax.numpy as jnp
from jax import lax
import numpy as np

D_MODEL = 1024
BATCH = 1
SEQ = 256
DEPTH = 2
DEC_BATCH = 8
DEC_SEQ = 8
PAST_LEN = 2048
PAGE_SIZE = 128

D_RNN = D_MODEL
N_RNN_HEADS = 16
RNN_BLOCK = D_RNN // N_RNN_HEADS
RG_CONV_W = 4
RG_C = 8.0
D_CONV = D_MODEL
CC_CONV_W = 31
D_FF = 2816
N_EXPERTS = 8
TOP_K = 2
D_FF_EXPERT = 1408
N_DENSE = (DEPTH + 1) // 2
N_MOE = DEPTH // 2
D_IN = 2 * D_RNN + 2 * D_CONV + 2 * D_MODEL
EPS = 1e-6

kernel_name = "hybrid_rglru_conformer_adaln_moe_step"

def rmsnorm(x, g):
    xf = x.astype(jnp.float32)
    y = xf * lax.rsqrt(jnp.mean(xf * xf, axis=-1, keepdims=True) + EPS)
    return (y * g.astype(jnp.float32)).astype(x.dtype)

def layernorm(x, g, b):
    xf = x.astype(jnp.float32)
    mu = jnp.mean(xf, axis=-1, keepdims=True)
    xc = xf - mu
    y = xc * lax.rsqrt(jnp.mean(xc * xc, axis=-1, keepdims=True) + EPS)
    return (y * g.astype(jnp.float32) + b.astype(jnp.float32)).astype(x.dtype)

def causal_depthwise_conv(u, buf, w, b):
    K, C = w.shape
    full = jnp.concatenate([buf.astype(u.dtype), u], axis=1)
    y = lax.conv_general_dilated(full, w.astype(u.dtype)[:, None, :], window_strides=(1,),
                                 padding="VALID", dimension_numbers=("NWC", "WIO", "NWC"),
                                 feature_group_count=C)
    return y + b.astype(u.dtype), full[:, full.shape[1] - (K - 1):]

def rg_lru(x, h0, wa, ba, wx, bx, lam):
    B, T, Dr = x.shape
    xf = x.astype(jnp.float32)
    xh = xf.reshape(B, T, N_RNN_HEADS, RNN_BLOCK)
    r = jax.nn.sigmoid(jnp.einsum("bthi,hij->bthj", xh, wa.astype(jnp.float32)).reshape(B, T, Dr) + ba.astype(jnp.float32))
    i = jax.nn.sigmoid(jnp.einsum("bthi,hij->bthj", xh, wx.astype(jnp.float32)).reshape(B, T, Dr) + bx.astype(jnp.float32))
    log_a = -RG_C * r * jax.nn.softplus(-lam.astype(jnp.float32))
    a = jnp.exp(log_a)
    bterm = jnp.sqrt(-jnp.expm1(2.0 * log_a)) * (i * xf)
    bterm = bterm.at[:, 0].add(a[:, 0] * h0.astype(jnp.float32))

    def combine(left, right):
        a1, b1 = left
        a2, b2 = right
        return a1 * a2, a2 * b1 + b2

    _, h = lax.associative_scan(combine, (a, bterm), axis=1)
    return h.astype(x.dtype), h[:, -1].astype(x.dtype)

def swiglu(x, wg, wu, wd):
    return (jax.nn.silu(x @ wg) * (x @ wu)) @ wd

def moe_swiglu(x, wr, br, wg, wu, wd):
    B, T, D = x.shape
    xt = x.reshape(B * T, D)
    logits = xt.astype(jnp.float32) @ wr.astype(jnp.float32) + br.astype(jnp.float32)
    probs = jax.nn.softmax(logits, axis=-1)
    topv, topi = lax.top_k(probs, TOP_K)
    topv = topv / jnp.sum(topv, axis=-1, keepdims=True)
    comb = jnp.sum(jax.nn.one_hot(topi, N_EXPERTS, dtype=jnp.float32) * topv[..., None], axis=1)
    out = jnp.zeros((B * T, D), jnp.float32)
    for e in range(N_EXPERTS):
        out = out + comb[:, e:e + 1] * swiglu(xt, wg[e], wu[e], wd[e]).astype(jnp.float32)
    return out.astype(x.dtype).reshape(B, T, D)

def trunk(x, c, h_state, rc_state, cc_state, p):
    splits = [D_RNN, 2 * D_RNN, 2 * D_RNN + D_CONV, 2 * D_RNN + 2 * D_CONV, 2 * D_RNN + 2 * D_CONV + D_MODEL]
    new_h, new_rc, new_cc = [], [], []
    for l in range(DEPTH):
        mod = jax.nn.silu(c) @ p["ada_w"][l] + p["ada_b"][l]
        sh1, sc1, g1, sh2, sc2, g2 = jnp.split(mod[:, None, :], 6, axis=-1)
        hn = rmsnorm(x, p["norm1_g"][l]) * (1.0 + sc1) + sh1
        proj = hn @ p["w_in"][l]
        xr, yr, ga, gb, gate_a, gate_b = jnp.split(proj, splits, axis=-1)
        xc, rc_new = causal_depthwise_conv(xr, rc_state[l], p["rg_conv_w"][l], p["rg_conv_b"][l])
        hseq, h_last = rg_lru(xc, h_state[l], p["rg_wa"][l], p["rg_ba"][l], p["rg_wx"][l], p["rg_bx"][l], p["rg_lambda"][l])
        ya = (jax.nn.gelu(yr) * hseq) @ p["w_branch_a"][l]
        u = ga * jax.nn.sigmoid(gb)
        v, cc_new = causal_depthwise_conv(u, cc_state[l], p["cc_dw_w"][l], p["cc_dw_b"][l])
        v = jax.nn.silu(layernorm(v, p["cc_ln_g"][l], p["cc_ln_b"][l]))
        yb = v @ p["w_branch_b"][l] + p["b_branch_b"][l]
        m = jax.nn.sigmoid(gate_a) * ya + jax.nn.sigmoid(gate_b) * yb
        x = x + (1.0 + g1) * (m @ p["w_out"][l])
        hn2 = rmsnorm(x, p["norm2_g"][l]) * (1.0 + sc2) + sh2
        if l % 2 == 0:
            j = l // 2
            f = swiglu(hn2, p["ffn_w_gate"][j], p["ffn_w_up"][j], p["ffn_w_down"][j])
        else:
            j = l // 2
            f = moe_swiglu(hn2, p["moe_router_w"][j], p["moe_router_b"][j], p["moe_w_gate"][j],
                           p["moe_w_up"][j], p["moe_w_down"][j])
        x = x + (1.0 + g2) * f
        new_h.append(h_last)
        new_rc.append(rc_new)
        new_cc.append(cc_new)
    y = rmsnorm(x, p["final_norm_g"])
    return y, jnp.stack(new_h), jnp.stack(new_rc), jnp.stack(new_cc)

def setup_inputs(seed: int = 0) -> dict:
    key = jax.random.key(seed)
    ks = iter(jax.random.split(key, 48))
    nrm = lambda shape, s: jax.random.normal(next(ks), shape, jnp.float32) * s
    D = D_MODEL
    u = jax.random.uniform(next(ks), (DEPTH, D_RNN), jnp.float32, 0.9, 0.999)
    a0 = u ** (1.0 / RG_C)
    rg_lambda = jnp.log(a0) - jnp.log1p(-a0)
    return {
        "x_prompt": nrm((BATCH, SEQ, D), 1.0),
        "x_sample": nrm((DEC_BATCH, DEC_SEQ, D), 1.0),
        "c_prompt": nrm((BATCH, D), 1.0),
        "c_sample": nrm((DEC_BATCH, D), 1.0),
        "state_rglru_h": nrm((DEPTH, DEC_BATCH, D_RNN), 0.5),
        "state_rglru_conv": nrm((DEPTH, DEC_BATCH, RG_CONV_W - 1, D_RNN), 1.0),
        "state_cconv": nrm((DEPTH, DEC_BATCH, CC_CONV_W - 1, D_CONV), 0.5),
        "ada_w": nrm((DEPTH, D, 6 * D), 0.5 * D ** -0.5),
        "ada_b": nrm((DEPTH, 6 * D), 0.02),
        "norm1_g": 1.0 + nrm((DEPTH, D), 0.02),
        "norm2_g": 1.0 + nrm((DEPTH, D), 0.02),
        "w_in": nrm((DEPTH, D, D_IN), D ** -0.5),
        "rg_conv_w": nrm((DEPTH, RG_CONV_W, D_RNN), RG_CONV_W ** -0.5),
        "rg_conv_b": nrm((DEPTH, D_RNN), 0.02),
        "rg_wa": nrm((DEPTH, N_RNN_HEADS, RNN_BLOCK, RNN_BLOCK), RNN_BLOCK ** -0.5),
        "rg_ba": nrm((DEPTH, D_RNN), 0.02),
        "rg_wx": nrm((DEPTH, N_RNN_HEADS, RNN_BLOCK, RNN_BLOCK), RNN_BLOCK ** -0.5),
        "rg_bx": nrm((DEPTH, D_RNN), 0.02),
        "rg_lambda": rg_lambda,
        "w_branch_a": nrm((DEPTH, D_RNN, D), D_RNN ** -0.5),
        "cc_dw_w": nrm((DEPTH, CC_CONV_W, D_CONV), CC_CONV_W ** -0.5),
        "cc_dw_b": nrm((DEPTH, D_CONV), 0.02),
        "cc_ln_g": 1.0 + nrm((DEPTH, D_CONV), 0.02),
        "cc_ln_b": nrm((DEPTH, D_CONV), 0.02),
        "w_branch_b": nrm((DEPTH, D_CONV, D), D_CONV ** -0.5),
        "b_branch_b": nrm((DEPTH, D), 0.02),
        "w_out": nrm((DEPTH, D, D), D ** -0.5),
        "ffn_w_gate": nrm((N_DENSE, D, D_FF), D ** -0.5),
        "ffn_w_up": nrm((N_DENSE, D, D_FF), D ** -0.5),
        "ffn_w_down": nrm((N_DENSE, D_FF, D), D_FF ** -0.5),
        "moe_router_w": nrm((N_MOE, D, N_EXPERTS), D ** -0.5),
        "moe_router_b": nrm((N_MOE, N_EXPERTS), 0.01),
        "moe_w_gate": nrm((N_MOE, N_EXPERTS, D, D_FF_EXPERT), D ** -0.5),
        "moe_w_up": nrm((N_MOE, N_EXPERTS, D, D_FF_EXPERT), D ** -0.5),
        "moe_w_down": nrm((N_MOE, N_EXPERTS, D_FF_EXPERT, D), D_FF_EXPERT ** -0.5),
        "final_norm_g": 1.0 + nrm((D,), 0.02),
    }

def reference(x_prompt, x_sample, c_prompt, c_sample, state_rglru_h, state_rglru_conv, state_cconv,
              ada_w, ada_b, norm1_g, norm2_g, w_in, rg_conv_w, rg_conv_b, rg_wa, rg_ba, rg_wx, rg_bx,
              rg_lambda, w_branch_a, cc_dw_w, cc_dw_b, cc_ln_g, cc_ln_b, w_branch_b, b_branch_b, w_out,
              ffn_w_gate, ffn_w_up, ffn_w_down, moe_router_w, moe_router_b, moe_w_gate, moe_w_up,
              moe_w_down, final_norm_g):
    p = {"ada_w": ada_w, "ada_b": ada_b, "norm1_g": norm1_g, "norm2_g": norm2_g, "w_in": w_in,
         "rg_conv_w": rg_conv_w, "rg_conv_b": rg_conv_b, "rg_wa": rg_wa, "rg_ba": rg_ba,
         "rg_wx": rg_wx, "rg_bx": rg_bx, "rg_lambda": rg_lambda, "w_branch_a": w_branch_a,
         "cc_dw_w": cc_dw_w, "cc_dw_b": cc_dw_b, "cc_ln_g": cc_ln_g, "cc_ln_b": cc_ln_b,
         "w_branch_b": w_branch_b, "b_branch_b": b_branch_b, "w_out": w_out,
         "ffn_w_gate": ffn_w_gate, "ffn_w_up": ffn_w_up, "ffn_w_down": ffn_w_down,
         "moe_router_w": moe_router_w, "moe_router_b": moe_router_b, "moe_w_gate": moe_w_gate,
         "moe_w_up": moe_w_up, "moe_w_down": moe_w_down, "final_norm_g": final_norm_g}
    B = x_prompt.shape[0]
    dt = x_prompt.dtype
    h0 = jnp.zeros((DEPTH, B, D_RNN), dt)
    rc0 = jnp.zeros((DEPTH, B, RG_CONV_W - 1, D_RNN), dt)
    cc0 = jnp.zeros((DEPTH, B, CC_CONV_W - 1, D_CONV), dt)
    y_prompt, h_p, rc_p, cc_p = trunk(x_prompt, c_prompt, h0, rc0, cc0, p)
    y_sample, h_s, rc_s, cc_s = trunk(x_sample, c_sample, state_rglru_h, state_rglru_conv, state_cconv, p)
    return (y_prompt, y_sample, h_p, rc_p, cc_p, h_s, rc_s, cc_s)


_drawn_inputs = setup_inputs


def setup_inputs(seed=0):
    import zlib

    import numpy as np

    out = dict(_drawn_inputs(seed))
    spreads = {}
    factors = {'rg_ba': 8.0, 'rg_bx': 3.862, 'final_norm_g': 2.953}
    for name, (base, spread) in spreads.items():
        noise = np.random.default_rng([zlib.crc32(name.encode()), seed]).standard_normal(out[name].shape)
        drawn = base * np.exp(spread * noise) if base else spread * noise
        out[name] = __import__('jax').numpy.asarray(drawn.astype(out[name].dtype))
    for name, factor in factors.items():
        out[name] = (out[name] * factor).astype(out[name].dtype)
    return out
```

```python
from contextlib import ExitStack

import concourse.bass as bass
from concourse import mybir

F32 = mybir.dt.float32
F32R = mybir.dt.float32r
I32 = mybir.dt.int32
ALU = mybir.AluOpType
ACT = mybir.ActivationFunctionType
AX = mybir.AxisListType

P = 128
DEPTH = 2
D = 1024
NT = D // P
TP = 256
NB, TS = 8, 8
T = TP + NB * TS
NSEQ = 1 + NB
KR, KC = 4, 31
PR, PC = KR - 1, KC - 1
XR_W = PR + TP + NB * (PR + TS)
U_W = PC + TP + NB * (PC + TS)
NF = 2816 // P
NE = 8
FE = 1408
NFE = FE // P
EPS = 1e-6

CH = 8 * P
RING = 4
PER_LAYER = 48 + 8 + 8 + 8
DENSE = 3 * NF
C_LAYER = (0, PER_LAYER + DENSE)
NCHUNK = 2 * PER_LAYER + DENSE
NSLICE = 12

MCH = 8 * 352
MRAW, MSPL = 4, 3
MPER = 12
GW, DW = FE // 4, D // 4
NBLK = 13
TT = (128, 128, 64)

_COL = {}
_n = 0
for _l in range(DEPTH):
    for _name, _w in (("n1g", NT), ("n2g", NT), ("rgw", KR * NT), ("rgb", NT), ("ba", NT), ("bx", NT),
                      ("lam", NT), ("ccw", KC * NT), ("ccb", NT), ("lng", NT), ("lnb", NT), ("bbb", NT),
                      ("adab", 48), ("h0", NT * NB)):
        _COL[_name, _l] = _n
        _n += _w
for _name, _w in (("fg", NT), ("c", NT * NSEQ), ("wr", NT * NE), ("br", NE)):
    _COL[_name] = _n
    _n += _w
NCOL = _n
_CST = {}
_n = 0
for _name, _w in (("ident", P), ("tri", P), ("iota", P), ("sel", NSEQ), ("jlt", NE * NE), ("eidx", NE),
                  ("blk", NBLK)):
    _CST[_name] = _n
    _n += _w
NCST = _n


def build(nc, stream, ada, moe, cols_d, cst_d, wrg_d, x_d, rc_d, cc_d, y_o, h_o, rc_o, cc_o):
    with ExitStack() as ctx:
        def sem(name):
            return ctx.enter_context(nc.semaphore(name))

        at = [16512]

        def place(name, shape, dt, offset=None):
            size = 4
            for n in shape[1:]:
                size *= n
            if offset is None:
                offset = at[0]
                at[0] += (size + 31) // 32 * 32
            return nc.alloc_sbuf_tensor_at(name, shape, dt, offset=offset)

        x = place("x", [P, NT, T], F32)
        cols = place("cols", [P, NCOL], F32)
        cst = place("cst", [P, NCST], F32)
        ones = place("ones", [P, P], F32)
        eps = place("eps", [P, 1], F32)
        sp8 = place("sp8", [P, DEPTH, NT], F32)
        csil = place("csil", [P, NT, 32], F32)
        small = place("small", [P, 8, DEPTH, NT], F32)
        mod = [place(f"mod{l}", [P, 48, NSEQ], F32) for l in range(DEPTH)]
        modrow = place("modrow", [P, 512], F32)
        std = place("std", [P, T], F32)
        rstd = place("rstd", [P, T], F32)
        mean = place("mean", [P, T], F32)
        hlast = place("hlast", [P, NT, NSEQ], F32)
        rclast = place("rclast", [P, NT, NSEQ, PR], F32)
        nbi = place("nbi", [P, 1], I32)
        ebi = place("ebi", [P, NBLK], I32)
        o_xn = at[0]
        xn_hi = place("xn_hi", [P, NT, T], F32R)
        xn_lo = place("xn_lo", [P, NT, T], F32R)
        o_tmp = at[0]
        tmp = place("tmp", [P, RING, T], F32)
        wrg = place("wrg", [P, 2, NT, P], F32)
        o_ring = at[0]
        raw = place("raw", [P, RING, CH], F32)
        whi = place("whi", [P, RING, CH], F32R)
        wlo = place("wlo", [P, RING, CH], F32R)
        o_arena = at[0]
        gy = place("gy", [P, NT, T], F32)
        sga = place("sga", [P, NT, T], F32)
        upad = place("upad", [P, NT, U_W], F32)
        o_xr = at[0]
        xrp = place("xrp", [P, NT, XR_W], F32)
        th = place("th", [P, NT, T], F32, o_xr)
        o_xc = at[0]
        xc = place("xc", [P, NT, T], F32)
        sgb = place("sgb", [P, NT, T], F32, o_xc)
        o_a = at[0]
        ab = place("ab", [P, NT, T], F32)
        q_hi = place("q_hi", [P, NT, T], F32R, o_a)
        o_b = at[0]
        bb = place("bb", [P, NT, T], F32)
        q_lo = place("q_lo", [P, NT, T], F32R, o_b)
        o_v = at[0]
        v = place("v", [P, NT, T], F32)
        assert o_v + 16384 <= 229344, o_v
        h_hi = place("h_hi", [P, NF, T], F32R, o_arena)
        h_lo = place("h_lo", [P, NF, T], F32R, o_arena + NF * T * 4)
        assert o_arena + 2 * NF * T * 4 <= o_a
        adas = [[place(f"ada0_{i}", [P, NT, 512], F32, o_arena + 16384 * i) for i in range(4)],
                [place("ada1_0", [P, NT, 512], F32, o_v), place("ada1_1", [P, NT, 512], F32, o_a)]]
        mraw = place("mraw", [P, MRAW, MCH], F32, o_ring)
        assert MRAW * MCH * 4 <= o_arena - o_ring
        mhi = place("mhi", [P, MSPL, MCH], F32R, o_arena)
        mlo = place("mlo", [P, MSPL, MCH], F32R, o_arena + MSPL * MCH * 4)
        assert o_arena + 2 * MSPL * MCH * 4 <= o_b
        hn_tok = place("hn_tok", [P, 3, D], F32, o_v)
        yblk = place("yblk", [P, D], F32, o_v + 3 * D * 4)
        acc = place("acc", [P, NT, T], F32, o_xn)
        xg_hi = place("xg_hi", [P, NT, P], F32R, o_xn + 10240)
        xg_lo = place("xg_lo", [P, NT, P], F32R, o_xn + 10240 + 4096)
        hT_hi = place("hT_hi", [P, NFE, P], F32R, o_tmp)
        hT_lo = place("hT_lo", [P, NFE, P], F32R, o_tmp + 5632)
        hblk = place("hblk", [P, FE], F32, o_b)
        gsil = place("gsil", [P, 2, GW], F32, o_b + 5632)
        o_s = o_ring + MRAW * MCH * 4
        sm = place("sm", [P, 3, P], F32, o_s)
        wc = place("wc", [P, 3, P], F32, o_s + 1536)
        wct = place("wct", [P, T], F32, o_xn + 10240 + 8192)
        route = place("route", [P, 2560], F32, o_a)
        colpos = place("colpos", [P, 3, NBLK], F32, o_s + 3072)
        colw = place("colw", [P, 3, NBLK], F32, o_s + 3072 + 160)
        assert o_s + 3072 + 320 <= o_arena

        ps = [ctx.enter_context(nc.psum_tensor(f"ps{i}", [P, 512], F32)) for i in range(8)]

        def col(name, l, i):
            n = _COL[name, l] if l is not None else _COL[name]
            return cols[:, bass.ds(n + i, 1)]

        def cv(name, l, w):
            n = _COL[name, l] if l is not None else _COL[name]
            return cols[:, n:n + w]

        def ct(name, w):
            return cst[:, _CST[name]:_CST[name] + w]

        ident = ct("ident", P)

        x_in = sem("x_in")
        wrg_in = sem("wrg_in")
        rc_in = sem("rc_in")
        raw_landed = [sem(f"raw_landed{i}") for i in range(RING)]
        hi_ready = sem("hi_ready")
        lo_ready = sem("lo_ready")
        chunk_done = sem("chunk_done")
        evac_done = sem("evac_done")
        tmp_used = sem("tmp_used")
        ada_landed = [sem(f"ada_landed{i}") for i in range(4)]
        ada_rows = sem("ada_rows")
        row_copied = sem("row_copied")
        ada_turned = sem("ada_turned")
        mod_copied = sem("mod_copied")
        mod_ready = sem("mod_ready")
        csil_ready = sem("csil_ready")
        pad_ready = sem("pad_ready")
        const_ready = sem("const_ready")
        sq_ready = sem("sq_ready")
        stat_done = sem("stat_done")
        std_ready = sem("std_ready")
        xs_ready = sem("xs_ready")
        hn_ready = sem("hn_ready")
        norm_ready = sem("norm_ready")
        rg_done = sem("rg_done")
        rg_sig = sem("rg_sig")
        rg_exp = sem("rg_exp")
        rg_sq = sem("rg_sq")
        rg_root = sem("rg_root")
        q_ready = sem("q_ready")
        conv_step = sem("conv_step")
        ln_cent = sem("ln_cent")
        ln_act = sem("ln_act")
        v_ready = sem("v_ready")
        m_ready = sem("m_ready")
        dve_c = sem("dve_c")
        act_c = sem("act_c")
        out_done = sem("out_done")
        st_ready = sem("st_ready")
        m_landed = [sem(f"m_landed{i}") for i in range(MRAW)]
        m_hi = sem("m_hi")
        m_lo_dve = sem("m_lo_dve")
        m_lo_pool = sem("m_lo_pool")
        m_done = sem("m_done")
        r_pe = sem("r_pe")
        r_dve = sem("r_dve")
        routed = sem("routed")
        s_ready = sem("s_ready")
        g_done = sem("g_done")
        wc_ready = sem("wc_ready")
        wt_done = sem("wt_done")
        wct_ready = sem("wct_ready")
        xg_hi_ready = sem("xg_hi_ready")
        xg_ready = sem("xg_ready")
        gsil_ready = sem("gsil_ready")
        hs_ready = sem("hs_ready")
        ht_done = sem("ht_done")
        hT_hi_ready = sem("hT_hi_ready")
        hT_ready = sem("hT_ready")
        y_ready = sem("y_ready")
        sc_done = sem("sc_done")
        acc_done = sem("acc_done")
        x_final = sem("x_final")
        y_out = sem("y_out")
        r_act = sem("r_act")

        def seg(buf, i, hist, off):
            w = hist + TS
            p0 = hist + TP
            prompt = buf[:, i, off:off + TP]
            s = buf[:, i, p0:p0 + NB * w].rearrange("p (b t) -> p b t", b=NB)[:, :, off:off + TS]
            return prompt, s

        def samples(ap):
            return ap[:, TP:T].rearrange("p (b t) -> p b t", b=NB)

        def samples8(buf):
            return buf[:, :, TP:T].rearrange("p i (b t) -> p i b t", b=NB)

        def bc_t(ap):
            return ap.unsqueeze(2).broadcast_to([P, NB, TS])

        def stages(l):
            c = C_LAYER[l]
            return dict(gg=c, xr=c + 16, yr=c + 24, ga=c + 32, ba=c + 40, gb=c + 48, bb=c + 56, wo=c + 64,
                        gu=c + 72, dn=c + 72 + 2 * NF)

        E_OFF = (0, NF - NT)
        T_BASE = (0, 16 + 8 + 8 + 2 * NF + NT)
        T_GU = 32
        CONVS = 2 * NT * (KR + KC)
        STORES = 16 * (3 + NT)
        R_SEL, R_P, R_T, R_W, R_C, R_N, R_BASE = 0, 24, 48, 64, 88, 112, 144
        R_A, R_B = 160, 352
        R_REL, R_M = 560, 560 + 3 * NBLK * NE

        block = ctx.enter_context(nc.Block())

        @block.sync
        def _(e):
            e.dma_start(cols[:], cols_d).then_inc(x_in, 16)
            e.dma_start(cst[:], cst_d).then_inc(x_in, 16)
            e.dma_start(x[:], x_d).then_inc(x_in, 16)
            for s in range(4):
                e.dma_start(adas[0][s][:], ada[s]).then_inc(ada_landed[s], 16)
            with e.Fori(0, NSLICE // 4 - 1) as g:
                for s in range(4):
                    e.wait_ge(ada_rows, g * 4 + s + 1)
                    e.dma_start(adas[0][s][:], ada[g * 4 + s + 4]).then_inc(ada_landed[s], 16)

            def chunk(c_static, c):
                s = c_static % RING
                e.dma_start(raw[:, s, :], stream[c]).then_inc(raw_landed[s], 16)

            for c in range(RING):
                chunk(c, c)
            e.dma_start(wrg[:], wrg_d[0]).then_inc(wrg_in, 16)

            def run(c0, n):
                k, r = n // 4, n % 4
                if k:
                    with e.Fori(0, k) as g:
                        for j in range(4):
                            e.wait_ge(lo_ready, g * 4 + (c0 + j - RING + 1))
                            chunk(c0 + j, g * 4 + (c0 + j))
                for j in range(4 * k, n):
                    e.wait_ge(lo_ready, c0 + j - RING + 1)
                    chunk(c0 + j, c0 + j)

            def states(l):
                for i in range(NT):
                    for buf, h, src in ((xrp, PR, rc_d), (upad, PC, cc_d)):
                        e.dma_start(buf[:, i, h + TP:].rearrange("p (b t) -> p b t", b=NB)[:, :, 0:h],
                                    src[l, :, i]).then_inc(rc_in, 16)

            st0, st1 = stages(0), stages(1)
            e.wait_ge(ada_rows, NSLICE)
            states(0)
            run(RING, st0["bb"] - RING)

            def store_states(l):
                e.wait_ge(st_ready, 2 * l + 1)
                e.dma_start(rc_o[l], rclast[:]).then_inc(out_done, 16)
                e.wait_ge(st_ready, 2 * l + 2)
                e.dma_start(h_o[l], hlast[:]).then_inc(out_done, 16)
                e.wait_ge(tmp_used, T_BASE[l] + 16)
                e.dma_start(cc_o[l, :, :, 0, :], upad[:, :, TP:TP + PC]).then_inc(out_done, 16)
                for i in range(NT):
                    e.dma_start(cc_o[l, :, i, 1:NSEQ, :], upad[:, i, PC + TP:].rearrange(
                        "p (b t) -> p b t", b=NB)[:, :, TS:TS + PC]).then_inc(out_done, 16)

            store_states(0)
            run(st0["bb"], 8 + 4)
            e.wait_ge(out_done, STORES)
            e.wait_ge(m_ready, NT)
            e.dma_start(adas[1][0][:], ada[NSLICE]).then_inc(ada_landed[0], 16)
            e.wait_ge(rg_done, 2 * NT)
            e.dma_start(wrg[:], wrg_d[1]).then_inc(wrg_in, 16)
            run(st0["wo"] + 4, 4 + 4)
            e.wait_ge(norm_ready, 2 * NT)
            e.dma_start(adas[1][1][:], ada[NSLICE + 1]).then_inc(ada_landed[1], 16)
            with e.Fori(0, 5) as g:
                for h in range(2):
                    for j in range(4):
                        c = st0["gu"] + 4 + 4 * h + j
                        e.wait_ge(lo_ready, g * 8 + (c - RING + 1))
                        chunk(c, g * 8 + c)
                    e.wait_ge(ada_rows, g * 2 + (NSLICE + h + 1))
                    e.dma_start(adas[1][h][:], ada[g * 2 + (NSLICE + h + 2)]).then_inc(ada_landed[h], 16)
            run(st0["dn"], NF)
            run(st1["gg"], 4)
            e.wait_ge(chunk_done, st1["gg"])
            states(1)
            run(st1["gg"] + 4, 72 - 4 - 16)
            store_states(1)
            run(st1["bb"], 16)
            e.wait_ge(chunk_done, NCHUNK)
            for k in range(MRAW):
                e.dma_start(mraw[:, k, :], moe[k]).then_inc(m_landed[k], 16)

            def freed(n_dve, n_pool, pool):
                if pool:
                    e.wait_ge(m_lo_pool, n_pool)
                else:
                    e.wait_ge(m_lo_dve, n_dve)

            def lo_count(k):
                return k - (k + 1) // 3 + 1, (k + 1) // 3

            for k in range(MRAW, MPER):
                nd, npl = lo_count(k - MRAW)
                freed(nd, npl, (k - MRAW) % 3 == 2)
                e.dma_start(mraw[:, k % MRAW, :], moe[k]).then_inc(m_landed[k % MRAW], 16)
            e.wait_ge(routed, 1)
            nblk = e.value_load(nbi[0:1, 0:1], min_val=NE, max_val=NBLK)
            with e.Fori(1, nblk) as b:
                ex = e.value_load(ebi[0:1, bass.ds(b, 1)], min_val=0, max_val=NE - 1)
                for k in range(MPER):
                    kk = k + MPER - MRAW
                    nd, npl = lo_count(kk)
                    freed((b - 1) * 8 + nd, (b - 1) * 4 + npl, kk % 3 == 2)
                    e.dma_start(mraw[:, k % MRAW, :], moe[ex * MPER + k]).then_inc(m_landed[k % MRAW], 16)
            for i in range(NT):
                e.wait_ge(y_out, i + 1)
                e.dma_start(y_o[:, i, :], bb[:, i, :]).then_inc(out_done, 16)
            e.wait_ge(out_done, DEPTH * STORES + 16 * NT)


        @block.gpsimd
        def _(e):
            e.memset(ones[:], 1.0).then_inc(const_ready, 1)
            e.memset(eps[:], EPS).then_inc(const_ready, 1)
            e.memset(csil[:], 0.0).then_inc(const_ready, 1)

            def low(c_static, c):
                s = c_static % RING
                e.wait_ge(hi_ready, c + 1)
                e.tensor_tensor(wlo[:, s, :], raw[:, s, :], whi[:, s, :].bitcast(F32), ALU.subtract
                                ).then_inc(lo_ready, 1)

            def run(c0, n):
                k = n // 4
                with e.Fori(0, k) as g:
                    for j in range(4):
                        low(c0 + j, g * 4 + (c0 + j))
                for c in range(c0 + 4 * k, c0 + n):
                    low(c, c)

            def pads():
                e.memset(upad[:, :, 0:PC], 0.0).then_inc(pad_ready, 1)
                e.memset(xrp[:, :, 0:PR], 0.0).then_inc(pad_ready, 1)

            for c in range(4):
                low(c, c)
            e.wait_ge(ada_rows, NSLICE)
            pads()
            g1 = stages(1)["gg"]
            run(4, g1)
            e.wait_ge(chunk_done, g1)
            pads()
            run(g1 + 4, NCHUNK - g1 - 4)

            e.wait_ge(routed, 1)
            nblk = e.value_load(nbi[0:1, 0:1], min_val=NE, max_val=NBLK - 1)
            with e.Fori(0, nblk) as b:
                for q in range(2, MPER, 3):
                    e.wait_ge(m_hi, b * MPER + (q + 1))
                    e.tensor_tensor(mlo[:, q % MSPL, :], mraw[:, q % MRAW, :], mhi[:, q % MSPL, :].bitcast(F32),
                                    ALU.subtract).then_inc(m_lo_pool, 1)

        @block.tensor
        def _(e):
            def split_mm(out, w, x2, start, stop):
                e.matmul(out, w[0], x2[0], start=start, stop=False)
                e.matmul(out, w[0], x2[1], start=False, stop=False)
                return e.matmul(out, w[1], x2[0], start=False, stop=stop)

            def wtile(s, u):
                return whi[:, s, u * P:(u + 1) * P], wlo[:, s, u * P:(u + 1) * P]

            def main(l, c0, n, xs):
                def one(c_static, c):
                    s = c_static % RING
                    e.wait_ge(lo_ready, c + 1)
                    if c_static - E_OFF[l] >= RING:
                        e.wait_ge(evac_done, c - (E_OFF[l] + 3))
                    for k in range(NT):
                        mm = split_mm(ps[s][:, 0:T], wtile(s, k), (xs[0][:, k, :], xs[1][:, k, :]),
                                      k == 0, k == NT - 1)
                    mm.then_inc(chunk_done, 1)

                if c0 == 0:
                    for c in range(4):
                        one(c, c)
                    c0, n = 4, n - 4
                with e.Fori(0, n // 4) as g:
                    for j in range(4):
                        one(c0 + j, g * 4 + (c0 + j))

            def rows(slot, s, n_landed, mk):
                e.wait_ge(ada_landed[slot], n_landed)
                e.wait_ge(row_copied, s + 1)
                for k in range(NT):
                    q = 32 * (k % 4)
                    mm = e.matmul(ps[5][q:q + 32, :], csil[:, k, :], mk[:, k, :], start=k < 4, stop=k >= 4)
                mm.then_inc(ada_rows, 1)

            def turn(s):
                e.wait_ge(row_copied, s + 2)
                e.wait_ge(mod_copied, s + 1)
                for j in range(4):
                    mm = e.matmul(ps[6][:, NSEQ * j:NSEQ * (j + 1)], modrow[:, j * P:(j + 1) * P],
                                  ct("sel", NSEQ), start=True, stop=True)
                mm.then_inc(ada_turned, 1)

            def stat(buf, waits):
                for i in range(NT):
                    if i in waits:
                        e.wait_ge(*waits[i])
                    mm = e.matmul(ps[4][:, 0:T], ones[:], buf[:, i, :], start=i == 0, stop=i == NT - 1)
                mm.then_inc(stat_done, 1)

            def norm(n):
                stat(ab, {0: (sq_ready, 2 * n + 1), 4: (sq_ready, 2 * n + 2)})

            e.sem_inc(ada_turned, 1)
            e.sem_inc(sc_done, 1)
            e.wait_ge(x_in, 48)
            e.wait_ge(csil_ready, 1)
            with e.Fori(0, NSLICE // 4) as g:
                for slot in range(4):
                    rows(slot, g * 4 + slot, g * 16 + 16, adas[0][slot])
                    turn(g * 4 + slot)

            for l in range(DEPTH):
                st = stages(l)
                norm(2 * l)
                e.wait_ge(norm_ready, NT * (2 * l + 1))
                xs = (xn_hi, xn_lo)
                main(l, st["gg"], 32, xs)
                e.wait_ge(wrg_in, 16 * (l + 1))
                for i in range(NT):
                    if i % 2 == 0:
                        e.wait_ge(conv_step, CONVS * l + 2 * KC * 2 + 4 * KR * (i // 2 + 1))
                    for w in range(2):
                        n = 2 * i + w
                        if n >= 4:
                            e.wait_ge(rg_sig, 2 * NT * l + n - 3)
                        e.matmul(ps[4 + n % 4][:, 0:T], wrg[:, w, i, :], xc[:, i, :], start=True, stop=True
                                 ).then_inc(rg_done, 1)
                main(l, st["ga"], 8, xs)
                e.wait_ge(q_ready, l + 1)
                main(l, st["ba"], 8, (q_hi, q_lo))
                main(l, st["gb"], 8, xs)
                e.wait_ge(conv_step, CONVS * (l + 1))
                stat(v, {})
                stat(th, {0: (ln_act, 10 * l + 2)})
                e.wait_ge(v_ready, 2 * (l + 1))
                main(l, st["bb"], 8, (q_hi, q_lo))
                e.wait_ge(m_ready, NT * (l + 1))
                main(l, st["wo"], 8, xs)
                norm(2 * l + 1)
                if l == 0:
                    rows(0, NSLICE, 16 * 4, adas[1][0])
                    turn(NSLICE)
                    e.wait_ge(norm_ready, 2 * NT)

                    def four(g8, h, last):
                        for j in range(4):
                            cs = st["gu"] + 4 * h + j
                            c = g8 + cs
                            s = cs % RING
                            e.wait_ge(lo_ready, c + 1)
                            e.wait_ge(evac_done, c - 3)
                            for k in range(NT):
                                mm = split_mm(ps[s][:, 0:T], wtile(s, k), (xn_hi[:, k, :], xn_lo[:, k, :]),
                                              k == 0, k == NT - 1)
                            mm.then_inc(chunk_done, 1)
                            if j == 1 and not last:
                                pass

                    four(0, 0, True)
                    rows(1, NSLICE + 1, 16 * 4, adas[1][1])
                    turn(NSLICE + 1)
                    with e.Fori(0, 5) as g:
                        for h in range(2):
                            four(g * 8 + 4, h, False)
                            rows(h, g * 2 + (NSLICE + 2 + h), g * 16 + 16 * 5, adas[1][h])
                            turn(g * 2 + (NSLICE + 2 + h))
                    e.wait_ge(evac_done, st["dn"])
                    e.wait_ge(mod_copied, 2 * NSLICE + 1)

                    def down(cs, k, start, stop):
                        s = cs % RING
                        e.wait_ge(lo_ready, k + (st["dn"] + 1))
                        e.wait_ge(tmp_used, k * 2 + (T_GU + 2))
                        for m in range(NT):
                            mm = split_mm(ps[m][:, 0:T], wtile(s, m),
                                          (h_hi[:, bass.ds(k, 1), :].rearrange("p a t -> p (a t)"),
                                           h_lo[:, bass.ds(k, 1), :].rearrange("p a t -> p (a t)")), start, stop)
                        mm.then_inc(chunk_done, 1)

                    for k in range(4):
                        down(st["dn"] + k, k, k == 0, False)
                    with e.Fori(0, 4) as g:
                        for j in range(4):
                            down(st["dn"] + 4 + j, g * 4 + (4 + j), False, False)
                    for k in range(20, NF):
                        down(st["dn"] + k, k, False, k == NF - 1)

            e.wait_ge(hn_ready, 4 * NT)
            for t, m in enumerate(TT):
                for k in range(NT):
                    n = _COL["wr"] + k * NE
                    mm = e.matmul(ps[0][0:m, t * NE:(t + 1) * NE], bb[:, k, t * P:t * P + m],
                                  cols[:, n:n + NE], start=k == 0, stop=k == NT - 1)
            mm.then_inc(r_pe, 1)
            for t, m in enumerate(TT):
                for i in range(NT):
                    mm = e.transpose(ps[2 + 2 * t + i // 4][0:m, (i % 4) * P:(i % 4 + 1) * P],
                                     bb[:, i, t * P:t * P + m], ident)
            mm.then_inc(r_pe, 1)
            e.wait_ge(r_dve, 2)
            sel = route[:, R_SEL:R_SEL + 24]
            for t in range(4):
                for u in range(3 if t == 0 else t):
                    w = ones[:] if t == 0 or u < t - 1 else ct("tri", P)
                    mm = e.matmul(ps[1][:, t * NE:(t + 1) * NE], w, sel[:, u * NE:(u + 1) * NE], start=u == 0,
                                  stop=u == (2 if t == 0 else t - 1))
            mm.then_inc(r_pe, 1)

            def gather(b):
                e.wait_ge(s_ready, b + 1)
                for i in range(NT):
                    for t, m in enumerate(TT):
                        mm = e.matmul(ps[6 + i // 4][:, (i % 4) * P:(i % 4 + 1) * P],
                                      hn_tok[0:m, t, i * P:(i + 1) * P], sm[0:m, t, :], start=t == 0, stop=t == 2)
                mm.then_inc(g_done, 1)

            e.wait_ge(routed, 1)
            nblk = e.value_load(nbi[0:1, 0:1], min_val=NE, max_val=NBLK - 1)
            e.wait_ge(r_act, 1)
            gather(0)
            with e.Fori(0, nblk) as b:
                def split_ready(q):
                    if q % 3 == 2:
                        e.wait_ge(m_lo_pool, b * 4 + (q + 1) // 3)
                    else:
                        e.wait_ge(m_lo_dve, b * 8 + (q - (q + 1) // 3 + 1))

                e.wait_ge(xg_ready, b + 1)
                for q in range(8):
                    i, bank = q // 2, 2 * (q // 2 % 2) + q % 2
                    split_ready(q)
                    if i >= 2:
                        e.wait_ge(hs_ready, b * 4 + (i - 1))
                    for k in range(NT):
                        wh = mhi[:, q % MSPL, k * GW:(k + 1) * GW]
                        wl = mlo[:, q % MSPL, k * GW:(k + 1) * GW]
                        e.matmul(ps[bank][:, 0:GW], xg_hi[:, k, :], wh, start=k == 0, stop=False)
                        e.matmul(ps[bank][:, 0:GW], xg_hi[:, k, :], wl, start=False, stop=False)
                        mm = e.matmul(ps[bank][:, 0:GW], xg_lo[:, k, :], wh, start=False, stop=k == NT - 1)
                    mm.then_inc(m_done, 1)
                e.wait_ge(acc_done, b * NT + 1)
                e.wait_ge(wc_ready, b + 1)
                for t, m in enumerate(TT):
                    mm = e.transpose(ps[5][:, t * P:t * P + m], wc[0:m, t, :], ident[0:m, 0:m])
                mm.then_inc(wt_done, 1)
                e.wait_ge(hs_ready, b * 4 + 4)
                for f in range(NFE):
                    mm = e.transpose(ps[(4, 0, 1)[f // 4]][:, (f % 4) * P:(f % 4 + 1) * P],
                                     hblk[:, f * P:(f + 1) * P], ident)
                mm.then_inc(ht_done, 1)
                gather(b + 1)
                e.wait_ge(hT_ready, b + 1)
                for j in range(4):
                    q = 8 + j
                    split_ready(q)
                    out = ps[(2 + j) % 4][:, 0:DW]
                    for f in range(NFE):
                        wh = mhi[:, q % MSPL, f * DW:(f + 1) * DW]
                        wl = mlo[:, q % MSPL, f * DW:(f + 1) * DW]
                        e.matmul(out, hT_hi[:, f, :], wh, start=f == 0, stop=False)
                        e.matmul(out, hT_hi[:, f, :], wl, start=False, stop=False)
                        mm = e.matmul(out, hT_lo[:, f, :], wh, start=False, stop=f == NFE - 1)
                    mm.then_inc(m_done, 1)
                e.wait_ge(y_ready, b * 4 + 4)
                e.wait_ge(wct_ready, b + 1)
                e.wait_ge(xg_ready, b + 2)
                for i in range(NT):
                    if i >= 4:
                        e.wait_ge(acc_done, b * NT + (i - 2))
                    e.matmul(ps[4 + i % 4][:, 0:T], yblk[:, i * P:(i + 1) * P], wct[:], start=True, stop=True
                             ).then_inc(sc_done, 1)
            norm(4)

        @block.scalar
        def _(e):
            links = [0]

            def link(ins):
                links[0] += 1
                ins.then_inc(act_c, 1)
                e.wait_ge(act_c, links[0])

            def high(c_static, c):
                s = c_static % RING
                e.wait_ge(raw_landed[s], (c - c_static) * 4 + 16 * (c_static // RING + 1))
                if c_static >= RING:
                    e.wait_ge(chunk_done, c - (RING - 1))
                e.activation(whi[:, s, :], raw[:, s, :], ACT.Copy).then_inc(hi_ready, 1)

            def stage(l, c0, n, evac, t0=None, splits=True):
                def one(c_static, c):
                    e.wait_ge(chunk_done, c + 1)
                    if t0 is not None and c_static - c0_first + t0 >= RING:
                        e.wait_ge(tmp_used, c - c0_first + (t0 - RING + 1))
                    evac(c_static - c0_first, c - c0_first, ps[c_static % RING][:, 0:T]).then_inc(evac_done, 1)
                    if splits:
                        high(c_static + RING, c + RING)

                c0_first = c0
                if t0 == 0 or not splits:
                    for c in range(c0, c0 + 4):
                        one(c, c)
                    c0, n = c0 + 4, n - 4
                if n:
                    with e.Fori(0, n // 4) as g:
                        for j in range(4):
                            one(c0 + j, g * 4 + (c0 + j))

            def tile(buf, i):
                return buf[:, bass.ds(i, 1), :].rearrange("p a t -> p (a t)")

            def ada_copy(s):
                e.wait_ge(ada_rows, s + 1)
                e.wait_ge(ada_turned, s + 1)
                e.activation(modrow[:], ps[5][:], ACT.Copy).then_inc(row_copied, 1)

            def mod_copy(l, s):
                e.wait_ge(ada_turned, s + 2)
                e.activation(mod[l][:, bass.ds((s - NSLICE * l) * 4, 4), :].rearrange("p a b -> p (a b)"),
                             ps[6][:, 0:4 * NSEQ], ACT.Copy).then_inc(mod_copied, 1)

            def norm(n, split):
                l, k = n // 2, n % 2
                for h in range(2):
                    if n == 4:
                        e.wait_ge(x_final, 1)
                    elif n:
                        e.wait_ge(tmp_used, (0, T_GU, T_BASE[1], T_BASE[1] + T_GU)[n] - 4 * (1 - h))
                    e.activation(ab[:, 4 * h:4 * h + 4, :], x[:, 4 * h:4 * h + 4, :], ACT.Square
                                 ).then_inc(sq_ready, 1)
                e.wait_ge(stat_done, (0, 3, 4, 7, 8)[n] + 1)
                e.activation(std[:], ps[4][:, 0:T], ACT.Sqrt, bias=eps[:], scale=1.0 / D).then_inc(std_ready, 1)
                if n == 4:
                    for i in range(NT):
                        e.wait_ge(xs_ready, NT * n + i + 1)
                        e.activation(bb[:, i, :], bb[:, i, :], ACT.Copy, scale=col("fg", None, i)
                                     ).then_inc(y_out, 1)
                    return
                for i in range(NT):
                    e.wait_ge(xs_ready, NT * n + i + 1)
                    e.activation(bb[:, i, 0:TP], bb[:, i, 0:TP], ACT.Identity,
                                 scale=mod[l][:, 24 * k + 8 + i, 0:1], bias=mod[l][:, 24 * k + i, 0:1]
                                 ).then_inc(hn_ready, 1)

            e.sem_inc(row_copied, 1)
            e.sem_inc(mod_copied, 1)
            e.wait_ge(x_in, 48)
            e.wait_ge(const_ready, 3)
            e.activation(csil[:, :, 0:NSEQ], cv("c", None, NT * NSEQ).rearrange("p (k b) -> p k b", b=NSEQ),
                         ACT.Silu).then_inc(csil_ready, 1)
            for l in range(DEPTH):
                link(e.activation(small[:, 0, l, :], cv("lam", l, NT), ACT.Abs))
            for l in range(DEPTH):
                e.activation(small[:, 1, l, :], small[:, 0, l, :], ACT.Exp, scale=-1.0).then_inc(csil_ready, 1)
            with e.Fori(0, NSLICE) as s:
                ada_copy(s)
                mod_copy(0, s)
            for c in range(RING):
                high(c, c)

            for l in range(DEPTH):
                st = stages(l)
                tb = T_BASE[l]
                norm(2 * l, True)

                stage(l, st["gg"], 16,
                      lambda j, i, p: e.activation(tmp[:, j % RING, :], p, ACT.Sigmoid if j % 2 == 0 else ACT.Copy),
                      t0=tb)

                def evac_xr(j, i, p):
                    e.activation(xrp[:, bass.ds(i, 1), PR:PR + TP].rearrange("p a t -> p (a t)"), p[:, 0:TP],
                                 ACT.Copy)
                    return e.activation(sa_of(xrp, i, PR), samples(p), ACT.Copy)

                def sa_of(buf, i, hist):
                    w = hist + TS
                    row = buf[:, bass.ds(i, 1), hist + TP:hist + TP + NB * w].rearrange("p a w -> p (a w)")
                    return row.rearrange("p (b t) -> p b t", b=NB)[:, :, hist:hist + TS]

                stage(l, st["xr"], 8, evac_xr)
                stage(l, st["yr"], 8, lambda j, i, p: e.activation(tile(gy, i), p, ACT.Gelu_apprx_tanh))

                for i in range(NT):
                    for w, (buf, b) in enumerate(((ab, "ba"), (bb, "bx"))):
                        n = 2 * i + w
                        e.wait_ge(rg_done, 2 * NT * l + n + 1)
                        e.activation(buf[:, i, :], ps[4 + n % 4][:, 0:T], ACT.Sigmoid, bias=col(b, l, i)
                                     ).then_inc(rg_sig, 1)
                stage(l, st["ga"], 4, lambda j, i, p: e.activation(tile(sga, i), p, ACT.Sigmoid))
                e.wait_ge(st_ready, 2 * l + 1)
                e.wait_ge(rg_sig, 2 * NT * (l + 1))
                for i in range(NT):
                    e.activation(th[:, i, :], ab[:, i, :], ACT.Tanh, scale=sp8[:, l, i:i + 1])
                    ins = e.activation(ab[:, i, :], ab[:, i, :], ACT.Exp, scale=sp8[:, l, i:i + 1])
                ins.then_inc(rg_exp, 1)
                stage(l, st["ga"] + 4, 4, lambda j, i, p: e.activation(tile(sga, i + 4), p, ACT.Sigmoid))
                e.wait_ge(rg_sq, l + 1)
                e.activation(th[:], th[:], ACT.Sqrt, scale=-1.0).then_inc(rg_root, 1)
                stage(l, st["ba"], 8, lambda j, i, p: e.activation(tile(gy, i), p, ACT.Copy))
                stage(l, st["gb"], 8, lambda j, i, p: e.activation(tile(sgb, i), p, ACT.Sigmoid))

                e.wait_ge(stat_done, 4 * l + 2)
                e.activation(mean[:], ps[4][:, 0:T], ACT.Copy, scale=1.0 / D).then_inc(ln_act, 1)
                e.wait_ge(ln_cent, 2 * l + 1)
                e.activation(th[:], v[:], ACT.Square).then_inc(ln_act, 1)
                e.wait_ge(stat_done, 4 * l + 3)
                e.activation(std[:], ps[4][:, 0:T], ACT.Sqrt, bias=eps[:], scale=1.0 / D).then_inc(std_ready, 1)
                e.wait_ge(ln_cent, 2 * l + 2)
                for i in range(NT):
                    e.activation(v[:, i, :], v[:, i, :], ACT.Silu, scale=col("lng", l, i), bias=col("lnb", l, i)
                                 ).then_inc(ln_act, 1)
                stage(l, st["bb"], 8, lambda j, i, p: e.activation(tmp[:, j % RING, :], p, ACT.Identity,
                                                                   bias=col("bbb", l, i)), t0=tb + 16)
                ev_tmp = lambda j, i, p: e.activation(tmp[:, j % RING, :], p, ACT.Copy)
                if l == 0:
                    stage(l, st["wo"], 8, ev_tmp, t0=tb + 24)
                else:
                    stage(l, st["wo"], 4, ev_tmp, t0=tb + 24)
                    stage(l, st["wo"] + 4, 4, ev_tmp, t0=tb + 28, splits=False)
                norm(2 * l + 1, l == 0)
                if l == 0:
                    ada_copy(NSLICE)
                    mod_copy(1, NSLICE)
                    gu = lambda j, i, p: e.activation(tmp[:, j % RING, :], p, ACT.Silu if j % 2 == 0 else ACT.Copy)

                    def four(g8, c0):
                        for j in range(4):
                            c = g8 + (c0 + j)
                            e.wait_ge(chunk_done, c + 1)
                            e.wait_ge(tmp_used, c + (T_GU - st["gu"] - RING + 1))
                            gu(j, None, ps[(c0 + j) % RING][:, 0:T]).then_inc(evac_done, 1)
                            high(c0 + j + RING, c + RING)

                    four(0, st["gu"])
                    ada_copy(NSLICE + 1)
                    mod_copy(1, NSLICE + 1)
                    with e.Fori(0, 5) as g:
                        for h in range(2):
                            four(g * 8, st["gu"] + 4 + 4 * h)
                            ada_copy(g * 2 + (NSLICE + 2 + h))
                            mod_copy(1, g * 2 + (NSLICE + 2 + h))
                    with e.Fori(0, NF // 4) as g:
                        for j in range(4):
                            high(st["dn"] + 4 + j, g * 4 + (st["dn"] + 4 + j))
                    for c in range(st["dn"] + 20 + 4, st["dn"] + NF + 4):
                        high(c, c)
                    e.wait_ge(chunk_done, st["dn"] + NF)
                    for m in range(NT):
                        e.wait_ge(tmp_used, T_GU + 2 * NF + m - 3)
                        e.activation(tmp[:, m % RING, :], ps[m][:, 0:T], ACT.Copy).then_inc(evac_done, 1)

            for t, m in enumerate(TT):
                for h in range(2):
                    e.wait_ge(r_pe, 2)
                    ins = e.activation(hn_tok[0:m, t, h * 512:(h + 1) * 512], ps[2 + 2 * t + h][0:m, :], ACT.Copy)
            ins.then_inc(r_act, 1)
            e.wait_ge(r_dve, 1)
            ins = e.activation(route[:, R_P:R_P + 24], route[:, R_P:R_P + 24], ACT.Exp)
            ins.then_inc(r_act, 1)
            e.wait_ge(routed, 1)
            nblk = e.value_load(nbi[0:1, 0:1], min_val=NE, max_val=NBLK - 1)

            def gathered(n):
                e.wait_ge(g_done, n + 1)
                for h in range(2):
                    ins = e.activation(xg_hi[:, 4 * h:4 * h + 4, :].rearrange("p a s -> p (a s)"), ps[6 + h][:],
                                       ACT.Copy)
                ins.then_inc(xg_hi_ready, 1)

            gathered(0)
            with e.Fori(0, nblk) as b:
                def mhigh(q):
                    e.wait_ge(m_landed[q % MRAW], b * (16 * MPER // MRAW) + 16 * (q // MRAW + 1))
                    if q >= MSPL:
                        e.wait_ge(m_done, b * MPER + (q - MSPL + 1))
                    e.activation(mhi[:, q % MSPL, :], mraw[:, q % MRAW, :], ACT.Copy).then_inc(m_hi, 1)

                for q in range(MSPL):
                    mhigh(q)
                for q in range(MPER):
                    if q < 8 and q % 2 == 0:
                        i = q // 2
                        e.wait_ge(m_done, b * MPER + (q + 1))
                        if i >= 2:
                            e.wait_ge(hs_ready, b * 4 + (i - 1))
                        e.activation(gsil[:, i % 2, :], ps[2 * (i % 2)][:, 0:GW], ACT.Silu).then_inc(gsil_ready, 1)
                    if q == 8:
                        e.wait_ge(wt_done, b + 1)
                        e.wait_ge(sc_done, b * NT + 1)
                        e.activation(wct[:], ps[5][:, 0:T], ACT.Copy).then_inc(wct_ready, 1)
                        e.wait_ge(ht_done, b + 1)
                        for n, (bank, w) in enumerate(((4, 512), (0, 512), (1, 384))):
                            ins = e.activation(hT_hi[:, 4 * n:4 * n + w // P, :].rearrange("p a s -> p (a s)"),
                                               ps[bank][:, 0:w], ACT.Copy)
                        ins.then_inc(hT_hi_ready, 1)
                        gathered(b + 1)
                    if q >= 8:
                        j = q - 8
                        e.wait_ge(m_done, b * MPER + (q + 1))
                        e.activation(yblk[:, j * DW:(j + 1) * DW], ps[(2 + j) % 4][:, 0:DW],
                                     ACT.Copy).then_inc(y_ready, 1)
                    if q < MPER - MSPL:
                        mhigh(q + MSPL)
            norm(4, False)

        @block.vector
        def _(e):
            links = [0]

            def link(ins):
                links[0] += 1
                ins.then_inc(dve_c, 1)
                e.wait_ge(dve_c, links[0])

            def low(n, out, hi, src):
                return e.tensor_tensor(out, src, hi.bitcast(F32), ALU.subtract)

            def bc_tiles(ap, w):
                return ap.unsqueeze(1).broadcast_to([P, NT, w])

            def bc_seq(ap):
                return ap.unsqueeze(3).broadcast_to([P, NT, NB, TS])

            def norm(n, split):
                l, k = n // 2, n % 2
                e.wait_ge(std_ready, (1, 3, 4, 6, 7)[n])
                link(e.reciprocal(rstd[:], std[:]))
                if n == 4:
                    for i in range(NT):
                        e.tensor_tensor(bb[:, i, :], x[:, i, :], rstd[:], ALU.mult).then_inc(xs_ready, 1)
                    return
                link(e.tensor_tensor(bb[:, :, TP:T], x[:, :, TP:T], bc_tiles(rstd[:, TP:T], T - TP), ALU.mult))
                link(e.tensor_tensor(samples8(bb), samples8(bb), bc_seq(mod[l][:, 24 * k + 8:24 * k + 16, 1:]),
                                     ALU.mult))
                link(e.tensor_tensor(samples8(bb), samples8(bb), bc_seq(mod[l][:, 24 * k:24 * k + 8, 1:]),
                                     ALU.add))
                for i in range(NT):
                    e.tensor_tensor(bb[:, i, 0:TP], x[:, i, 0:TP], rstd[:, 0:TP], ALU.mult).then_inc(xs_ready, 1)
                if split:
                    for i in range(NT):
                        e.wait_ge(hn_ready, NT * n + i + 1)
                        link(e.tensor_copy(xn_hi[:, i, :], bb[:, i, :]))
                        low(1, xn_lo[:, i, :], xn_hi[:, i, :], bb[:, i, :]).then_inc(norm_ready, 1)

            conv_n = [0]

            def conv(l, K, pair, srcs, dst, w, b):
                for k in range(K):
                    for t in range(2):
                        i = 2 * pair + t
                        pr, sa = seg(srcs, i, K - 1, k)
                        for src, out in ((pr, dst[:, i, 0:TP]), (sa, samples(dst[:, i, :]))):
                            if k == 0:
                                ins = e.tensor_scalar(out, src, col(w, l, i), col(b, l, i), ALU.mult, ALU.add)
                            else:
                                e.wait_ge(conv_step, conv_n[0] - 3)
                                ins = e.scalar_tensor_tensor(out=out, in0=src, scalar=col(w, l, k * NT + i),
                                                             in1=out, op0=ALU.mult, op1=ALU.add)
                            ins.then_inc(conv_step, 1)
                            conv_n[0] += 1

            def finish_mod(l):
                e.wait_ge(mod_copied, NSLICE * (l + 1) + 1)
                m = mod[l]
                link(e.tensor_tensor(m[:], m[:], cv("adab", l, 48).unsqueeze(2).broadcast_to([P, 48, NSEQ]), ALU.add))
                for k, g in ((8, "n1g"), (32, "n2g")):
                    e.scalar_tensor_tensor(out=m[:, k:k + 8, :], in0=m[:, k:k + 8, :], scalar=1.0,
                                           in1=cv(g, l, NT).unsqueeze(2).broadcast_to([P, NT, NSEQ]),
                                           op0=ALU.add, op1=ALU.mult).then_inc(mod_ready, 1)
                for k in (16, 40):
                    e.tensor_scalar(m[:, k:k + 8, :], m[:, k:k + 8, :], 1.0, None, ALU.add).then_inc(mod_ready, 1)
                e.wait_ge(mod_ready, 4 * (l + 1))

            def residual(l, k, i, src, last):
                e.scalar_tensor_tensor(out=x[:, i, 0:TP], in0=src[:, 0:TP], scalar=mod[l][:, k + i, 0:1],
                                       in1=x[:, i, 0:TP], op0=ALU.mult, op1=ALU.add)
                link(e.tensor_tensor(samples(src), samples(src), bc_t(mod[l][:, k + i, 1:]), ALU.mult))
                e.tensor_tensor(samples(x[:, i, :]), samples(x[:, i, :]), samples(src), ALU.add
                                ).then_inc(last, 1)

            e.sem_inc(acc_done, 1)
            e.wait_ge(x_in, 48)
            e.wait_ge(csil_ready, 1 + DEPTH)
            lam2 = [small[:, k, :, :].rearrange("p l i -> p (l i)") for k in range(8)]
            link(e.tensor_scalar(lam2[2], lam2[1], 2.0, None, ALU.add))
            link(e.reciprocal(lam2[3], lam2[2]))
            link(e.tensor_tensor(lam2[4], lam2[1], lam2[3], ALU.mult))
            link(e.tensor_tensor(lam2[5], lam2[4], lam2[4], ALU.mult))
            link(e.tensor_scalar(lam2[6], lam2[5], 1.0 / 19, None, ALU.mult))
            for k in range(8, 0, -1):
                link(e.scalar_tensor_tensor(out=lam2[6], in0=lam2[6], scalar=1.0 / (2 * k + 1), in1=lam2[5],
                                            op0=ALU.add, op1=ALU.mult))
            link(e.scalar_tensor_tensor(out=lam2[6], in0=lam2[6], scalar=1.0, in1=lam2[4], op0=ALU.add,
                                        op1=ALU.mult))
            for l in range(DEPTH):
                link(e.tensor_scalar(small[:, 7, l, :], cv("lam", l, NT), -1.0, 0.0, ALU.mult, ALU.max))
            link(e.scalar_tensor_tensor(out=lam2[6], in0=lam2[6], scalar=2.0, in1=lam2[7], op0=ALU.mult,
                                        op1=ALU.add))
            link(e.tensor_scalar(sp8[:].rearrange("p l i -> p (l i)"), lam2[6], -8.0, None, ALU.mult))

            flat = lambda buf: buf[:].rearrange("p i t -> p (i t)")
            for l in range(DEPTH):
                st = stages(l)
                tb, eo = T_BASE[l], E_OFF[l]
                finish_mod(l)
                norm(2 * l, True)
                if l == 0:
                    e.wait_ge(pad_ready, 2)
                for i in range(NT):
                    e.wait_ge(evac_done, st["gg"] - eo + 2 * i + 2)
                    s = 2 * i % RING
                    pr, sa = seg(upad, i, PC, PC)
                    e.tensor_tensor(pr, tmp[:, s, 0:TP], tmp[:, s + 1, 0:TP], ALU.mult)
                    e.tensor_tensor(sa, samples(tmp[:, s, :]), samples(tmp[:, s + 1, :]), ALU.mult
                                    ).then_inc(tmp_used, 2)
                e.wait_ge(rc_in, 16 * 2 * NT * (l + 1))
                e.wait_ge(pad_ready, 2 * (l + 1))
                e.wait_ge(tmp_used, tb + 16)
                conv(l, KC, 0, upad, v, "ccw", "ccb")
                e.wait_ge(evac_done, st["xr"] - eo + NT)
                for pair in range(NT // 2):
                    conv(l, KR, pair, xrp, xc, "rgw", "rgb")
                if l:
                    e.wait_ge(out_done, STORES * l)
                e.tensor_copy(rclast[:, :, 0, :], xrp[:, :, TP:TP + PR])
                e.tensor_copy(rclast[:, :, 1:, :], xrp[:, :, PR + TP:].rearrange(
                    "p i (b t) -> p i b t", b=NB)[:, :, :, TS:TS + PR]).then_inc(st_ready, 1)
                conv(l, KC, 1, upad, v, "ccw", "ccb")
                e.wait_ge(rg_exp, l + 1)
                link(e.tensor_tensor(flat(bb), flat(bb), flat(xc), ALU.mult))
                link(e.tensor_tensor(flat(xc), flat(ab), flat(ab), ALU.mult))
                e.scalar_tensor_tensor(out=flat(th), in0=flat(xc), scalar=1.0, in1=flat(th), op0=ALU.add,
                                       op1=ALU.mult).then_inc(rg_sq, 1)
                e.wait_ge(rg_root, l + 1)
                link(e.tensor_tensor(flat(bb), flat(bb), flat(th), ALU.mult))
                first = lambda buf: samples8(buf)[:, :, :, 0]
                h9 = hlast[:, :, 1:]
                link(e.tensor_tensor(h9, first(ab), cv("h0", l, NT * NB).rearrange("p (i b) -> p i b", b=NB),
                                     ALU.mult))
                link(e.tensor_tensor(first(bb), first(bb), h9, ALU.add))
                e.memset(first(ab), 0.0).then_inc(dve_c, 1)
                e.memset(ab[:, :, 0], 0.0).then_inc(dve_c, 1)
                links[0] += 2
                e.wait_ge(dve_c, links[0])
                link(e.tensor_tensor_scan(flat(xc), flat(ab), flat(bb), 0.0, ALU.mult, ALU.add))
                e.tensor_copy(hlast[:, :, 0], xc[:, :, TP - 1])
                e.tensor_copy(hlast[:, :, 1:], samples8(xc)[:, :, :, TS - 1]).then_inc(st_ready, 1)
                e.wait_ge(evac_done, st["yr"] - eo + NT)
                link(e.tensor_tensor(flat(gy), flat(gy), flat(xc), ALU.mult))
                link(e.tensor_copy(flat(q_hi), flat(gy)))
                low(1, flat(q_lo), flat(q_hi), flat(gy)).then_inc(q_ready, 1)
                conv(l, KC, 2, upad, v, "ccw", "ccb")
                conv(l, KC, 3, upad, v, "ccw", "ccb")
                e.wait_ge(ln_act, 10 * l + 1)
                e.tensor_tensor(v[:], v[:], bc_tiles(mean[:], T), ALU.subtract).then_inc(ln_cent, 1)
                e.wait_ge(std_ready, 3 * l + 2)
                link(e.reciprocal(rstd[:], std[:]))
                e.tensor_tensor(v[:], v[:], bc_tiles(rstd[:], T), ALU.mult).then_inc(ln_cent, 1)
                for h in range(2):
                    e.wait_ge(ln_act, 10 * l + 2 + 4 * (h + 1))
                    link(e.tensor_copy(q_hi[:, 4 * h:4 * h + 4, :], v[:, 4 * h:4 * h + 4, :]))
                    low(1, q_lo[:, 4 * h:4 * h + 4, :], q_hi[:, 4 * h:4 * h + 4, :], v[:, 4 * h:4 * h + 4, :]
                        ).then_inc(v_ready, 1)
                link(e.tensor_tensor(flat(gy), flat(gy), flat(sga), ALU.mult))
                for i in range(NT):
                    e.wait_ge(evac_done, st["bb"] - eo + i + 1)
                    tm = tmp[:, i % RING, :]
                    link(e.tensor_tensor(tm, tm, sgb[:, i, :], ALU.mult))
                    e.tensor_tensor(sgb[:, i, :], tm, gy[:, i, :], ALU.add).then_inc(tmp_used, 1)
                    e.wait_ge(tmp_used, tb + 16 + i + 1)
                    link(e.tensor_copy(xn_hi[:, i, :], sgb[:, i, :]))
                    low(1, xn_lo[:, i, :], xn_hi[:, i, :], sgb[:, i, :]).then_inc(m_ready, 1)
                for i in range(NT):
                    e.wait_ge(evac_done, st["wo"] - eo + i + 1)
                    residual(l, 16, i, tmp[:, i % RING, :], tmp_used)
                norm(2 * l + 1, l == 0)
                if l == 0:
                    for f in range(NF):
                        e.wait_ge(evac_done, st["gu"] + 2 * f + 2)
                        s = 2 * f % RING
                        hf = tmp[:, s, :]
                        link(e.tensor_tensor(hf, hf, tmp[:, s + 1, :], ALU.mult))
                        link(e.tensor_copy(h_hi[:, f, :], hf))
                        low(1, h_lo[:, f, :], h_hi[:, f, :], hf).then_inc(tmp_used, 2)
                    for i in range(NT):
                        e.wait_ge(evac_done, st["dn"] + i + 1)
                        residual(l, 40, i, tmp[:, i % RING, :], tmp_used)

            R = lambda off, n: route[:, off:off + n]
            S3 = lambda ap: ap.rearrange("p (t e) -> p t e", e=NE)
            bias = cv("br", None, NE).unsqueeze(1).broadcast_to([P, 3, NE])
            link(e.memset(R(R_P, 24), 0.0))
            e.wait_ge(r_pe, 1)
            link(e.tensor_copy(R(R_P, 16), ps[0][:, 0:16]))
            link(e.tensor_copy(route[0:64, R_P + 16:R_P + 24], ps[0][0:64, 16:24]))
            pp = R(R_P, 24)
            link(e.tensor_tensor(S3(pp), S3(pp), bias, ALU.add))
            link(e.tensor_reduce(R(R_T, 3), S3(pp), AX.X, ALU.max))
            bc3 = lambda ap: ap.unsqueeze(2).broadcast_to([P, 3, NE])
            e.tensor_tensor(S3(pp), S3(pp), bc3(R(R_T, 3)), ALU.subtract).then_inc(r_dve, 1)
            e.wait_ge(r_act, 2)
            link(e.tensor_reduce(R(R_T, 3), S3(pp), AX.X, ALU.add))
            link(e.reciprocal(R(R_T + 4, 3), R(R_T, 3)))
            link(e.tensor_tensor(S3(pp), S3(pp), bc3(R(R_T + 4, 3)), ALU.mult))
            pj = S3(pp).unsqueeze(2).broadcast_to([P, 3, NE, NE])
            pe_ = S3(pp).unsqueeze(3).broadcast_to([P, 3, NE, NE])
            g4 = lambda ap: ap.rearrange("p (t e j) -> p t e j", e=NE, j=NE)
            link(e.tensor_tensor(g4(R(R_A, 192)), pj, pe_, ALU.is_gt))
            link(e.tensor_tensor(g4(R(R_B, 192)), pj, pe_, ALU.is_equal))
            before = ct("jlt", NE * NE)
            link(e.tensor_tensor(R(R_B, 192).rearrange("p (t m) -> p t m", t=3),
                                 R(R_B, 192).rearrange("p (t m) -> p t m", t=3),
                                 before.unsqueeze(1).broadcast_to([P, 3, NE * NE]), ALU.mult))
            link(e.tensor_tensor(R(R_A, 192), R(R_A, 192), R(R_B, 192), ALU.add))
            link(e.tensor_reduce(S3(R(R_C, 24)), g4(R(R_A, 192)), AX.X, ALU.add))
            sel = R(R_SEL, 24)
            link(e.tensor_scalar(sel, R(R_C, 24), 2.0, None, ALU.is_lt))
            link(e.memset(route[64:128, R_SEL + 16:R_SEL + 24], 0.0))
            e.tensor_tensor(R(R_W, 24), sel, pp, ALU.mult).then_inc(r_dve, 1)
            e.wait_ge(r_dve, 2)
            link(e.tensor_reduce(R(R_T, 3), S3(R(R_W, 24)), AX.X, ALU.add))
            link(e.tensor_scalar(R(R_T, 3), R(R_T, 3), 1e-30, None, ALU.max))
            link(e.reciprocal(R(R_T + 4, 3), R(R_T, 3)))
            link(e.tensor_tensor(S3(R(R_W, 24)), S3(R(R_W, 24)), bc3(R(R_T + 4, 3)), ALU.mult))
            e.wait_ge(r_pe, 3)
            link(e.tensor_copy(R(R_N, 32), ps[1][:, 0:32]))
            link(e.tensor_scalar(R(R_T, 8), R(R_N, 8), float(P), None, ALU.is_gt))
            link(e.tensor_scalar(R(R_T + 8, 8), R(R_N, 8), float(2 * P), 1.0, ALU.is_gt, ALU.add))
            link(e.tensor_tensor(R(R_T, 8), R(R_T, 8), R(R_T + 8, 8), ALU.add))
            link(e.tensor_tensor(R(R_A, 64).rearrange("p (e j) -> p e j", j=NE),
                                 R(R_T, 8).unsqueeze(1).broadcast_to([P, NE, NE]),
                                 before.rearrange("p (e j) -> p e j", j=NE), ALU.mult))
            link(e.tensor_reduce(R(R_BASE, 8), R(R_A, 64).rearrange("p (e j) -> p e j", j=NE), AX.X, ALU.add))
            link(e.tensor_reduce(R(R_T + 8, 1), R(R_T, 8), AX.X, ALU.add))
            link(e.tensor_copy(nbi[:], R(R_T + 8, 1)))
            link(e.tensor_scalar(R(R_BASE, 8), R(R_BASE, 8), float(P), None, ALU.mult))
            slot = R(R_C, 24)
            link(e.tensor_tensor(S3(slot), S3(R(R_N + 8, 24)), R(R_BASE, 8).unsqueeze(1).broadcast_to([P, 3, NE]),
                                 ALU.add))
            link(e.scalar_tensor_tensor(out=slot, in0=slot, scalar=1.0, in1=sel, op0=ALU.add, op1=ALU.mult))
            link(e.tensor_scalar(slot, slot, -1.0, None, ALU.add))
            n3 = 3 * NBLK * NE
            b4 = lambda ap: ap.rearrange("p (t b e) -> p t b e", b=NBLK, e=NE)
            blk4 = ct("blk", NBLK).unsqueeze(1).unsqueeze(3).broadcast_to([P, 3, NBLK, NE])
            over_b = lambda ap: S3(ap).unsqueeze(2).broadcast_to([P, 3, NBLK, NE])
            link(e.tensor_tensor(b4(R(R_REL, n3)), over_b(slot), blk4, ALU.subtract))
            link(e.tensor_scalar(R(R_M, n3), R(R_REL, n3), 0.0, None, ALU.is_ge))
            link(e.scalar_tensor_tensor(out=R(R_M, n3), in0=R(R_REL, n3), scalar=float(P), in1=R(R_M, n3),
                                        op0=ALU.is_lt, op1=ALU.mult))
            link(e.scalar_tensor_tensor(out=R(R_REL, n3), in0=R(R_REL, n3), scalar=1.0, in1=R(R_M, n3),
                                        op0=ALU.add, op1=ALU.mult))
            link(e.tensor_reduce(colpos[:], b4(R(R_REL, n3)), AX.X, ALU.add))
            link(e.tensor_scalar(colpos[:], colpos[:], -1.0, None, ALU.add))
            link(e.tensor_tensor(b4(R(R_M, n3)), b4(R(R_M, n3)), over_b(R(R_W, 24)), ALU.mult))
            link(e.tensor_reduce(colw[:], b4(R(R_M, n3)), AX.X, ALU.add))
            be = R(R_REL, NBLK * NE).rearrange("p (b e) -> p b e", e=NE)
            link(e.tensor_tensor(be, R(R_BASE, 8).unsqueeze(1).broadcast_to([P, NBLK, NE]),
                                 ct("blk", NBLK).unsqueeze(2).broadcast_to([P, NBLK, NE]), ALU.is_le))
            link(e.tensor_reduce(R(R_T, NBLK), be, AX.X, ALU.add))
            link(e.tensor_scalar(R(R_T, NBLK), R(R_T, NBLK), -1.0, None, ALU.add))
            link(e.tensor_copy(ebi[:], R(R_T, NBLK)))
            link(e.memset(acc[:], 0.0))

            def pick(b):
                for t, m in enumerate(TT):
                    ins = e.tensor_scalar(sm[0:m, t, :], ct("iota", P)[0:m, :],
                                          colpos[0:m, t, bass.ds(b, 1)], None, ALU.is_equal)
                ins.then_inc(s_ready, 1)

            def tokens(n):
                e.wait_ge(xg_hi_ready, n + 1)
                for h in range(2):
                    ins = low(1, xg_lo[:, 4 * h:4 * h + 4, :].rearrange("p a s -> p (a s)"),
                              xg_hi[:, 4 * h:4 * h + 4, :].rearrange("p a s -> p (a s)"), ps[6 + h][:])
                ins.then_inc(xg_ready, 1)

            pick(0)
            e.wait_ge(s_ready, 1)
            e.sem_inc(routed, 1)
            nblk = e.value_load(nbi[0:1, 0:1], min_val=NE, max_val=NBLK - 1)
            tokens(0)
            with e.Fori(0, nblk) as b:
                def mlow(q):
                    if q < MPER and q % 3 != 2:
                        e.wait_ge(m_hi, b * MPER + (q + 1))
                        low(1, mlo[:, q % MSPL, :], mhi[:, q % MSPL, :], mraw[:, q % MRAW, :]
                            ).then_inc(m_lo_dve, 1)

                mlow(0)
                mlow(1)
                for t, m in enumerate(TT):
                    ins = e.tensor_scalar(wc[0:m, t, :], ct("iota", P)[0:m, :], colpos[0:m, t, bass.ds(b, 1)],
                                          colw[0:m, t, bass.ds(b, 1)], ALU.is_equal, ALU.mult)
                ins.then_inc(wc_ready, 1)
                e.wait_ge(g_done, b + 1)
                pick(b + 1)
                for q in range(MPER):
                    if q < 8 and q % 2 == 1:
                        i = q // 2
                        e.wait_ge(m_done, b * MPER + (q + 1))
                        e.wait_ge(gsil_ready, b * 4 + (i + 1))
                        e.tensor_tensor(hblk[:, i * GW:(i + 1) * GW], gsil[:, i % 2, :], ps[2 * (i % 2) + 1][:, 0:GW],
                                        ALU.mult).then_inc(hs_ready, 1)
                    if q == 8:
                        e.wait_ge(hT_hi_ready, b + 1)
                        for n, (bank, w) in enumerate(((4, 512), (0, 512), (1, 384))):
                            hi = hT_hi[:, 4 * n:4 * n + w // P, :].rearrange("p a s -> p (a s)")
                            lo = hT_lo[:, 4 * n:4 * n + w // P, :].rearrange("p a s -> p (a s)")
                            ins = low(1, lo, hi, ps[bank][:, 0:w])
                        ins.then_inc(hT_ready, 1)
                        tokens(b + 1)
                    mlow(q + MSPL)
                for i in range(NT):
                    e.wait_ge(sc_done, b * NT + (i + 2))
                    e.tensor_tensor(acc[:, i, :], acc[:, i, :], ps[4 + i % 4][:, 0:T], ALU.add
                                    ).then_inc(acc_done, 1)
            e.wait_ge(acc_done, nblk * NT + 1)
            for i in range(NT):
                e.scalar_tensor_tensor(out=x[:, i, 0:TP], in0=acc[:, i, 0:TP], scalar=mod[1][:, 40 + i, 0:1],
                                       in1=x[:, i, 0:TP], op0=ALU.mult, op1=ALU.add)
            link(e.tensor_tensor(samples8(acc), samples8(acc), bc_seq(mod[1][:, 40:48, 1:]), ALU.mult))
            e.tensor_tensor(samples8(x), samples8(x), samples8(acc), ALU.add).then_inc(x_final, 1)
            e.wait_ge(x_final, 1)
            norm(4, False)


def kernel(**a):
    import numpy as np
    import concourse.bacc as bacc
    from concourse.bass_utils import run_bass_kernel_spmd

    a = {k: np.asarray(v) for k, v in a.items()}

    def tiles(w):
        k, m = w.shape
        return w.reshape(k // P, P, m // P, P).transpose(2, 1, 0, 3).reshape(m // P, P, k)

    def slices(w, n):
        k, m = w.shape
        return w.reshape(k // P, P, m // n, n).transpose(2, 1, 0, 3).reshape(m // n, P, k // P * n)

    def columns(v):
        v = np.moveaxis(v.reshape(v.shape[:-1] + (v.shape[-1] // P, P)), -1, 0)
        return v.reshape(P, -1)

    parts = []
    for l in range(DEPTH):
        w = tiles(a["w_in"][l])
        parts.append(np.stack([w[24:32], w[16:24]], 1).reshape(16, P, D))
        parts += [w[0:16], w[32:40], tiles(a["w_branch_a"][l]), w[40:48], tiles(a["w_branch_b"][l]),
                  tiles(a["w_out"][l])]
        if l == 0:
            parts.append(np.stack([tiles(a["ffn_w_gate"][0]), tiles(a["ffn_w_up"][0])], 1).reshape(2 * NF, P, D))
            parts.append(a["ffn_w_down"][0].reshape(NF, P, D))
    stream = np.concatenate(parts)
    ada = np.concatenate([slices(a["ada_w"][l], 512) for l in range(DEPTH)]).reshape(DEPTH * NSLICE, P, NT, 512)
    moe = []
    for x in range(NE):
        g, u = slices(a["moe_w_gate"][0, x], GW), slices(a["moe_w_up"][0, x], GW)
        moe += [np.stack([g, u], 1).reshape(8, P, MCH), slices(a["moe_w_down"][0, x], DW)]
    moe = np.concatenate(moe)

    pk = []
    for l in range(DEPTH):
        for n in ("norm1_g", "norm2_g", "rg_conv_w", "rg_conv_b", "rg_ba", "rg_bx", "rg_lambda", "cc_dw_w",
                  "cc_dw_b", "cc_ln_g", "cc_ln_b", "b_branch_b", "ada_b"):
            pk.append(columns(a[n][l]))
        pk.append(a["state_rglru_h"][l].reshape(NB, NT, P).transpose(2, 1, 0).reshape(P, -1))
    pk.append(columns(a["final_norm_g"]))
    c = np.concatenate([a["c_prompt"], a["c_sample"]])
    pk.append(c.reshape(NSEQ, NT, P).transpose(2, 1, 0).reshape(P, -1))
    pk.append(a["moe_router_w"][0].reshape(NT, P, NE).transpose(1, 0, 2).reshape(P, -1))
    pk.append(np.broadcast_to(a["moe_router_b"], (P, NE)))
    cols = np.concatenate(pk, 1)

    f = np.arange(P)
    sel = np.zeros((P, NSEQ), np.float32)
    for q in range(4):
        sel[32 * q:32 * q + NSEQ] = np.eye(NSEQ, dtype=np.float32)
    e8 = np.arange(NE)
    rep = lambda r: np.broadcast_to(np.asarray(r, np.float32).reshape(1, -1), (P, np.size(r)))
    cst = np.concatenate([np.eye(P, dtype=np.float32), (f[:, None] < f[None, :]).astype(np.float32), rep(f), sel,
                          rep(e8[None, :] < e8[:, None]), rep(e8), rep(P * np.arange(NBLK))], 1)

    wrg = np.zeros((DEPTH, P, 2, NT, P), np.float32)
    for w, n in enumerate(("rg_wa", "rg_wx")):
        b = a[n].reshape(DEPTH, NT, 2, 64, 64)
        for h in range(2):
            wrg[:, 64 * h:64 * h + 64, w, :, 64 * h:64 * h + 64] = b[:, :, h].transpose(0, 2, 1, 3)
    x = np.concatenate([a["x_prompt"].reshape(TP, D), a["x_sample"].reshape(NB * TS, D)])
    x = x.T.reshape(NT, P, T).transpose(1, 0, 2)
    rc = a["state_rglru_conv"].reshape(DEPTH, NB, PR, NT, P).transpose(0, 4, 3, 1, 2).reshape(DEPTH, P, NT, NB, PR)
    cc = a["state_cconv"].reshape(DEPTH, NB, PC, NT, P).transpose(0, 4, 3, 1, 2).reshape(DEPTH, P, NT, NB, PC)
    arrays = {k: np.ascontiguousarray(v) for k, v in dict(
        stream=stream, ada=ada, moe=moe, cols=cols, cst=cst, wrg=wrg, x=x, rc=rc, cc=cc).items()}

    nc = bacc.Bacc("TRN2", target_bir_lowering=False, num_devices=1)
    ins = [nc.dram_tensor("in_" + k, v.shape, F32, kind="ExternalInput").ap() for k, v in arrays.items()]
    shapes = dict(y=(P, NT, T), h=(DEPTH, P, NT, NSEQ), rc=(DEPTH, P, NT, NSEQ, PR), cc=(DEPTH, P, NT, NSEQ, PC))
    outs = [nc.dram_tensor("out_" + k, s, F32, kind="ExternalOutput").ap() for k, s in shapes.items()]
    build(nc, *ins, *outs)
    r = run_bass_kernel_spmd(nc, [{"in_" + k: v for k, v in arrays.items()}], core_ids=[0]).results[0]
    y = r["out_y"].transpose(2, 1, 0).reshape(T, D)
    h = r["out_h"].transpose(0, 3, 2, 1).reshape(DEPTH, NSEQ, D)
    rco = r["out_rc"].transpose(0, 3, 4, 2, 1).reshape(DEPTH, NSEQ, PR, D)
    cco = r["out_cc"].transpose(0, 3, 4, 2, 1).reshape(DEPTH, NSEQ, PC, D)
    return (y[:TP].reshape(1, TP, D), y[TP:].reshape(NB, TS, D), h[:, :1], rco[:, :1], cco[:, :1], h[:, 1:],
            rco[:, 1:], cco[:, 1:])
```

```python
from contextlib import ExitStack

import concourse.bass as bass
from concourse import mybir

F32 = mybir.dt.float32
F32R = mybir.dt.float32r
BF16 = mybir.dt.bfloat16
I32 = mybir.dt.int32
ALU = mybir.AluOpType
ACT = mybir.ActivationFunctionType
AX = mybir.AxisListType

P = 128
DEPTH = 2
D = 1024
NT = D // P
TP = 256
NB, TS = 8, 8
T = TP + NB * TS
NSEQ = 1 + NB
KR, KC = 4, 31
PR, PC = KR - 1, KC - 1
XR_W = PR + TP + NB * (PR + TS)
U_W = PC + TP + NB * (PC + TS)
NF = 2816 // P
NE = 8
FE = 1408
NFE = FE // P
EPS = 1e-6

CH = 8 * P
RING = 4
PER_LAYER = 48 + 8 + 8 + 8
DENSE = 3 * NF
C_LAYER = (0, PER_LAYER + DENSE)
NCHUNK = 2 * PER_LAYER + DENSE
NSLICE = 12

MCH = 8 * 352
MRAW, MSPL = 4, 3
MPER = 12
GW, DW = FE // 4, D // 4
NBLK = 12
MDVE = 5 * MCH // 8
TT = (128, 128, 64)

_COL = {}
_n = 0
for _l in range(DEPTH):
    for _name, _w in (("n1g", NT), ("n2g", NT), ("rgw", KR * NT), ("rgb", NT), ("ba", NT), ("bx", NT),
                      ("lam", NT), ("ccw", KC * NT), ("ccb", NT), ("lng", NT), ("lnb", NT), ("bbb", NT),
                      ("adab", 48), ("h0", NT * NB)):
        _COL[_name, _l] = _n
        _n += _w
for _name, _w in (("fg", NT), ("c", NT * NSEQ), ("wr", NT * NE), ("br", NE)):
    _COL[_name] = _n
    _n += _w
NCOL = _n
_CST = {}
_n = 0
for _name, _w in (("ident", P), ("tri", P), ("iota", P), ("sel", NSEQ), ("jlt", NE * NE), ("eidx", NE),
                  ("blk", NBLK)):
    _CST[_name] = _n
    _n += _w
NCST = _n


def build(nc, stream, ada, moe, cols_d, cst_d, wrg_d, x_d, rc_d, cc_d, y_o, h_o, rc_o, cc_o):
    with ExitStack() as ctx:
        def sem(name):
            return ctx.enter_context(nc.semaphore(name))

        at = [16512]

        def place(name, shape, dt, offset=None):
            size = 2 if dt == BF16 else 4
            for n in shape[1:]:
                size *= n
            if offset is None:
                offset = at[0]
                at[0] += (size + 31) // 32 * 32
            return nc.alloc_sbuf_tensor_at(name, shape, dt, offset=offset)

        x = place("x", [P, NT, T], F32)
        cols = place("cols", [P, NCOL], F32)
        cst = place("cst", [P, NCST], F32)
        ones = place("ones", [P, P], F32)
        eps = place("eps", [P, 1], F32)
        sp8 = place("sp8", [P, DEPTH, NT], F32)
        csil = place("csil", [P, NT, 32], F32)
        small = place("small", [P, 8, DEPTH, NT], F32)
        mod = [place(f"mod{l}", [P, 48, NSEQ], F32) for l in range(DEPTH)]
        modrow = place("modrow", [P, 512], F32)
        std = place("std", [P, T], F32)
        rstd = place("rstd", [P, T], F32)
        mean = place("mean", [P, T], F32)
        hlast = place("hlast", [P, NT, NSEQ], F32)
        rclast = place("rclast", [P, NT, NSEQ, PR], F32)
        nbi = place("nbi", [P, 2], I32)
        ebi = place("ebi", [P, NBLK], I32)
        o_xn = at[0]
        xn_hi = place("xn_hi", [P, NT, T], F32R)
        xn_lo = place("xn_lo", [P, NT, T], F32R)
        o_tmp = at[0]
        tmp = place("tmp", [P, RING, T], F32)
        wrg = place("wrg", [P, 2, NT, P], F32)
        o_ring = at[0]
        raw = place("raw", [P, RING, CH], F32)
        whi = place("whi", [P, RING, CH], F32R)
        wlo = place("wlo", [P, RING, CH], F32R)
        o_arena = at[0]
        gy = place("gy", [P, NT, T], F32)
        sga = place("sga", [P, NT, T], F32)
        upad = place("upad", [P, NT, U_W], F32)
        o_xr = at[0]
        xrp = place("xrp", [P, NT, XR_W], F32)
        th = place("th", [P, NT, T], F32, o_xr)
        o_xc = at[0]
        xc = place("xc", [P, NT, T], F32)
        sgb = place("sgb", [P, NT, T], F32, o_xc)
        o_a = at[0]
        ab = place("ab", [P, NT, T], F32)
        q_hi = place("q_hi", [P, NT, T], F32R, o_a)
        o_b = at[0]
        bb = place("bb", [P, NT, T], F32)
        q_lo = place("q_lo", [P, NT, T], F32R, o_b)
        o_v = at[0]
        v = place("v", [P, NT, T], F32)
        assert o_v + 18432 <= 229344, o_v
        h_hi = place("h_hi", [P, NF, T], F32R, o_arena)
        h_lo = place("h_lo", [P, NF, T], F32R, o_arena + NF * T * 4)
        assert o_arena + 2 * NF * T * 4 <= o_a
        adas = [[place(f"ada0_{i}", [P, NT, 512], F32, o_arena + 16384 * i) for i in range(4)],
                [place("ada1_0", [P, NT, 512], F32, o_v), place("ada1_1", [P, NT, 512], F32, o_a)]]
        mraw = place("mraw", [P, MRAW, MCH], F32, o_ring)
        assert MRAW * MCH * 4 <= o_arena - o_ring
        mhi = place("mhi", [P, MSPL, MCH], F32R, o_arena)
        mlo = place("mlo", [P, MSPL, MCH], F32R, o_arena + MSPL * MCH * 4)
        assert o_arena + 2 * MSPL * MCH * 4 <= o_b
        hn_tok = place("hn_tok", [P, 3, 3, D], BF16, o_v)
        acc = place("acc", [P, NT, T], F32, o_xn)
        route = place("route", [P, 2560], F32, o_xn)
        xg_hi = place("xg_hi", [P, NT, P], F32R, o_xn + 10240)
        xg_lo = place("xg_lo", [P, NT, P], F32R, o_xn + 10240 + 4096)
        hT_hi = place("hT_hi", [P, NFE, P], F32R, o_tmp)
        hT_lo = place("hT_lo", [P, NFE, P], F32R, o_tmp + 5632)
        o_h = o_arena + 2 * MSPL * MCH * 4
        hblk = place("hblk", [P, FE], F32, o_h)
        gsil = place("gsil", [P, 2, GW], F32, o_h + 5632)
        yblk = place("yblk", [P, D], F32, o_h + 5632 + 2816)
        rest = place("rest", [P, 3, D], F32, o_h)
        assert o_h + 5632 + 2816 + 4096 <= o_v and o_h > o_a
        o_s = o_ring + MRAW * MCH * 4
        sm = place("sm", [P, 3, P], BF16, o_s)
        wc = place("wc", [P, 3, P], F32, o_s + 1536)
        wct = place("wct", [P, T], F32, o_xn + 10240 + 8192)
        colpos = place("colpos", [P, 3, NBLK], F32, o_s + 3072)
        colw = place("colw", [P, 3, NBLK], F32, o_s + 3072 + 160)
        assert o_s + 3072 + 320 <= o_arena

        ps = [ctx.enter_context(nc.psum_tensor(f"ps{i}", [P, 512], F32)) for i in range(8)]

        def col(name, l, i):
            n = _COL[name, l] if l is not None else _COL[name]
            return cols[:, bass.ds(n + i, 1)]

        def cv(name, l, w):
            n = _COL[name, l] if l is not None else _COL[name]
            return cols[:, n:n + w]

        def ct(name, w):
            return cst[:, _CST[name]:_CST[name] + w]

        ident = ct("ident", P)

        x_in = sem("x_in")
        wrg_in = sem("wrg_in")
        rc_in = sem("rc_in")
        raw_landed = [sem(f"raw_landed{i}") for i in range(RING)]
        hi_ready = sem("hi_ready")
        lo_ready = sem("lo_ready")
        chunk_done = sem("chunk_done")
        evac_done = sem("evac_done")
        tmp_used = sem("tmp_used")
        ada_landed = [sem(f"ada_landed{i}") for i in range(4)]
        ada_rows = sem("ada_rows")
        row_copied = sem("row_copied")
        ada_turned = sem("ada_turned")
        mod_copied = sem("mod_copied")
        mod_ready = sem("mod_ready")
        csil_ready = sem("csil_ready")
        pad_ready = sem("pad_ready")
        const_ready = sem("const_ready")
        sq_ready = sem("sq_ready")
        stat_done = sem("stat_done")
        std_ready = sem("std_ready")
        xs_ready = sem("xs_ready")
        hn_ready = sem("hn_ready")
        norm_ready = sem("norm_ready")
        rg_done = sem("rg_done")
        rg_sig = sem("rg_sig")
        rg_exp = sem("rg_exp")
        rg_sq = sem("rg_sq")
        rg_root = sem("rg_root")
        q_ready = sem("q_ready")
        conv_step = sem("conv_step")
        ln_cent = sem("ln_cent")
        ln_act = sem("ln_act")
        v_ready = sem("v_ready")
        m_ready = sem("m_ready")
        dve_c = sem("dve_c")
        act_c = sem("act_c")
        out_done = sem("out_done")
        st_ready = sem("st_ready")
        m_landed = [sem(f"m_landed{i}") for i in range(MRAW)]
        m_hi = sem("m_hi")
        m_lo_dve = sem("m_lo_dve")
        m_lo_pool = sem("m_lo_pool")
        hn_part = sem("hn_part")
        hn_rest = sem("hn_rest")
        hn_last = sem("hn_last")
        acc_zero = sem("acc_zero")
        m_done = sem("m_done")
        r_pe = sem("r_pe")
        r_dve = sem("r_dve")
        routed = sem("routed")
        s_ready = sem("s_ready")
        g_done = sem("g_done")
        wc_ready = sem("wc_ready")
        wt_done = sem("wt_done")
        wct_ready = sem("wct_ready")
        xg_hi_ready = sem("xg_hi_ready")
        xg_ready = sem("xg_ready")
        gsil_ready = sem("gsil_ready")
        hs_ready = sem("hs_ready")
        ht_done = sem("ht_done")
        hT_hi_ready = sem("hT_hi_ready")
        hT_ready = sem("hT_ready")
        y_ready = sem("y_ready")
        sc_done = sem("sc_done")
        acc_done = sem("acc_done")
        x_final = sem("x_final")
        y_out = sem("y_out")
        r_act = sem("r_act")

        def seg(buf, i, hist, off):
            w = hist + TS
            p0 = hist + TP
            prompt = buf[:, i, off:off + TP]
            s = buf[:, i, p0:p0 + NB * w].rearrange("p (b t) -> p b t", b=NB)[:, :, off:off + TS]
            return prompt, s

        def samples(ap):
            return ap[:, TP:T].rearrange("p (b t) -> p b t", b=NB)

        def samples8(buf):
            return buf[:, :, TP:T].rearrange("p i (b t) -> p i b t", b=NB)

        def bc_t(ap):
            return ap.unsqueeze(2).broadcast_to([P, NB, TS])

        def stages(l):
            c = C_LAYER[l]
            return dict(gg=c, xr=c + 16, yr=c + 24, ga=c + 32, ba=c + 40, gb=c + 48, bb=c + 56, wo=c + 64,
                        gu=c + 72, dn=c + 72 + 2 * NF)

        E_OFF = (0, NF - NT)
        T_BASE = (0, 16 + 8 + 8 + 2 * NF + NT)
        T_GU = 32
        CONVS = 2 * NT * (KR + KC)
        STORES = 16 * (3 + NT)
        R_SEL, R_P, R_T, R_W, R_C, R_N, R_BASE = 0, 24, 48, 64, 88, 112, 144
        R_A, R_B = 160, 352
        R_REL, R_M = 560, 560 + 3 * NBLK * NE

        block = ctx.enter_context(nc.Block())

        @block.sync
        def _(e):
            e.dma_start(cols[:], cols_d).then_inc(x_in, 16)
            e.dma_start(cst[:], cst_d).then_inc(x_in, 16)
            e.dma_start(x[:], x_d).then_inc(x_in, 16)
            for s in range(4):
                e.dma_start(adas[0][s][:], ada[s]).then_inc(ada_landed[s], 16)
            with e.Fori(0, NSLICE // 4 - 1) as g:
                for s in range(4):
                    e.wait_ge(ada_rows, g * 4 + s + 1)
                    e.dma_start(adas[0][s][:], ada[g * 4 + s + 4]).then_inc(ada_landed[s], 16)

            def chunk(c_static, c):
                s = c_static % RING
                e.dma_start(raw[:, s, :], stream[c]).then_inc(raw_landed[s], 16)

            for c in range(RING):
                chunk(c, c)
            e.dma_start(wrg[:], wrg_d[0]).then_inc(wrg_in, 16)

            def run(c0, n):
                k, r = n // 4, n % 4
                if k:
                    with e.Fori(0, k) as g:
                        for j in range(4):
                            e.wait_ge(lo_ready, g * 4 + (c0 + j - RING + 1))
                            chunk(c0 + j, g * 4 + (c0 + j))
                for j in range(4 * k, n):
                    e.wait_ge(lo_ready, c0 + j - RING + 1)
                    chunk(c0 + j, c0 + j)

            def states(l):
                for i in range(NT):
                    for buf, h, src in ((xrp, PR, rc_d), (upad, PC, cc_d)):
                        e.dma_start(buf[:, i, h + TP:].rearrange("p (b t) -> p b t", b=NB)[:, :, 0:h],
                                    src[l, :, i]).then_inc(rc_in, 16)

            st0, st1 = stages(0), stages(1)
            e.wait_ge(ada_rows, NSLICE)
            states(0)
            run(RING, st0["bb"] - RING)

            def store_states(l):
                e.wait_ge(st_ready, 2 * l + 1)
                e.dma_start(rc_o[l], rclast[:]).then_inc(out_done, 16)
                e.wait_ge(st_ready, 2 * l + 2)
                e.dma_start(h_o[l], hlast[:]).then_inc(out_done, 16)
                e.wait_ge(tmp_used, T_BASE[l] + 16)
                e.dma_start(cc_o[l, :, :, 0, :], upad[:, :, TP:TP + PC]).then_inc(out_done, 16)
                for i in range(NT):
                    e.dma_start(cc_o[l, :, i, 1:NSEQ, :], upad[:, i, PC + TP:].rearrange(
                        "p (b t) -> p b t", b=NB)[:, :, TS:TS + PC]).then_inc(out_done, 16)

            store_states(0)
            run(st0["bb"], 8 + 4)
            e.wait_ge(out_done, STORES)
            e.wait_ge(m_ready, NT)
            e.dma_start(adas[1][0][:], ada[NSLICE]).then_inc(ada_landed[0], 16)
            e.wait_ge(rg_done, 2 * NT)
            e.dma_start(wrg[:], wrg_d[1]).then_inc(wrg_in, 16)
            run(st0["wo"] + 4, 4 + 4)
            e.wait_ge(norm_ready, 2 * NT)
            e.dma_start(adas[1][1][:], ada[NSLICE + 1]).then_inc(ada_landed[1], 16)
            with e.Fori(0, 5) as g:
                for h in range(2):
                    for j in range(4):
                        c = st0["gu"] + 4 + 4 * h + j
                        e.wait_ge(lo_ready, g * 8 + (c - RING + 1))
                        chunk(c, g * 8 + c)
                    e.wait_ge(ada_rows, g * 2 + (NSLICE + h + 1))
                    e.dma_start(adas[1][h][:], ada[g * 2 + (NSLICE + h + 2)]).then_inc(ada_landed[h], 16)
            run(st0["dn"], NF)
            run(st1["gg"], 4)
            e.wait_ge(chunk_done, st1["gg"])
            states(1)
            run(st1["gg"] + 4, 72 - 4 - 16)
            store_states(1)
            run(st1["bb"], 16)
            e.wait_ge(chunk_done, NCHUNK)
            for k in range(MRAW):
                e.dma_start(mraw[:, k, :], moe[k]).then_inc(m_landed[k], 16)

            def freed(n):
                e.wait_ge(m_lo_dve, n + 1)
                e.wait_ge(m_lo_pool, n + 1)

            for k in range(MRAW, MPER):
                freed(k - MRAW)
                e.dma_start(mraw[:, k % MRAW, :], moe[k]).then_inc(m_landed[k % MRAW], 16)
            e.wait_ge(routed, 1)
            nblk = e.value_load(nbi[0:1, 0:1], min_val=NE, max_val=NBLK)
            with e.Fori(1, nblk) as b:
                ex = e.value_load(ebi[0:1, bass.ds(b, 1)], min_val=0, max_val=NE - 1)
                for k in range(MPER):
                    freed(b * MPER + (k - MRAW))
                    e.dma_start(mraw[:, k % MRAW, :], moe[ex * MPER + k]).then_inc(m_landed[k % MRAW], 16)
            for i in range(NT):
                e.wait_ge(y_out, i + 1)
                e.dma_start(y_o[:, i, :], bb[:, i, :]).then_inc(out_done, 16)
            e.wait_ge(out_done, DEPTH * STORES + 16 * NT)


        @block.gpsimd
        def _(e):
            e.memset(ones[:], 1.0).then_inc(const_ready, 1)
            e.memset(eps[:], EPS).then_inc(const_ready, 1)
            e.memset(csil[:], 0.0).then_inc(const_ready, 1)

            def low(c_static, c):
                s = c_static % RING
                e.wait_ge(hi_ready, c + 1)
                e.tensor_tensor(wlo[:, s, :], raw[:, s, :], whi[:, s, :].bitcast(F32), ALU.subtract
                                ).then_inc(lo_ready, 1)

            def run(c0, n):
                k = n // 4
                with e.Fori(0, k) as g:
                    for j in range(4):
                        low(c0 + j, g * 4 + (c0 + j))
                for c in range(c0 + 4 * k, c0 + n):
                    low(c, c)

            def pads():
                e.memset(upad[:, :, 0:PC], 0.0).then_inc(pad_ready, 1)
                e.memset(xrp[:, :, 0:PR], 0.0).then_inc(pad_ready, 1)

            for c in range(4):
                low(c, c)
            e.wait_ge(ada_rows, NSLICE)
            pads()
            g1 = stages(1)["gg"]
            run(4, g1)
            e.wait_ge(chunk_done, g1)
            pads()
            run(g1 + 4, NCHUNK - g1 - 4)

            def mlow(b, q):
                s = q % MPER
                e.wait_ge(m_hi, b * MPER + (q + 1))
                e.tensor_tensor(mlo[:, s % MSPL, MDVE:], mraw[:, s % MRAW, MDVE:],
                                mhi[:, s % MSPL, MDVE:].bitcast(F32), ALU.subtract).then_inc(m_lo_pool, 1)

            for q in range(MSPL):
                mlow(0, q)
            for t, m in enumerate(TT):
                e.wait_ge(hn_part, 6 + t + 1)
                e.tensor_tensor(hn_tok[0:m, 2, t, :], rest[0:m, t, :], hn_tok[0:m, 1, t, :], ALU.subtract
                                ).then_inc(hn_last, 1)
            e.wait_ge(routed, 1)
            e.memset(acc[:], 0.0).then_inc(acc_zero, 1)
            last = e.value_load(nbi[0:1, 1:2], min_val=NE - 1, max_val=NBLK - 1)
            with e.Fori(0, last) as b:
                for q in range(MPER):
                    mlow(b, q + MSPL)
            for q in range(MPER - MSPL):
                mlow(last, q + MSPL)

        @block.tensor
        def _(e):
            def split_mm(out, w, x2, start, stop):
                e.matmul(out, w[0], x2[0], start=start, stop=False)
                e.matmul(out, w[0], x2[1], start=False, stop=False)
                return e.matmul(out, w[1], x2[0], start=False, stop=stop)

            def wtile(s, u):
                return whi[:, s, u * P:(u + 1) * P], wlo[:, s, u * P:(u + 1) * P]

            def main(l, c0, n, xs, ready=None):
                def one(c_static, c, ready=None):
                    s = c_static % RING
                    e.wait_ge(lo_ready, c + 1)
                    if c_static - E_OFF[l] >= RING:
                        e.wait_ge(evac_done, c - (E_OFF[l] + 3))
                    for k in range(NT):
                        if ready is not None:
                            e.wait_ge(*ready(k))
                        mm = split_mm(ps[s][:, 0:T], wtile(s, k), (xs[0][:, k, :], xs[1][:, k, :]),
                                      k == 0, k == NT - 1)
                    mm.then_inc(chunk_done, 1)

                if ready is not None or n < 4:
                    for c in range(c0, c0 + min(n, 4)):
                        one(c, c, ready if c == c0 else None)
                    c0, n = c0 + 4, n - 4
                if n > 0:
                    with e.Fori(0, n // 4) as g:
                        for j in range(4):
                            one(c0 + j, g * 4 + (c0 + j))

            def rows(slot, s, n_landed, mk):
                e.wait_ge(ada_landed[slot], n_landed)
                e.wait_ge(row_copied, s + 1)
                for k in range(NT):
                    q = 32 * (k % 4)
                    mm = e.matmul(ps[5][q:q + 32, :], csil[:, k, :], mk[:, k, :], start=k < 4, stop=k >= 4)
                mm.then_inc(ada_rows, 1)

            def turn(s):
                e.wait_ge(row_copied, s + 2)
                e.wait_ge(mod_copied, s + 1)
                for j in range(4):
                    mm = e.matmul(ps[6][:, NSEQ * j:NSEQ * (j + 1)], modrow[:, j * P:(j + 1) * P],
                                  ct("sel", NSEQ), start=True, stop=True)
                mm.then_inc(ada_turned, 1)

            def stat(buf, waits):
                for i in range(NT):
                    if i in waits:
                        e.wait_ge(*waits[i])
                    mm = e.matmul(ps[4][:, 0:T], ones[:], buf[:, i, :], start=i == 0, stop=i == NT - 1)
                mm.then_inc(stat_done, 1)

            def norm(n):
                stat(ab, {i: (sq_ready, NT * n + i + 1) for i in range(NT)})

            e.sem_inc(ada_turned, 1)
            e.sem_inc(sc_done, 1)
            e.wait_ge(x_in, 48)
            e.wait_ge(csil_ready, 1)
            with e.Fori(0, NSLICE // 4) as g:
                for slot in range(4):
                    rows(slot, g * 4 + slot, g * 16 + 16, adas[0][slot])
                    turn(g * 4 + slot)

            for l in range(DEPTH):
                st = stages(l)
                norm(2 * l)
                xs = (xn_hi, xn_lo)
                main(l, st["gg"], 28, xs, lambda k: (norm_ready, NT * 2 * l + k + 1))
                e.wait_ge(wrg_in, 16 * (l + 1))
                for i in range(NT):
                    if i % 2 == 0:
                        e.wait_ge(conv_step, CONVS * l + 2 * (2 * 2 * KC) + 2 * 2 * KR * (i // 2 + 1))
                    for w in range(2):
                        n = 2 * i + w
                        if n >= 4:
                            e.wait_ge(rg_sig, 2 * NT * l + n - 3)
                        e.matmul(ps[4 + n % 4][:, 0:T], wrg[:, w, i, :], xc[:, i, :], start=True, stop=True
                                 ).then_inc(rg_done, 1)
                main(l, st["yr"] + 4, 4, xs)
                main(l, st["ga"], 8, xs)
                main(l, st["ba"], 8, (q_hi, q_lo), lambda k: (q_ready, 2 * l + k // 4 + 1))
                main(l, st["gb"], 2, xs)
                e.wait_ge(conv_step, CONVS * (l + 1))
                stat(v, {})
                main(l, st["gb"] + 2, 4, xs)
                stat(th, {0: (ln_act, 10 * l + 2)})
                main(l, st["gb"] + 6, 2, xs)
                main(l, st["bb"], 8, (q_hi, q_lo), lambda k: (v_ready, NT * l + k + 1))
                main(l, st["wo"], 8, xs, lambda k: (m_ready, NT * l + k + 1))
                norm(2 * l + 1)
                if l == 0:
                    rows(0, NSLICE, 16 * 4, adas[1][0])
                    turn(NSLICE)

                    def four(g8, h, first):
                        for j in range(4):
                            cs = st["gu"] + 4 * h + j
                            c = g8 + cs
                            s = cs % RING
                            e.wait_ge(lo_ready, c + 1)
                            e.wait_ge(evac_done, c - 3)
                            for k in range(NT):
                                if first and j == 0:
                                    e.wait_ge(norm_ready, NT + k + 1)
                                mm = split_mm(ps[s][:, 0:T], wtile(s, k), (xn_hi[:, k, :], xn_lo[:, k, :]),
                                              k == 0, k == NT - 1)
                            mm.then_inc(chunk_done, 1)

                    four(0, 0, True)
                    rows(1, NSLICE + 1, 16 * 4, adas[1][1])
                    turn(NSLICE + 1)
                    with e.Fori(0, 5) as g:
                        for h in range(2):
                            four(g * 8 + 4, h, False)
                            rows(h, g * 2 + (NSLICE + 2 + h), g * 16 + 16 * 5, adas[1][h])
                            turn(g * 2 + (NSLICE + 2 + h))
                    e.wait_ge(evac_done, st["dn"])
                    e.wait_ge(mod_copied, 2 * NSLICE + 1)

                    def down(cs, k, start, stop):
                        s = cs % RING
                        e.wait_ge(lo_ready, k + (st["dn"] + 1))
                        e.wait_ge(tmp_used, k * 2 + (T_GU + 2))
                        for m in range(NT):
                            mm = split_mm(ps[m][:, 0:T], wtile(s, m),
                                          (h_hi[:, bass.ds(k, 1), :].rearrange("p a t -> p (a t)"),
                                           h_lo[:, bass.ds(k, 1), :].rearrange("p a t -> p (a t)")), start, stop)
                        mm.then_inc(chunk_done, 1)

                    for k in range(4):
                        down(st["dn"] + k, k, k == 0, False)
                    with e.Fori(0, 4) as g:
                        for j in range(4):
                            down(st["dn"] + 4 + j, g * 4 + (4 + j), False, False)
                    for k in range(20, NF):
                        down(st["dn"] + k, k, False, k == NF - 1)

            e.wait_ge(hn_ready, 4 * NT)
            e.wait_ge(norm_ready, 3 * NT + 1)
            for t, m in enumerate(TT):
                for k in range(NT):
                    n = _COL["wr"] + k * NE
                    mm = e.matmul(ps[0][0:m, t * NE:(t + 1) * NE], bb[:, k, t * P:t * P + m],
                                  cols[:, n:n + NE], start=k == 0, stop=k == NT - 1)
            mm.then_inc(r_pe, 1)
            for t, m in enumerate(TT):
                for i in range(NT):
                    mm = e.transpose(ps[2 + 2 * t + i // 4][0:m, (i % 4) * P:(i % 4 + 1) * P],
                                     bb[:, i, t * P:t * P + m], ident)
            mm.then_inc(r_pe, 1)
            e.wait_ge(r_dve, 2)
            sel = route[:, R_SEL:R_SEL + 24]
            for t in range(4):
                for u in range(3 if t == 0 else t):
                    w = ones[:] if t == 0 or u < t - 1 else ct("tri", P)
                    mm = e.matmul(ps[1][:, t * NE:(t + 1) * NE], w, sel[:, u * NE:(u + 1) * NE], start=u == 0,
                                  stop=u == (2 if t == 0 else t - 1))
            mm.then_inc(r_pe, 1)

            def gather(b):
                e.wait_ge(s_ready, b + 1)
                for i in range(NT):
                    for t, m in enumerate(TT):
                        for part in range(3):
                            mm = e.matmul(ps[6 + i // 4][:, (i % 4) * P:(i % 4 + 1) * P],
                                          hn_tok[0:m, part, t, i * P:(i + 1) * P], sm[0:m, t, :],
                                          start=t + part == 0, stop=t + part == 4)
                mm.then_inc(g_done, 1)

            e.wait_ge(routed, 1)
            last = e.value_load(nbi[0:1, 1:2], min_val=NE - 1, max_val=NBLK - 1)
            e.wait_ge(hn_part, 9)
            e.wait_ge(hn_last, 3)
            gather(0)

            def expert(b, more):
                def split_ready(q):
                    e.wait_ge(m_lo_dve, b * MPER + (q + 1))
                    e.wait_ge(m_lo_pool, b * MPER + (q + 1))

                def combine(i):
                    e.wait_ge(y_ready, b * 4 + (i // 2 + 1))
                    if i >= 4:
                        e.wait_ge(acc_done, b * NT + (i - 2))
                    e.matmul(ps[4 + i % 4][:, 0:T], yblk[:, i * P:(i + 1) * P], wct[:], start=True, stop=True
                             ).then_inc(sc_done, 1)

                e.wait_ge(xg_ready, b + 1)
                for q in range(8):
                    i, bank = q // 2, 2 * (q // 2 % 2) + q % 2
                    split_ready(q)
                    if i >= 2:
                        e.wait_ge(hs_ready, b * 4 + (i - 1))
                    for k in range(NT):
                        wh = mhi[:, q % MSPL, k * GW:(k + 1) * GW]
                        wl = mlo[:, q % MSPL, k * GW:(k + 1) * GW]
                        e.matmul(ps[bank][:, 0:GW], xg_hi[:, k, :], wh, start=k == 0, stop=False)
                        e.matmul(ps[bank][:, 0:GW], xg_hi[:, k, :], wl, start=False, stop=False)
                        mm = e.matmul(ps[bank][:, 0:GW], xg_lo[:, k, :], wh, start=False, stop=k == NT - 1)
                    mm.then_inc(m_done, 1)
                e.wait_ge(acc_done, b * NT + 1)
                e.wait_ge(wc_ready, b + 1)
                for t, m in enumerate(TT):
                    mm = e.transpose(ps[5][:, t * P:t * P + m], wc[0:m, t, :], ident[0:m, 0:m])
                mm.then_inc(wt_done, 1)
                if more:
                    gather(b + 1)
                e.wait_ge(hs_ready, b * 4 + 4)
                for f in range(NFE):
                    mm = e.transpose(ps[(4, 0, 1)[f // 4]][:, (f % 4) * P:(f % 4 + 1) * P],
                                     hblk[:, f * P:(f + 1) * P], ident)
                mm.then_inc(ht_done, 1)
                e.wait_ge(hT_ready, b + 1)
                for j in range(4):
                    q = 8 + j
                    split_ready(q)
                    out = ps[(2 + j) % 4][:, 0:DW]
                    for f in range(NFE):
                        wh = mhi[:, q % MSPL, f * DW:(f + 1) * DW]
                        wl = mlo[:, q % MSPL, f * DW:(f + 1) * DW]
                        e.matmul(out, hT_hi[:, f, :], wh, start=f == 0, stop=False)
                        e.matmul(out, hT_hi[:, f, :], wl, start=False, stop=False)
                        mm = e.matmul(out, hT_lo[:, f, :], wh, start=False, stop=f == NFE - 1)
                    mm.then_inc(m_done, 1)
                    if j == 1:
                        e.wait_ge(wct_ready, b + 1)
                        if more:
                            e.wait_ge(xg_ready, b + 2)
                    if j >= 1:
                        combine(2 * j - 2)
                        combine(2 * j - 1)
                combine(6)
                combine(7)

            with e.Fori(0, last) as b:
                expert(b, True)
            expert(last, False)
            norm(4)

        @block.scalar
        def _(e):
            links = [0]

            def link(ins):
                links[0] += 1
                ins.then_inc(act_c, 1)
                e.wait_ge(act_c, links[0])

            def high(c_static, c):
                s = c_static % RING
                e.wait_ge(raw_landed[s], (c - c_static) * 4 + 16 * (c_static // RING + 1))
                if c_static >= RING:
                    e.wait_ge(chunk_done, c - (RING - 1))
                e.activation(whi[:, s, :], raw[:, s, :], ACT.Copy).then_inc(hi_ready, 1)

            def stage(l, c0, n, evac, t0=None, splits=True):
                def one(c_static, c):
                    e.wait_ge(chunk_done, c + 1)
                    if t0 is not None and c_static - c0_first + t0 >= RING:
                        e.wait_ge(tmp_used, c - c0_first + (t0 - RING + 1))
                    evac(c_static - c0_first, c - c0_first, ps[c_static % RING][:, 0:T]).then_inc(evac_done, 1)
                    if splits:
                        high(c_static + RING, c + RING)

                c0_first = c0
                if t0 == 0 or not splits or n < 4:
                    for c in range(c0, c0 + min(n, 4)):
                        one(c, c)
                    c0, n = c0 + 4, n - 4
                if n > 0:
                    with e.Fori(0, n // 4) as g:
                        for j in range(4):
                            one(c0 + j, g * 4 + (c0 + j))

            def tile(buf, i):
                return buf[:, bass.ds(i, 1), :].rearrange("p a t -> p (a t)")

            def ada_copy(s):
                e.wait_ge(ada_rows, s + 1)
                e.wait_ge(ada_turned, s + 1)
                e.activation(modrow[:], ps[5][:], ACT.Copy).then_inc(row_copied, 1)

            def mod_copy(l, s):
                e.wait_ge(ada_turned, s + 2)
                e.activation(mod[l][:, bass.ds((s - NSLICE * l) * 4, 4), :].rearrange("p a b -> p (a b)"),
                             ps[6][:, 0:4 * NSEQ], ACT.Copy).then_inc(mod_copied, 1)

            def square(n, i):
                if n == 4:
                    e.wait_ge(x_final, 1)
                elif n:
                    e.wait_ge(tmp_used, (0, T_GU, T_BASE[1], T_BASE[1] + T_GU)[n] - (NT - 1 - i))
                e.activation(ab[:, i, :], x[:, i, :], ACT.Square).then_inc(sq_ready, 1)

            def norm(n, i0=0):
                l, k = n // 2, n % 2
                for i in range(i0, NT):
                    square(n, i)
                e.wait_ge(stat_done, (0, 3, 4, 7, 8)[n] + 1)
                e.activation(std[:], ps[4][:, 0:T], ACT.Sqrt, bias=eps[:], scale=1.0 / D).then_inc(std_ready, 1)
                if n == 4:
                    for i in range(NT):
                        e.wait_ge(xs_ready, NT * n + i + 1)
                        e.activation(bb[:, i, :], bb[:, i, :], ACT.Copy, scale=col("fg", None, i)
                                     ).then_inc(y_out, 1)
                    return
                for i in range(NT):
                    e.wait_ge(xs_ready, NT * n + i + 1)
                    e.activation(bb[:, i, 0:TP], bb[:, i, 0:TP], ACT.Identity,
                                 scale=mod[l][:, 24 * k + 8 + i, 0:1], bias=mod[l][:, 24 * k + i, 0:1]
                                 ).then_inc(hn_ready, 1)

            e.sem_inc(row_copied, 1)
            e.sem_inc(mod_copied, 1)
            e.wait_ge(x_in, 48)
            e.wait_ge(const_ready, 3)
            e.activation(csil[:, :, 0:NSEQ], cv("c", None, NT * NSEQ).rearrange("p (k b) -> p k b", b=NSEQ),
                         ACT.Silu).then_inc(csil_ready, 1)
            for l in range(DEPTH):
                link(e.activation(small[:, 0, l, :], cv("lam", l, NT), ACT.Abs))
            for l in range(DEPTH):
                e.activation(small[:, 1, l, :], small[:, 0, l, :], ACT.Exp, scale=-1.0).then_inc(csil_ready, 1)
            with e.Fori(0, NSLICE) as s:
                ada_copy(s)
                mod_copy(0, s)
            for c in range(RING):
                high(c, c)

            for l in range(DEPTH):
                st = stages(l)
                tb = T_BASE[l]
                norm(2 * l)

                stage(l, st["gg"], 16,
                      lambda j, i, p: e.activation(tmp[:, j % RING, :], p, ACT.Sigmoid if j % 2 == 0 else ACT.Copy),
                      t0=tb)

                def evac_xr(j, i, p):
                    e.activation(xrp[:, bass.ds(i, 1), PR:PR + TP].rearrange("p a t -> p (a t)"), p[:, 0:TP],
                                 ACT.Copy)
                    return e.activation(sa_of(xrp, i, PR), samples(p), ACT.Copy)

                def sa_of(buf, i, hist):
                    w = hist + TS
                    row = buf[:, bass.ds(i, 1), hist + TP:hist + TP + NB * w].rearrange("p a w -> p (a w)")
                    return row.rearrange("p (b t) -> p b t", b=NB)[:, :, hist:hist + TS]

                stage(l, st["xr"], 8, evac_xr)
                stage(l, st["yr"], 4, lambda j, i, p: e.activation(tile(gy, i), p, ACT.Gelu_apprx_tanh))

                for i in range(NT):
                    for w, (buf, b) in enumerate(((ab, "ba"), (bb, "bx"))):
                        n = 2 * i + w
                        e.wait_ge(rg_done, 2 * NT * l + n + 1)
                        e.activation(buf[:, i, :], ps[4 + n % 4][:, 0:T], ACT.Sigmoid, bias=col(b, l, i)
                                     ).then_inc(rg_sig, 1)
                stage(l, st["yr"] + 4, 4, lambda j, i, p: e.activation(tile(gy, i + 4), p, ACT.Gelu_apprx_tanh))
                e.wait_ge(st_ready, 2 * l + 1)
                e.wait_ge(rg_sig, 2 * NT * (l + 1))
                for i in range(NT):
                    e.activation(th[:, i, :], ab[:, i, :], ACT.Tanh, scale=sp8[:, l, i:i + 1])
                    ins = e.activation(ab[:, i, :], ab[:, i, :], ACT.Exp, scale=sp8[:, l, i:i + 1])
                ins.then_inc(rg_exp, 1)
                stage(l, st["ga"], 4, lambda j, i, p: e.activation(tile(sga, i), p, ACT.Sigmoid))
                e.wait_ge(rg_sq, l + 1)
                e.activation(th[:], th[:], ACT.Sqrt, scale=-1.0).then_inc(rg_root, 1)
                stage(l, st["ga"] + 4, 4, lambda j, i, p: e.activation(tile(sga, i + 4), p, ACT.Sigmoid))
                stage(l, st["ba"], 8, lambda j, i, p: e.activation(tile(gy, i), p, ACT.Copy))
                def gate_b(j0):
                    stage(l, st["gb"] + j0, 2, lambda j, i, p: e.activation(tile(sgb, i + j0), p, ACT.Sigmoid))

                gate_b(0)
                e.wait_ge(stat_done, 4 * l + 2)
                e.activation(mean[:], ps[4][:, 0:T], ACT.Copy, scale=1.0 / D).then_inc(ln_act, 1)
                gate_b(2)
                e.wait_ge(ln_cent, (1 + NT) * l + 1)
                e.activation(th[:], v[:], ACT.Square).then_inc(ln_act, 1)
                gate_b(4)
                e.wait_ge(stat_done, 4 * l + 3)
                e.activation(std[:], ps[4][:, 0:T], ACT.Sqrt, bias=eps[:], scale=1.0 / D).then_inc(std_ready, 1)
                gate_b(6)
                for i in range(NT):
                    e.wait_ge(ln_cent, (1 + NT) * l + 1 + i + 1)
                    e.activation(v[:, i, :], v[:, i, :], ACT.Silu, scale=col("lng", l, i), bias=col("lnb", l, i)
                                 ).then_inc(ln_act, 1)
                stage(l, st["bb"], 8, lambda j, i, p: e.activation(tmp[:, j % RING, :], p, ACT.Identity,
                                                                   bias=col("bbb", l, i)), t0=tb + 16)
                ev_tmp = lambda j, i, p: e.activation(tmp[:, j % RING, :], p, ACT.Copy)
                stage(l, st["wo"], 4, ev_tmp, t0=tb + 24)
                for j in range(4):
                    stage(l, st["wo"] + 4 + j, 1, lambda _, i, p: ev_tmp(j, i, p), t0=tb + 28 + j, splits=l == 0)
                    square(2 * l + 1, j)
                norm(2 * l + 1, 4)
                if l == 0:
                    ada_copy(NSLICE)
                    mod_copy(1, NSLICE)
                    gu = lambda j, i, p: e.activation(tmp[:, j % RING, :], p, ACT.Silu if j % 2 == 0 else ACT.Copy)

                    def four(g8, c0):
                        for j in range(4):
                            c = g8 + (c0 + j)
                            e.wait_ge(chunk_done, c + 1)
                            e.wait_ge(tmp_used, c + (T_GU - st["gu"] - RING + 1))
                            gu(j, None, ps[(c0 + j) % RING][:, 0:T]).then_inc(evac_done, 1)
                            high(c0 + j + RING, c + RING)

                    four(0, st["gu"])
                    ada_copy(NSLICE + 1)
                    mod_copy(1, NSLICE + 1)
                    with e.Fori(0, 5) as g:
                        for h in range(2):
                            four(g * 8, st["gu"] + 4 + 4 * h)
                            ada_copy(g * 2 + (NSLICE + 2 + h))
                            mod_copy(1, g * 2 + (NSLICE + 2 + h))
                    with e.Fori(0, NF // 4) as g:
                        for j in range(4):
                            high(st["dn"] + 4 + j, g * 4 + (st["dn"] + 4 + j))
                    for c in range(st["dn"] + 20 + 4, st["dn"] + NF + 4):
                        high(c, c)
                    e.wait_ge(chunk_done, st["dn"] + NF)
                    for m in range(NT):
                        e.wait_ge(tmp_used, T_GU + 2 * NF + m - 3)
                        e.activation(tmp[:, m % RING, :], ps[m][:, 0:T], ACT.Copy).then_inc(evac_done, 1)

            def mhigh(b, q):
                s = q % MPER
                e.wait_ge(m_landed[s % MRAW], b * (16 * MPER // MRAW) + 16 * (q // MRAW + 1))
                if q >= MSPL:
                    e.wait_ge(m_done, b * MPER + (q - MSPL + 1))
                e.activation(mhi[:, s % MSPL, :], mraw[:, s % MRAW, :], ACT.Copy).then_inc(m_hi, 1)

            for q in range(MSPL):
                mhigh(0, q)
            e.wait_ge(r_dve, 1)
            e.activation(route[:, R_P:R_P + 24], route[:, R_P:R_P + 24], ACT.Exp).then_inc(r_act, 1)
            e.wait_ge(r_pe, 2)
            for t, m in enumerate(TT):
                for h in range(2):
                    e.activation(hn_tok[0:m, 0, t, h * 512:(h + 1) * 512], ps[2 + 2 * t + h][0:m, :], ACT.Copy
                                 ).then_inc(hn_part, 1)
            for t, m in enumerate(TT):
                e.wait_ge(hn_rest, 2 * t + 2)
                e.activation(hn_tok[0:m, 1, t, :], rest[0:m, t, :], ACT.Copy).then_inc(hn_part, 1)
            e.wait_ge(routed, 1)
            last = e.value_load(nbi[0:1, 1:2], min_val=NE - 1, max_val=NBLK - 1)

            def gathered(n):
                e.wait_ge(g_done, n + 1)
                for h in range(2):
                    ins = e.activation(xg_hi[:, 4 * h:4 * h + 4, :].rearrange("p a s -> p (a s)"), ps[6 + h][:],
                                       ACT.Copy)
                ins.then_inc(xg_hi_ready, 1)

            gathered(0)

            def expert(b, more):
                for q in range(MPER):
                    if q < 8 and q % 2 == 0:
                        i = q // 2
                        e.wait_ge(m_done, b * MPER + (q + 1))
                        if i >= 2:
                            e.wait_ge(hs_ready, b * 4 + (i - 1))
                        e.activation(gsil[:, i % 2, :], ps[2 * (i % 2)][:, 0:GW], ACT.Silu).then_inc(gsil_ready, 1)
                    if q == 8:
                        e.wait_ge(wt_done, b + 1)
                        e.wait_ge(sc_done, b * NT + 1)
                        e.activation(wct[:], ps[5][:, 0:T], ACT.Copy).then_inc(wct_ready, 1)
                        if more:
                            gathered(b + 1)
                        e.wait_ge(ht_done, b + 1)
                        for n, (bank, w) in enumerate(((4, 512), (0, 512), (1, 384))):
                            e.activation(hT_hi[:, 4 * n:4 * n + w // P, :].rearrange("p a s -> p (a s)"),
                                         ps[bank][:, 0:w], ACT.Copy).then_inc(hT_hi_ready, 1)
                    if q >= 8:
                        j = q - 8
                        e.wait_ge(m_done, b * MPER + (q + 1))
                        e.activation(yblk[:, j * DW:(j + 1) * DW], ps[(2 + j) % 4][:, 0:DW],
                                     ACT.Copy).then_inc(y_ready, 1)
                    if q + MSPL < MPER or more:
                        mhigh(b, q + MSPL)

            with e.Fori(0, last) as b:
                expert(b, True)
            expert(last, False)
            norm(4)

        @block.vector
        def _(e):
            links = [0]

            def link(ins):
                links[0] += 1
                ins.then_inc(dve_c, 1)
                e.wait_ge(dve_c, links[0])

            def low(n, out, hi, src):
                return e.tensor_tensor(out, src, hi.bitcast(F32), ALU.subtract)

            def bc_tiles(ap, w):
                return ap.unsqueeze(1).broadcast_to([P, NT, w])

            def bc_seq(ap):
                return ap.unsqueeze(3).broadcast_to([P, NT, NB, TS])

            def norm(n, split):
                l, k = n // 2, n % 2
                e.wait_ge(std_ready, (1, 3, 4, 6, 7)[n])
                link(e.reciprocal(rstd[:], std[:]))
                if n == 4:
                    for i in range(NT):
                        e.tensor_tensor(bb[:, i, :], x[:, i, :], rstd[:], ALU.mult).then_inc(xs_ready, 1)
                    return
                for i in range(NT):
                    e.tensor_tensor(bb[:, i, 0:TP], x[:, i, 0:TP], rstd[:, 0:TP], ALU.mult).then_inc(xs_ready, 1)
                link(e.tensor_tensor(bb[:, :, TP:T], x[:, :, TP:T], bc_tiles(rstd[:, TP:T], T - TP), ALU.mult))
                link(e.tensor_tensor(samples8(bb), samples8(bb), bc_seq(mod[l][:, 24 * k + 8:24 * k + 16, 1:]),
                                     ALU.mult))
                link(e.tensor_tensor(samples8(bb), samples8(bb), bc_seq(mod[l][:, 24 * k:24 * k + 8, 1:]),
                                     ALU.add))
                if not split:
                    e.sem_inc(norm_ready, 1)
                else:
                    for i in range(NT):
                        e.wait_ge(hn_ready, NT * n + i + 1)
                        link(e.tensor_copy(xn_hi[:, i, :], bb[:, i, :]))
                        low(1, xn_lo[:, i, :], xn_hi[:, i, :], bb[:, i, :]).then_inc(norm_ready, 1)

            conv_n = [0]

            def conv(l, K, pair, srcs, dst, w, b, between=None):
                for k in range(K):
                    if between and k in between:
                        between[k]()
                    for t in range(2):
                        i = 2 * pair + t
                        pr, sa = seg(srcs, i, K - 1, k)
                        for src, out in ((pr, dst[:, i, 0:TP]), (sa, samples(dst[:, i, :]))):
                            if k == 0:
                                ins = e.tensor_scalar(out, src, col(w, l, i), col(b, l, i), ALU.mult, ALU.add)
                            else:
                                e.wait_ge(conv_step, conv_n[0] - 3)
                                ins = e.scalar_tensor_tensor(out=out, in0=src, scalar=col(w, l, k * NT + i),
                                                             in1=out, op0=ALU.mult, op1=ALU.add)
                            ins.then_inc(conv_step, 1)
                            conv_n[0] += 1

            def finish_mod(l):
                e.wait_ge(mod_copied, NSLICE * (l + 1) + 1)
                m = mod[l]
                link(e.tensor_tensor(m[:], m[:], cv("adab", l, 48).unsqueeze(2).broadcast_to([P, 48, NSEQ]), ALU.add))
                for k, g in ((8, "n1g"), (32, "n2g")):
                    e.scalar_tensor_tensor(out=m[:, k:k + 8, :], in0=m[:, k:k + 8, :], scalar=1.0,
                                           in1=cv(g, l, NT).unsqueeze(2).broadcast_to([P, NT, NSEQ]),
                                           op0=ALU.add, op1=ALU.mult).then_inc(mod_ready, 1)
                for k in (16, 40):
                    e.tensor_scalar(m[:, k:k + 8, :], m[:, k:k + 8, :], 1.0, None, ALU.add).then_inc(mod_ready, 1)
                e.wait_ge(mod_ready, 4 * (l + 1))

            def residual(l, k, i, src, last):
                e.scalar_tensor_tensor(out=x[:, i, 0:TP], in0=src[:, 0:TP], scalar=mod[l][:, k + i, 0:1],
                                       in1=x[:, i, 0:TP], op0=ALU.mult, op1=ALU.add)
                link(e.tensor_tensor(samples(src), samples(src), bc_t(mod[l][:, k + i, 1:]), ALU.mult))
                e.tensor_tensor(samples(x[:, i, :]), samples(x[:, i, :]), samples(src), ALU.add
                                ).then_inc(last, 1)

            e.sem_inc(acc_done, 1)
            e.wait_ge(x_in, 48)
            e.wait_ge(csil_ready, 1 + DEPTH)
            lam2 = [small[:, k, :, :].rearrange("p l i -> p (l i)") for k in range(8)]
            link(e.tensor_scalar(lam2[2], lam2[1], 2.0, None, ALU.add))
            link(e.reciprocal(lam2[3], lam2[2]))
            link(e.tensor_tensor(lam2[4], lam2[1], lam2[3], ALU.mult))
            link(e.tensor_tensor(lam2[5], lam2[4], lam2[4], ALU.mult))
            link(e.tensor_scalar(lam2[6], lam2[5], 1.0 / 19, None, ALU.mult))
            for k in range(8, 0, -1):
                link(e.scalar_tensor_tensor(out=lam2[6], in0=lam2[6], scalar=1.0 / (2 * k + 1), in1=lam2[5],
                                            op0=ALU.add, op1=ALU.mult))
            link(e.scalar_tensor_tensor(out=lam2[6], in0=lam2[6], scalar=1.0, in1=lam2[4], op0=ALU.add,
                                        op1=ALU.mult))
            for l in range(DEPTH):
                link(e.tensor_scalar(small[:, 7, l, :], cv("lam", l, NT), -1.0, 0.0, ALU.mult, ALU.max))
            link(e.scalar_tensor_tensor(out=lam2[6], in0=lam2[6], scalar=2.0, in1=lam2[7], op0=ALU.mult,
                                        op1=ALU.add))
            link(e.tensor_scalar(sp8[:].rearrange("p l i -> p (l i)"), lam2[6], -8.0, None, ALU.mult))

            flat = lambda buf: buf[:].rearrange("p i t -> p (i t)")
            for l in range(DEPTH):
                st = stages(l)
                tb, eo = T_BASE[l], E_OFF[l]
                finish_mod(l)
                norm(2 * l, True)
                if l == 0:
                    e.wait_ge(pad_ready, 2)
                def make_u(i):
                    e.wait_ge(evac_done, st["gg"] - eo + 2 * i + 2)
                    s = 2 * i % RING
                    pr, sa = seg(upad, i, PC, PC)
                    e.tensor_tensor(pr, tmp[:, s, 0:TP], tmp[:, s + 1, 0:TP], ALU.mult)
                    e.tensor_tensor(sa, samples(tmp[:, s, :]), samples(tmp[:, s + 1, :]), ALU.mult
                                    ).then_inc(tmp_used, 2)

                make_u(0)
                make_u(1)
                e.wait_ge(rc_in, 16 * 2 * NT * (l + 1))
                e.wait_ge(pad_ready, 2 * (l + 1))
                e.wait_ge(tmp_used, tb + 4)
                conv(l, KC, 0, upad, v, "ccw", "ccb", {7 * n: (lambda i=n + 1: make_u(i)) for n in range(1, 5)})
                e.wait_ge(tmp_used, tb + 12)
                conv(l, KC, 1, upad, v, "ccw", "ccb", {4: lambda: make_u(6), 11: lambda: make_u(7)})
                e.wait_ge(evac_done, st["xr"] - eo + NT)
                for pair in range(NT // 2):
                    conv(l, KR, pair, xrp, xc, "rgw", "rgb")
                if l:
                    e.wait_ge(out_done, STORES * l)
                e.tensor_copy(rclast[:, :, 0, :], xrp[:, :, TP:TP + PR])
                e.tensor_copy(rclast[:, :, 1:, :], xrp[:, :, PR + TP:].rearrange(
                    "p i (b t) -> p i b t", b=NB)[:, :, :, TS:TS + PR]).then_inc(st_ready, 1)
                e.wait_ge(tmp_used, tb + 16)
                conv(l, KC, 2, upad, v, "ccw", "ccb")
                e.wait_ge(rg_exp, l + 1)
                link(e.tensor_tensor(flat(bb), flat(bb), flat(xc), ALU.mult))
                link(e.tensor_tensor(flat(xc), flat(ab), flat(ab), ALU.mult))
                e.scalar_tensor_tensor(out=flat(th), in0=flat(xc), scalar=1.0, in1=flat(th), op0=ALU.add,
                                       op1=ALU.mult).then_inc(rg_sq, 1)
                e.wait_ge(rg_root, l + 1)
                link(e.tensor_tensor(flat(bb), flat(bb), flat(th), ALU.mult))
                first = lambda buf: samples8(buf)[:, :, :, 0]
                h9 = hlast[:, :, 1:]
                link(e.tensor_tensor(h9, first(ab), cv("h0", l, NT * NB).rearrange("p (i b) -> p i b", b=NB),
                                     ALU.mult))
                link(e.tensor_tensor(first(bb), first(bb), h9, ALU.add))
                e.memset(first(ab), 0.0).then_inc(dve_c, 1)
                e.memset(ab[:, :, 0], 0.0).then_inc(dve_c, 1)
                links[0] += 2
                e.wait_ge(dve_c, links[0])
                link(e.tensor_tensor_scan(flat(xc), flat(ab), flat(bb), 0.0, ALU.mult, ALU.add))
                e.tensor_copy(hlast[:, :, 0], xc[:, :, TP - 1])
                e.tensor_copy(hlast[:, :, 1:], samples8(xc)[:, :, :, TS - 1]).then_inc(st_ready, 1)
                e.wait_ge(evac_done, st["yr"] - eo + NT)
                for h in range(2):
                    half = lambda buf: buf[:, 4 * h:4 * h + 4, :].rearrange("p i t -> p (i t)")
                    link(e.tensor_tensor(half(gy), half(gy), half(xc), ALU.mult))
                    link(e.tensor_copy(half(q_hi), half(gy)))
                    low(1, half(q_lo), half(q_hi), half(gy)).then_inc(q_ready, 1)
                conv(l, KC, 3, upad, v, "ccw", "ccb")
                e.wait_ge(ln_act, 10 * l + 1)
                e.tensor_tensor(v[:], v[:], bc_tiles(mean[:], T), ALU.subtract).then_inc(ln_cent, 1)
                e.wait_ge(std_ready, 3 * l + 2)
                link(e.reciprocal(rstd[:], std[:]))
                for i in range(NT):
                    e.tensor_tensor(v[:, i, :], v[:, i, :], rstd[:], ALU.mult).then_inc(ln_cent, 1)
                for i in range(NT):
                    e.wait_ge(ln_act, 10 * l + 2 + i + 1)
                    link(e.tensor_copy(q_hi[:, i, :], v[:, i, :]))
                    low(1, q_lo[:, i, :], q_hi[:, i, :], v[:, i, :]).then_inc(v_ready, 1)
                link(e.tensor_tensor(flat(gy), flat(gy), flat(sga), ALU.mult))
                for i in range(NT):
                    e.wait_ge(evac_done, st["bb"] - eo + i + 1)
                    tm = tmp[:, i % RING, :]
                    link(e.tensor_tensor(tm, tm, sgb[:, i, :], ALU.mult))
                    e.tensor_tensor(sgb[:, i, :], tm, gy[:, i, :], ALU.add).then_inc(tmp_used, 1)
                    e.wait_ge(tmp_used, tb + 16 + i + 1)
                    link(e.tensor_copy(xn_hi[:, i, :], sgb[:, i, :]))
                    low(1, xn_lo[:, i, :], xn_hi[:, i, :], sgb[:, i, :]).then_inc(m_ready, 1)
                for i in range(NT):
                    e.wait_ge(evac_done, st["wo"] - eo + i + 1)
                    residual(l, 16, i, tmp[:, i % RING, :], tmp_used)
                norm(2 * l + 1, l == 0)
                if l == 0:
                    for f in range(NF):
                        e.wait_ge(evac_done, st["gu"] + 2 * f + 2)
                        s = 2 * f % RING
                        hf = tmp[:, s, :]
                        link(e.tensor_tensor(hf, hf, tmp[:, s + 1, :], ALU.mult))
                        link(e.tensor_copy(h_hi[:, f, :], hf))
                        low(1, h_lo[:, f, :], h_hi[:, f, :], hf).then_inc(tmp_used, 2)
                    for i in range(NT):
                        e.wait_ge(evac_done, st["dn"] + i + 1)
                        residual(l, 40, i, tmp[:, i % RING, :], tmp_used)

            R = lambda off, n: route[:, off:off + n]
            S3 = lambda ap: ap.rearrange("p (t e) -> p t e", e=NE)
            bias = cv("br", None, NE).unsqueeze(1).broadcast_to([P, 3, NE])

            def mlow(b, q):
                s = q % MPER
                e.wait_ge(m_hi, b * MPER + (q + 1))
                low(1, mlo[:, s % MSPL, 0:MDVE], mhi[:, s % MSPL, 0:MDVE], mraw[:, s % MRAW, 0:MDVE]
                    ).then_inc(m_lo_dve, 1)

            for q in range(MSPL):
                mlow(0, q)
            link(e.memset(R(R_P, 24), 0.0))
            e.wait_ge(r_pe, 1)
            link(e.tensor_copy(R(R_P, 16), ps[0][:, 0:16]))
            link(e.tensor_copy(route[0:64, R_P + 16:R_P + 24], ps[0][0:64, 16:24]))
            pp = R(R_P, 24)
            link(e.tensor_tensor(S3(pp), S3(pp), bias, ALU.add))
            link(e.tensor_reduce(R(R_T, 3), S3(pp), AX.X, ALU.max))
            bc3 = lambda ap: ap.unsqueeze(2).broadcast_to([P, 3, NE])
            e.tensor_tensor(S3(pp), S3(pp), bc3(R(R_T, 3)), ALU.subtract).then_inc(r_dve, 1)
            e.wait_ge(r_act, 1)
            link(e.tensor_reduce(R(R_T, 3), S3(pp), AX.X, ALU.add))
            link(e.reciprocal(R(R_T + 4, 3), R(R_T, 3)))
            link(e.tensor_tensor(S3(pp), S3(pp), bc3(R(R_T + 4, 3)), ALU.mult))
            pj = S3(pp).unsqueeze(2).broadcast_to([P, 3, NE, NE])
            pe_ = S3(pp).unsqueeze(3).broadcast_to([P, 3, NE, NE])
            g4 = lambda ap: ap.rearrange("p (t e j) -> p t e j", e=NE, j=NE)
            link(e.tensor_tensor(g4(R(R_A, 192)), pj, pe_, ALU.is_gt))
            link(e.tensor_tensor(g4(R(R_B, 192)), pj, pe_, ALU.is_equal))
            before = ct("jlt", NE * NE)
            link(e.tensor_tensor(R(R_B, 192).rearrange("p (t m) -> p t m", t=3),
                                 R(R_B, 192).rearrange("p (t m) -> p t m", t=3),
                                 before.unsqueeze(1).broadcast_to([P, 3, NE * NE]), ALU.mult))
            link(e.tensor_tensor(R(R_A, 192), R(R_A, 192), R(R_B, 192), ALU.add))
            link(e.tensor_reduce(S3(R(R_C, 24)), g4(R(R_A, 192)), AX.X, ALU.add))
            sel = R(R_SEL, 24)
            link(e.tensor_scalar(sel, R(R_C, 24), 2.0, None, ALU.is_lt))
            link(e.memset(route[64:128, R_SEL + 16:R_SEL + 24], 0.0))
            e.tensor_tensor(R(R_W, 24), sel, pp, ALU.mult).then_inc(r_dve, 1)
            e.wait_ge(r_dve, 2)
            link(e.tensor_reduce(R(R_T, 3), S3(R(R_W, 24)), AX.X, ALU.add))
            link(e.tensor_scalar(R(R_T, 3), R(R_T, 3), 1e-30, None, ALU.max))
            link(e.reciprocal(R(R_T + 4, 3), R(R_T, 3)))
            link(e.tensor_tensor(S3(R(R_W, 24)), S3(R(R_W, 24)), bc3(R(R_T + 4, 3)), ALU.mult))
            for t, m in enumerate(TT):
                for h in range(2):
                    e.wait_ge(hn_part, 2 * t + h + 1)
                    e.tensor_tensor(rest[0:m, t, h * 512:(h + 1) * 512], ps[2 + 2 * t + h][0:m, :],
                                    hn_tok[0:m, 0, t, h * 512:(h + 1) * 512], ALU.subtract).then_inc(hn_rest, 1)
            e.wait_ge(r_pe, 3)
            link(e.tensor_copy(R(R_N, 32), ps[1][:, 0:32]))
            link(e.tensor_scalar(R(R_T, 8), R(R_N, 8), float(P), None, ALU.is_gt))
            link(e.tensor_scalar(R(R_T + 8, 8), R(R_N, 8), float(2 * P), 1.0, ALU.is_gt, ALU.add))
            link(e.tensor_tensor(R(R_T, 8), R(R_T, 8), R(R_T + 8, 8), ALU.add))
            link(e.tensor_tensor(R(R_A, 64).rearrange("p (e j) -> p e j", j=NE),
                                 R(R_T, 8).unsqueeze(1).broadcast_to([P, NE, NE]),
                                 before.rearrange("p (e j) -> p e j", j=NE), ALU.mult))
            link(e.tensor_reduce(R(R_BASE, 8), R(R_A, 64).rearrange("p (e j) -> p e j", j=NE), AX.X, ALU.add))
            link(e.tensor_reduce(R(R_T + 8, 1), R(R_T, 8), AX.X, ALU.add))
            link(e.tensor_scalar(R(R_T + 9, 1), R(R_T + 8, 1), -1.0, None, ALU.add))
            link(e.tensor_copy(nbi[:], R(R_T + 8, 2)))
            link(e.tensor_scalar(R(R_BASE, 8), R(R_BASE, 8), float(P), None, ALU.mult))
            slot = R(R_C, 24)
            link(e.tensor_tensor(S3(slot), S3(R(R_N + 8, 24)), R(R_BASE, 8).unsqueeze(1).broadcast_to([P, 3, NE]),
                                 ALU.add))
            link(e.scalar_tensor_tensor(out=slot, in0=slot, scalar=1.0, in1=sel, op0=ALU.add, op1=ALU.mult))
            link(e.tensor_scalar(slot, slot, -1.0, None, ALU.add))
            n3 = 3 * NBLK * NE
            b4 = lambda ap: ap.rearrange("p (t b e) -> p t b e", b=NBLK, e=NE)
            blk4 = ct("blk", NBLK).unsqueeze(1).unsqueeze(3).broadcast_to([P, 3, NBLK, NE])
            over_b = lambda ap: S3(ap).unsqueeze(2).broadcast_to([P, 3, NBLK, NE])
            link(e.tensor_tensor(b4(R(R_REL, n3)), over_b(slot), blk4, ALU.subtract))
            link(e.tensor_scalar(R(R_M, n3), R(R_REL, n3), 0.0, None, ALU.is_ge))
            link(e.scalar_tensor_tensor(out=R(R_M, n3), in0=R(R_REL, n3), scalar=float(P), in1=R(R_M, n3),
                                        op0=ALU.is_lt, op1=ALU.mult))
            link(e.scalar_tensor_tensor(out=R(R_REL, n3), in0=R(R_REL, n3), scalar=1.0, in1=R(R_M, n3),
                                        op0=ALU.add, op1=ALU.mult))
            link(e.tensor_reduce(colpos[:], b4(R(R_REL, n3)), AX.X, ALU.add))
            link(e.tensor_scalar(colpos[:], colpos[:], -1.0, None, ALU.add))
            link(e.tensor_tensor(b4(R(R_M, n3)), b4(R(R_M, n3)), over_b(R(R_W, 24)), ALU.mult))
            link(e.tensor_reduce(colw[:], b4(R(R_M, n3)), AX.X, ALU.add))
            be = R(R_REL, NBLK * NE).rearrange("p (b e) -> p b e", e=NE)
            link(e.tensor_tensor(be, R(R_BASE, 8).unsqueeze(1).broadcast_to([P, NBLK, NE]),
                                 ct("blk", NBLK).unsqueeze(2).broadcast_to([P, NBLK, NE]), ALU.is_le))
            link(e.tensor_reduce(R(R_T, NBLK), be, AX.X, ALU.add))
            link(e.tensor_scalar(R(R_T, NBLK), R(R_T, NBLK), -1.0, None, ALU.add))
            link(e.tensor_copy(ebi[:], R(R_T, NBLK)))

            def pick(b):
                for t, m in enumerate(TT):
                    ins = e.tensor_scalar(sm[0:m, t, :], ct("iota", P)[0:m, :],
                                          colpos[0:m, t, bass.ds(b, 1)], None, ALU.is_equal)
                ins.then_inc(s_ready, 1)

            def tokens(n):
                e.wait_ge(xg_hi_ready, n + 1)
                for h in range(2):
                    ins = low(1, xg_lo[:, 4 * h:4 * h + 4, :].rearrange("p a s -> p (a s)"),
                              xg_hi[:, 4 * h:4 * h + 4, :].rearrange("p a s -> p (a s)"), ps[6 + h][:])
                ins.then_inc(xg_ready, 1)

            pick(0)
            e.wait_ge(s_ready, 1)
            e.sem_inc(routed, 1)
            last = e.value_load(nbi[0:1, 1:2], min_val=NE - 1, max_val=NBLK - 1)
            tokens(0)
            e.wait_ge(acc_zero, 1)

            def expert(b, more):
                def add(i):
                    e.wait_ge(sc_done, b * NT + (i + 2))
                    e.tensor_tensor(acc[:, i, :], acc[:, i, :], ps[4 + i % 4][:, 0:T], ALU.add
                                    ).then_inc(acc_done, 1)

                for t, m in enumerate(TT):
                    ins = e.tensor_scalar(wc[0:m, t, :], ct("iota", P)[0:m, :], colpos[0:m, t, bass.ds(b, 1)],
                                          colw[0:m, t, bass.ds(b, 1)], ALU.is_equal, ALU.mult)
                ins.then_inc(wc_ready, 1)
                if more:
                    e.wait_ge(g_done, b + 1)
                    pick(b + 1)
                for q in range(MPER):
                    if q < 8 and q % 2 == 1:
                        i = q // 2
                        e.wait_ge(m_done, b * MPER + (q + 1))
                        e.wait_ge(gsil_ready, b * 4 + (i + 1))
                        e.tensor_tensor(hblk[:, i * GW:(i + 1) * GW], gsil[:, i % 2, :], ps[2 * (i % 2) + 1][:, 0:GW],
                                        ALU.mult).then_inc(hs_ready, 1)
                    if q == 8:
                        if more:
                            tokens(b + 1)
                        for n, (bank, w) in enumerate(((4, 512), (0, 512), (1, 384))):
                            e.wait_ge(hT_hi_ready, b * 3 + (n + 1))
                            hi = hT_hi[:, 4 * n:4 * n + w // P, :].rearrange("p a s -> p (a s)")
                            lo = hT_lo[:, 4 * n:4 * n + w // P, :].rearrange("p a s -> p (a s)")
                            ins = low(1, lo, hi, ps[bank][:, 0:w])
                        ins.then_inc(hT_ready, 1)
                    if q + MSPL < MPER or more:
                        mlow(b, q + MSPL)
                    if q >= 9:
                        add(2 * q - 18)
                        add(2 * q - 17)
                add(6)
                add(7)

            with e.Fori(0, last) as b:
                expert(b, True)
            expert(last, False)
            e.wait_ge(acc_done, last * NT + (NT + 1))
            for i in range(NT):
                e.scalar_tensor_tensor(out=x[:, i, 0:TP], in0=acc[:, i, 0:TP], scalar=mod[1][:, 40 + i, 0:1],
                                       in1=x[:, i, 0:TP], op0=ALU.mult, op1=ALU.add)
            link(e.tensor_tensor(samples8(acc), samples8(acc), bc_seq(mod[1][:, 40:48, 1:]), ALU.mult))
            e.tensor_tensor(samples8(x), samples8(x), samples8(acc), ALU.add).then_inc(x_final, 1)
            e.wait_ge(x_final, 1)
            norm(4, False)


def kernel(**a):
    import numpy as np
    import concourse.bacc as bacc
    from concourse.bass_utils import run_bass_kernel_spmd

    a = {k: np.asarray(v) for k, v in a.items()}

    def tiles(w):
        k, m = w.shape
        return w.reshape(k // P, P, m // P, P).transpose(2, 1, 0, 3).reshape(m // P, P, k)

    def slices(w, n):
        k, m = w.shape
        return w.reshape(k // P, P, m // n, n).transpose(2, 1, 0, 3).reshape(m // n, P, k // P * n)

    def columns(v):
        v = np.moveaxis(v.reshape(v.shape[:-1] + (v.shape[-1] // P, P)), -1, 0)
        return v.reshape(P, -1)

    parts = []
    for l in range(DEPTH):
        w = tiles(a["w_in"][l])
        parts.append(np.stack([w[24:32], w[16:24]], 1).reshape(16, P, D))
        parts += [w[0:16], w[32:40], tiles(a["w_branch_a"][l]), w[40:48], tiles(a["w_branch_b"][l]),
                  tiles(a["w_out"][l])]
        if l == 0:
            parts.append(np.stack([tiles(a["ffn_w_gate"][0]), tiles(a["ffn_w_up"][0])], 1).reshape(2 * NF, P, D))
            parts.append(a["ffn_w_down"][0].reshape(NF, P, D))
    stream = np.concatenate(parts)
    ada = np.concatenate([slices(a["ada_w"][l], 512) for l in range(DEPTH)]).reshape(DEPTH * NSLICE, P, NT, 512)
    moe = []
    for x in range(NE):
        g, u = slices(a["moe_w_gate"][0, x], GW), slices(a["moe_w_up"][0, x], GW)
        moe += [np.stack([g, u], 1).reshape(8, P, MCH), slices(a["moe_w_down"][0, x], DW)]
    moe = np.concatenate(moe)

    pk = []
    for l in range(DEPTH):
        for n in ("norm1_g", "norm2_g", "rg_conv_w", "rg_conv_b", "rg_ba", "rg_bx", "rg_lambda", "cc_dw_w",
                  "cc_dw_b", "cc_ln_g", "cc_ln_b", "b_branch_b", "ada_b"):
            pk.append(columns(a[n][l]))
        pk.append(a["state_rglru_h"][l].reshape(NB, NT, P).transpose(2, 1, 0).reshape(P, -1))
    pk.append(columns(a["final_norm_g"]))
    c = np.concatenate([a["c_prompt"], a["c_sample"]])
    pk.append(c.reshape(NSEQ, NT, P).transpose(2, 1, 0).reshape(P, -1))
    pk.append(a["moe_router_w"][0].reshape(NT, P, NE).transpose(1, 0, 2).reshape(P, -1))
    pk.append(np.broadcast_to(a["moe_router_b"], (P, NE)))
    cols = np.concatenate(pk, 1)

    f = np.arange(P)
    sel = np.zeros((P, NSEQ), np.float32)
    for q in range(4):
        sel[32 * q:32 * q + NSEQ] = np.eye(NSEQ, dtype=np.float32)
    e8 = np.arange(NE)
    rep = lambda r: np.broadcast_to(np.asarray(r, np.float32).reshape(1, -1), (P, np.size(r)))
    cst = np.concatenate([np.eye(P, dtype=np.float32), (f[:, None] < f[None, :]).astype(np.float32), rep(f), sel,
                          rep(e8[None, :] < e8[:, None]), rep(e8), rep(P * np.arange(NBLK))], 1)

    wrg = np.zeros((DEPTH, P, 2, NT, P), np.float32)
    for w, n in enumerate(("rg_wa", "rg_wx")):
        b = a[n].reshape(DEPTH, NT, 2, 64, 64)
        for h in range(2):
            wrg[:, 64 * h:64 * h + 64, w, :, 64 * h:64 * h + 64] = b[:, :, h].transpose(0, 2, 1, 3)
    x = np.concatenate([a["x_prompt"].reshape(TP, D), a["x_sample"].reshape(NB * TS, D)])
    x = x.T.reshape(NT, P, T).transpose(1, 0, 2)
    rc = a["state_rglru_conv"].reshape(DEPTH, NB, PR, NT, P).transpose(0, 4, 3, 1, 2).reshape(DEPTH, P, NT, NB, PR)
    cc = a["state_cconv"].reshape(DEPTH, NB, PC, NT, P).transpose(0, 4, 3, 1, 2).reshape(DEPTH, P, NT, NB, PC)
    arrays = {k: np.ascontiguousarray(v) for k, v in dict(
        stream=stream, ada=ada, moe=moe, cols=cols, cst=cst, wrg=wrg, x=x, rc=rc, cc=cc).items()}

    nc = bacc.Bacc("TRN2", target_bir_lowering=False, num_devices=1)
    ins = [nc.dram_tensor("in_" + k, v.shape, F32, kind="ExternalInput").ap() for k, v in arrays.items()]
    shapes = dict(y=(P, NT, T), h=(DEPTH, P, NT, NSEQ), rc=(DEPTH, P, NT, NSEQ, PR), cc=(DEPTH, P, NT, NSEQ, PC))
    outs = [nc.dram_tensor("out_" + k, s, F32, kind="ExternalOutput").ap() for k, s in shapes.items()]
    build(nc, *ins, *outs)
    r = run_bass_kernel_spmd(nc, [{"in_" + k: v for k, v in arrays.items()}], core_ids=[0]).results[0]
    y = r["out_y"].transpose(2, 1, 0).reshape(T, D)
    h = r["out_h"].transpose(0, 3, 2, 1).reshape(DEPTH, NSEQ, D)
    rco = r["out_rc"].transpose(0, 3, 4, 2, 1).reshape(DEPTH, NSEQ, PR, D)
    cco = r["out_cc"].transpose(0, 3, 4, 2, 1).reshape(DEPTH, NSEQ, PC, D)
    return (y[:TP].reshape(1, TP, D), y[TP:].reshape(NB, TS, D), h[:, :1], rco[:, :1], cco[:, :1], h[:, 1:],
            rco[:, 1:], cco[:, 1:])
```

```python
from contextlib import ExitStack

import concourse.bass as bass
from concourse import mybir

F32 = mybir.dt.float32
F32R = mybir.dt.float32r
BF16 = mybir.dt.bfloat16
I32 = mybir.dt.int32
ALU = mybir.AluOpType
ACT = mybir.ActivationFunctionType
AX = mybir.AxisListType

P = 128
DEPTH = 2
D = 1024
NT = D // P
TP = 256
NB, TS = 8, 8
T = TP + NB * TS
NSEQ = 1 + NB
KR, KC = 4, 31
PR, PC = KR - 1, KC - 1
XR_W = PR + TP + NB * (PR + TS)
U_W = PC + TP + NB * (PC + TS)
NF = 2816 // P
NE = 8
FE = 1408
NFE = FE // P
EPS = 1e-6

CH = 8 * P
RING = 4
PER_LAYER = 48 + 8 + 8 + 8
DENSE = 3 * NF
C_LAYER = (0, PER_LAYER + DENSE)
NCHUNK = 2 * PER_LAYER + DENSE
NSLICE = 12

MCH = 8 * 352
MRAW, MSPL = 4, 3
MPER = 12
GW, DW = FE // 4, D // 4
NBLK = 12
NV = 4
MDVE = 5 * MCH // 8
TT = (128, 128, 64)

_COL = {}
_n = 0
for _l in range(DEPTH):
    for _name, _w in (("n1g", NT), ("n2g", NT), ("rgw", KR * NT), ("rgb", NT), ("ba", NT), ("bx", NT),
                      ("lam", NT), ("ccw", KC * NT), ("ccb", NT), ("lng", NT), ("lnb", NT), ("bbb", NT),
                      ("adab", 48), ("h0", NT * NB)):
        _COL[_name, _l] = _n
        _n += _w
for _name, _w in (("fg", NT), ("c", NT * NSEQ), ("wr", NT * NE), ("br", NE)):
    _COL[_name] = _n
    _n += _w
NCOL = _n
_CST = {}
_n = 0
for _name, _w in (("ident", P), ("tri", P), ("iota", P), ("sel", NSEQ), ("jlt", NE * NE), ("eidx", NE),
                  ("blk", NBLK)):
    _CST[_name] = _n
    _n += _w
NCST = _n


def build(nc, stream, ada, moe, cols_d, cst_d, wrg_d, x_d, rc_d, cc_d, y_o, h_o, rc_o, cc_o):
    with ExitStack() as ctx:
        def sem(name):
            return ctx.enter_context(nc.semaphore(name))

        at = [16512]

        def place(name, shape, dt, offset=None):
            size = 2 if dt == BF16 else 4
            for n in shape[1:]:
                size *= n
            if offset is None:
                offset = at[0]
                at[0] += (size + 31) // 32 * 32
            return nc.alloc_sbuf_tensor_at(name, shape, dt, offset=offset)

        x = place("x", [P, NT, T], F32)
        cols = place("cols", [P, NCOL], F32)
        cst = place("cst", [P, NCST], F32)
        ones = place("ones", [P, P], F32)
        eps = place("eps", [P, 1], F32)
        sp8 = place("sp8", [P, DEPTH, NT], F32)
        csil = place("csil", [P, NT, 32], F32)
        small = place("small", [P, 8, DEPTH, NT], F32)
        mod = [place(f"mod{l}", [P, 48, NSEQ], F32) for l in range(DEPTH)]
        modrow = place("modrow", [P, 512], F32)
        std = place("std", [P, T], F32)
        o_rstd = at[0]
        rstd = place("rstd", [P, T], F32)
        assert (NT - NV) * NB * TS <= T
        prod = place("prod", [P, (NT - NV) * NB * TS], F32, o_rstd)
        mean = place("mean", [P, T], F32)
        hlast = place("hlast", [P, NT, NSEQ], F32)
        rclast = place("rclast", [P, NT, NSEQ, PR], F32)
        nbi = place("nbi", [P, 2], I32)
        ebi = place("ebi", [P, NBLK], I32)
        o_xn = at[0]
        xn_hi = place("xn_hi", [P, NT, T], F32R)
        xn_lo = place("xn_lo", [P, NT, T], F32R)
        o_tmp = at[0]
        tmp = place("tmp", [P, RING, T], F32)
        wrg = place("wrg", [P, 2, NT, P], F32)
        o_ring = at[0]
        raw = place("raw", [P, RING, CH], F32)
        whi = place("whi", [P, RING, CH], F32R)
        wlo = place("wlo", [P, RING, CH], F32R)
        o_arena = at[0]
        gy = place("gy", [P, NT, T], F32)
        sga = place("sga", [P, NT, T], F32)
        upad = place("upad", [P, NT, U_W], F32)
        o_xr = at[0]
        xrp = place("xrp", [P, NT, XR_W], F32)
        th = place("th", [P, NT, T], F32, o_xr)
        o_xc = at[0]
        xc = place("xc", [P, NT, T], F32)
        sgb = place("sgb", [P, NT, T], F32, o_xc)
        o_a = at[0]
        ab = place("ab", [P, NT, T], F32)
        q_hi = place("q_hi", [P, NT, T], F32R, o_a)
        o_b = at[0]
        bb = place("bb", [P, NT, T], F32)
        q_lo = place("q_lo", [P, NT, T], F32R, o_b)
        o_v = at[0]
        v = place("v", [P, NT, T], F32)
        assert o_v + 18432 <= 229344, o_v
        h_hi = place("h_hi", [P, NF, T], F32R, o_arena)
        h_lo = place("h_lo", [P, NF, T], F32R, o_arena + NF * T * 4)
        assert o_arena + 2 * NF * T * 4 <= o_a
        NA = 4
        assert NA * 512 == 2 * D and o_arena + 49152 <= o_a
        adas = [[place(f"ada0_{i}", [P, NT, 512], F32, o) for i, o in enumerate(
                    (o_arena, o_arena + 16384, o_arena + 32768, o_v, o_a))],
                [place("ada1_0", [P, NT, 512], F32, o_v), place("ada1_1", [P, NT, 512], F32, o_a)]]
        mraw = place("mraw", [P, MRAW, MCH], F32, o_ring)
        assert MRAW * MCH * 4 <= o_arena - o_ring
        mhi = place("mhi", [P, MSPL, MCH], F32R, o_arena)
        mlo = place("mlo", [P, MSPL, MCH], F32R, o_arena + MSPL * MCH * 4)
        assert o_arena + 2 * MSPL * MCH * 4 <= o_b
        hn_tok = place("hn_tok", [P, 3, 3, D], BF16, o_v)
        acc = place("acc", [P, NT, T], F32, o_xn)
        route = place("route", [P, 2560], F32, o_xn)
        xg_hi = place("xg_hi", [P, NT, P], F32R, o_xn + 10240)
        xg_lo = place("xg_lo", [P, NT, P], F32R, o_xn + 10240 + 4096)
        hT_hi = place("hT_hi", [P, NFE, P], F32R, o_tmp)
        hT_lo = place("hT_lo", [P, NFE, P], F32R, o_tmp + 5632)
        o_h = o_arena + 2 * MSPL * MCH * 4
        hblk = place("hblk", [P, FE], F32, o_h)
        gsil = place("gsil", [P, 2, GW], F32, o_h + 5632)
        y_hi = place("y_hi", [P, D], F32R, o_h + 5632 + 2816)
        y_lo = place("y_lo", [P, D], F32R, o_h)
        rest = place("rest", [P, 3, D], F32, o_h)
        assert o_h + 5632 + 2816 + 4096 <= o_v and o_h > o_a
        o_s = o_ring + MRAW * MCH * 4
        sm = place("sm", [P, 3, P], BF16, o_s)
        wc = place("wc", [P, 3, P], F32, o_s + 1536)
        turned = place("turned", [P, T], F32R, o_xn + 10240 + 8192)
        colpos = place("colpos", [P, 3, NBLK], F32, o_s + 3072)
        colw = place("colw", [P, 3, NBLK], F32, o_s + 3072 + 160)
        wslot = place("wslot", [P, 1], F32, o_s + 3072 + 320)
        assert o_s + 3072 + 352 <= o_arena

        ps = [ctx.enter_context(nc.psum_tensor(f"ps{i}", [P, 512], F32)) for i in range(8)]

        def col(name, l, i):
            n = _COL[name, l] if l is not None else _COL[name]
            return cols[:, bass.ds(n + i, 1)]

        def cv(name, l, w):
            n = _COL[name, l] if l is not None else _COL[name]
            return cols[:, n:n + w]

        def ct(name, w):
            return cst[:, _CST[name]:_CST[name] + w]

        ident = ct("ident", P)

        x_in = sem("x_in")
        wrg_in = sem("wrg_in")
        rc_in = sem("rc_in")
        raw_landed = [sem(f"raw_landed{i}") for i in range(RING)]
        hi_ready = sem("hi_ready")
        lo_ready = sem("lo_ready")
        chunk_done = sem("chunk_done")
        down_done = sem("down_done")
        evac_done = sem("evac_done")
        tmp_used = sem("tmp_used")
        ada_landed = [sem(f"ada_landed{i}") for i in range(5)]
        ada_rows = sem("ada_rows")
        row_copied = sem("row_copied")
        ada_turned = sem("ada_turned")
        mod_copied = sem("mod_copied")
        mod_ready = sem("mod_ready")
        csil_ready = sem("csil_ready")
        pad_ready = sem("pad_ready")
        const_ready = sem("const_ready")
        sq_ready = sem("sq_ready")
        stat_done = sem("stat_done")
        std_ready = sem("std_ready")
        xs_ready = sem("xs_ready")
        hn_ready = sem("hn_ready")
        norm_ready = sem("norm_ready")
        rg_done = sem("rg_done")
        rg_sig = sem("rg_sig")
        rg_exp = sem("rg_exp")
        rg_sq = sem("rg_sq")
        rg_root = sem("rg_root")
        q_ready = sem("q_ready")
        conv_step = sem("conv_step")
        pool_step = sem("pool_step")
        ln_cent = sem("ln_cent")
        ln_act = sem("ln_act")
        v_ready = sem("v_ready")
        m_ready = sem("m_ready")
        dve_c = sem("dve_c")
        act_c = sem("act_c")
        out_done = sem("out_done")
        st_ready = sem("st_ready")
        m_landed = [sem(f"m_landed{i}") for i in range(MRAW)]
        m_hi = sem("m_hi")
        m_lo_dve = sem("m_lo_dve")
        m_lo_pool = sem("m_lo_pool")
        hn_part = sem("hn_part")
        hn_rest = sem("hn_rest")
        hn_last = sem("hn_last")
        acc_zero = sem("acc_zero")
        m_done = sem("m_done")
        r_pe = sem("r_pe")
        r_dve = sem("r_dve")
        routed = sem("routed")
        s_ready = sem("s_ready")
        g_done = sem("g_done")
        wc_ready = sem("wc_ready")
        wt_done = sem("wt_done")
        wct_ready = sem("wct_ready")
        xg_hi_ready = sem("xg_hi_ready")
        xg_ready = sem("xg_ready")
        gsil_ready = sem("gsil_ready")
        hs_ready = sem("hs_ready")
        ht_done = sem("ht_done")
        hT_hi_ready = sem("hT_hi_ready")
        hT_ready = sem("hT_ready")
        y_hi_ready = sem("y_hi_ready")
        y_ready = sem("y_ready")
        sc_done = sem("sc_done")
        acc_done = sem("acc_done")
        x_final = sem("x_final")
        y_out = sem("y_out")
        r_act = sem("r_act")

        def seg(buf, i, hist, off):
            w = hist + TS
            p0 = hist + TP
            prompt = buf[:, i, off:off + TP]
            s = buf[:, i, p0:p0 + NB * w].rearrange("p (b t) -> p b t", b=NB)[:, :, off:off + TS]
            return prompt, s

        def samples(ap):
            return ap[:, TP:T].rearrange("p (b t) -> p b t", b=NB)

        def samples8(buf):
            return buf[:, :, TP:T].rearrange("p i (b t) -> p i b t", b=NB)

        def bc_t(ap):
            return ap.unsqueeze(2).broadcast_to([P, NB, TS])

        def stages(l):
            c = C_LAYER[l]
            return dict(gg=c, xr=c + 16, yr=c + 24, ga=c + 32, ba=c + 40, gb=c + 48, bb=c + 56, wo=c + 64,
                        gu=c + 72, dn=c + 72 + 2 * NF)

        E_OFF = (0, NF - NT)
        T_BASE = (0, 16 + 8 + 8 + 2 * NF + NT)
        T_GU = 32
        K_SHORT = 20
        CONVS = 2 * NT * KR + (NT + NV) * KC
        STORES = 16 * (3 + NT)
        R_SEL, R_P, R_T, R_W, R_C, R_N, R_BASE = 0, 24, 48, 64, 88, 112, 144
        R_A, R_B = 160, 352
        R_REL, R_M = 560, 560 + 3 * NBLK * NE

        block = ctx.enter_context(nc.Block())

        @block.sync
        def _(e):
            e.dma_start(cols[:], cols_d).then_inc(x_in, 16)
            e.dma_start(cst[:], cst_d).then_inc(x_in, 16)
            e.dma_start(x[:], x_d).then_inc(x_in, 16)
            for s in range(NA):
                e.dma_start(adas[0][s][:], ada[s]).then_inc(ada_landed[s], 16)

            def chunk(c_static, c):
                s = c_static % RING
                e.dma_start(raw[:, s, :], stream[c]).then_inc(raw_landed[s], 16)

            for c in range(RING):
                chunk(c, c)
            e.dma_start(wrg[:], wrg_d[0]).then_inc(wrg_in, 16)

            def run(c0, n):
                k, r = n // 4, n % 4
                if k:
                    with e.Fori(0, k) as g:
                        for j in range(4):
                            e.wait_ge(lo_ready, g * 4 + (c0 + j - RING + 1))
                            chunk(c0 + j, g * 4 + (c0 + j))
                for j in range(4 * k, n):
                    e.wait_ge(lo_ready, c0 + j - RING + 1)
                    chunk(c0 + j, c0 + j)

            def states(l):
                for i in range(NT):
                    for buf, h, src in ((xrp, PR, rc_d), (upad, PC, cc_d)):
                        e.dma_start(buf[:, i, h + TP:].rearrange("p (b t) -> p b t", b=NB)[:, :, 0:h],
                                    src[l, :, i]).then_inc(rc_in, 16)

            st0, st1 = stages(0), stages(1)
            e.wait_ge(ada_rows, NA)
            e.dma_start(adas[0][NA - 1][:], ada[NA]).then_inc(ada_landed[NA - 1], 16)
            run(RING, 2)
            states(0)
            run(RING + 2, 2)
            e.wait_ge(norm_ready, NT)
            e.dma_start(adas[0][NA][:], ada[NA + 1]).then_inc(ada_landed[NA], 16)
            with e.Fori(0, NSLICE - NA - 2) as g:
                e.wait_ge(ada_rows, g + (NA + 2))
                e.dma_start(adas[0][NA][:], ada[g + (NA + 2)]).then_inc(ada_landed[NA], 16)
                for j in range(4):
                    e.wait_ge(lo_ready, g * 4 + (8 + j - RING + 1))
                    chunk(j, g * 4 + (8 + j))
            c_next = 8 + 4 * (NSLICE - NA - 2)
            run(c_next, st0["bb"] - c_next)

            def store_states(l):
                e.wait_ge(st_ready, 2 * l + 1)
                e.dma_start(rc_o[l], rclast[:]).then_inc(out_done, 16)
                e.wait_ge(st_ready, 2 * l + 2)
                e.dma_start(h_o[l], hlast[:]).then_inc(out_done, 16)
                e.wait_ge(tmp_used, T_BASE[l] + 16)
                e.dma_start(cc_o[l, :, :, 0, :], upad[:, :, TP:TP + PC]).then_inc(out_done, 16)
                for i in range(NT):
                    e.dma_start(cc_o[l, :, i, 1:NSEQ, :], upad[:, i, PC + TP:].rearrange(
                        "p (b t) -> p b t", b=NB)[:, :, TS:TS + PC]).then_inc(out_done, 16)

            store_states(0)
            run(st0["bb"], 8 + 4)
            e.wait_ge(out_done, STORES)
            e.wait_ge(m_ready, NT)
            e.dma_start(adas[1][0][:], ada[NSLICE]).then_inc(ada_landed[0], 16)
            e.wait_ge(rg_done, 2 * NT)
            e.dma_start(wrg[:], wrg_d[1]).then_inc(wrg_in, 16)
            run(st0["wo"] + 4, 4 + 4)
            e.wait_ge(norm_ready, 2 * NT)
            e.dma_start(adas[1][1][:], ada[NSLICE + 1]).then_inc(ada_landed[1], 16)
            with e.Fori(0, 5) as g:
                for h in range(2):
                    for j in range(4):
                        c = st0["gu"] + 4 + 4 * h + j
                        e.wait_ge(lo_ready, g * 8 + (c - RING + 1))
                        chunk(c, g * 8 + c)
                    e.wait_ge(ada_rows, g * 2 + (NSLICE + h + 1))
                    e.dma_start(adas[1][h][:], ada[g * 2 + (NSLICE + h + 2)]).then_inc(ada_landed[h], 16)
            run(st0["dn"], NF)
            run(st1["gg"], 4)
            e.wait_ge(chunk_done, st1["gg"])
            states(1)
            run(st1["gg"] + 4, 72 - 4 - 16)
            store_states(1)
            run(st1["bb"], 16)
            e.wait_ge(chunk_done, NCHUNK)
            for k in range(MRAW):
                e.dma_start(mraw[:, k, :], moe[k]).then_inc(m_landed[k], 16)

            def freed(n):
                e.wait_ge(m_lo_dve, n + 1)
                e.wait_ge(m_lo_pool, n + 1)

            for k in range(MRAW, MPER):
                freed(k - MRAW)
                e.dma_start(mraw[:, k % MRAW, :], moe[k]).then_inc(m_landed[k % MRAW], 16)
            e.wait_ge(routed, 1)
            nblk = e.value_load(nbi[0:1, 0:1], min_val=NE, max_val=NBLK)
            with e.Fori(1, nblk) as b:
                ex = e.value_load(ebi[0:1, bass.ds(b, 1)], min_val=0, max_val=NE - 1)
                for k in range(MPER):
                    freed(b * MPER + (k - MRAW))
                    e.dma_start(mraw[:, k % MRAW, :], moe[ex * MPER + k]).then_inc(m_landed[k % MRAW], 16)
            for i in range(NT):
                e.wait_ge(y_out, i + 1)
                e.dma_start(y_o[:, i, :], bb[:, i, :]).then_inc(out_done, 16)
            e.wait_ge(out_done, DEPTH * STORES + 16 * NT)


        @block.gpsimd
        def _(e):
            e.memset(ones[:], 1.0).then_inc(const_ready, 1)
            e.memset(eps[:], EPS).then_inc(const_ready, 1)
            e.memset(csil[:], 0.0).then_inc(const_ready, 1)

            def low(c_static, c):
                s = c_static % RING
                e.wait_ge(hi_ready, c + 1)
                e.tensor_tensor(wlo[:, s, :], raw[:, s, :], whi[:, s, :].bitcast(F32), ALU.subtract
                                ).then_inc(lo_ready, 1)

            def run(c0, n):
                k = n // 4
                with e.Fori(0, k) as g:
                    for j in range(4):
                        low(c0 + j, g * 4 + (c0 + j))
                for c in range(c0 + 4 * k, c0 + n):
                    low(c, c)

            def pads():
                e.memset(upad[:, :, 0:PC], 0.0).then_inc(pad_ready, 1)
                e.memset(xrp[:, :, 0:PR], 0.0).then_inc(pad_ready, 1)

            for c in range(4):
                low(c, c)
            e.wait_ge(ada_rows, NA)
            pads()
            def conv_tap(l, k):
                rows_of = lambda buf, h, o: buf[:, NV:, h + TP:].rearrange("p i (b t) -> p i b t", b=NB)[:, :, :, o:o + TS]
                src, out = rows_of(upad, PC, k), rows_of(v, 0, 0)
                vec = lambda name, k: cv(name, l, (k + 1) * NT)[:, k * NT + NV:(k + 1) * NT].unsqueeze(2).unsqueeze(
                    3).broadcast_to([P, NT - NV, NB, TS])
                n = pool_n[0]
                if k == 0:
                    e.tensor_tensor(out, src, vec("ccw", 0), ALU.mult).then_inc(pool_step, 1)
                    e.wait_ge(pool_step, n + 1)
                    e.tensor_tensor(out, out, vec("ccb", 0), ALU.add).then_inc(pool_step, 1)
                else:
                    e.wait_ge(pool_step, n)
                    prod4 = prod[:].rearrange("p (i b t) -> p i b t", b=NB, t=TS)
                    e.tensor_tensor(prod4, src, vec("ccw", k), ALU.mult).then_inc(pool_step, 1)
                    e.wait_ge(pool_step, n + 1)
                    e.tensor_tensor(out, out, prod4, ALU.add).then_inc(pool_step, 1)
                pool_n[0] += 2

            pool_n = [0]

            MIX = 20 + KC - 8

            def mixer(l):
                st = stages(l)
                run(st["gg"] + 4, 16)
                e.wait_ge(rc_in, 16 * 2 * NT * (l + 1))
                e.wait_ge(pad_ready, 2 * (l + 1))
                e.wait_ge(tmp_used, T_BASE[l] + 16)
                k = 0
                for c in range(st["gg"] + 20, st["gg"] + MIX):
                    for _ in range(1 if c != st["yr"] + 8 else 9):
                        conv_tap(l, k)
                        k += 1
                    low(c, c)
                assert k == KC

            mixer(0)
            g1 = stages(1)["gg"]
            run(MIX, g1 + 4 - MIX)
            e.wait_ge(chunk_done, g1)
            pads()
            mixer(1)
            run(g1 + MIX, NCHUNK - g1 - MIX)

            def mlow(b, q):
                s = q % MPER
                e.wait_ge(m_hi, b * MPER + (q + 1))
                e.tensor_tensor(mlo[:, s % MSPL, MDVE:], mraw[:, s % MRAW, MDVE:],
                                mhi[:, s % MSPL, MDVE:].bitcast(F32), ALU.subtract).then_inc(m_lo_pool, 1)

            for q in range(MSPL):
                mlow(0, q)
            for t, m in enumerate(TT):
                e.wait_ge(hn_part, 6 + t + 1)
                e.tensor_tensor(hn_tok[0:m, 2, t, :], rest[0:m, t, :], hn_tok[0:m, 1, t, :], ALU.subtract
                                ).then_inc(hn_last, 1)
            e.wait_ge(routed, 1)
            e.memset(acc[:], 0.0).then_inc(acc_zero, 1)
            last = e.value_load(nbi[0:1, 1:2], min_val=NE - 1, max_val=NBLK - 1)
            with e.Fori(0, last) as b:
                for q in range(MPER):
                    mlow(b, q + MSPL)
            for q in range(MPER - MSPL):
                mlow(last, q + MSPL)

        @block.tensor
        def _(e):
            def split_mm(out, w, x2, start, stop):
                e.matmul(out, w[0], x2[0], start=start, stop=False)
                e.matmul(out, w[0], x2[1], start=False, stop=False)
                return e.matmul(out, w[1], x2[0], start=False, stop=stop)

            def wtile(s, u):
                return whi[:, s, u * P:(u + 1) * P], wlo[:, s, u * P:(u + 1) * P]

            def main(l, c0, n, xs, ready=None, slices=None):
                def one(c_static, c, ready=None):
                    s = c_static % RING
                    e.wait_ge(lo_ready, c + 1)
                    if c_static - E_OFF[l] >= RING:
                        e.wait_ge(evac_done, c - (E_OFF[l] + 3))
                    for k in range(NT):
                        if ready is not None:
                            e.wait_ge(*ready(k))
                        mm = split_mm(ps[s][:, 0:T], wtile(s, k), (xs[0][:, k, :], xs[1][:, k, :]),
                                      k == 0, k == NT - 1)
                    mm.then_inc(chunk_done, 1)

                if ready is not None or n < 4:
                    for c in range(c0, c0 + min(n, 4)):
                        one(c, c, ready if c == c0 else None)
                    c0, n = c0 + 4, n - 4
                if n > 0:
                    with e.Fori(0, n // 4) as g:
                        for j in range(4):
                            one(c0 + j, g * 4 + (c0 + j))
                            if slices is not None and j == 1:
                                turn(g + slices)
                        if slices is not None:
                            rows(NA, g + (slices + 1), g * 16 + 16 * (slices - NA + 1), adas[0][NA])

            def rows(slot, s, n_landed, mk):
                e.wait_ge(ada_landed[slot], n_landed)
                e.wait_ge(row_copied, s + 1)
                for k in range(NT):
                    q = 32 * (k % 4)
                    mm = e.matmul(ps[5][q:q + 32, :], csil[:, k, :], mk[:, k, :], start=k < 4, stop=k >= 4)
                mm.then_inc(ada_rows, 1)

            def turn(s):
                e.wait_ge(row_copied, s + 2)
                e.wait_ge(mod_copied, s + 1)
                for j in range(4):
                    mm = e.matmul(ps[6][:, NSEQ * j:NSEQ * (j + 1)], modrow[:, j * P:(j + 1) * P],
                                  ct("sel", NSEQ), start=True, stop=True)
                mm.then_inc(ada_turned, 1)

            def stat(buf, waits):
                for i in range(NT):
                    if i in waits:
                        e.wait_ge(*waits[i])
                    mm = e.matmul(ps[4][:, 0:T], ones[:], buf[:, i, :], start=i == 0, stop=i == NT - 1)
                mm.then_inc(stat_done, 1)

            def norm(n):
                stat(ab, {i: (sq_ready, NT * n + i + 1) for i in range(NT)})

            e.sem_inc(ada_turned, 1)
            e.sem_inc(sc_done, 1)
            e.wait_ge(x_in, 48)
            e.wait_ge(csil_ready, 1)
            norm(0)
            for slot in range(NA):
                rows(slot, slot, 16, adas[0][slot])
                turn(slot)

            for l in range(DEPTH):
                st = stages(l)
                if l:
                    e.wait_ge(evac_done, C_LAYER[1] - NF + 5)
                    norm(2 * l)
                xs = (xn_hi, xn_lo)
                first = lambda k: (norm_ready, NT * 2 * l + k + 1)
                if l == 0:
                    main(l, st["gg"], 2, xs, first)
                    rows(NA - 1, NA, 32, adas[0][NA - 1])
                    main(l, st["gg"] + 2, 1, xs)
                    turn(NA)
                    main(l, st["gg"] + 3, 1, xs)
                    rows(NA, NA + 1, 16, adas[0][NA])
                    main(l, st["gg"] + 4, 24, xs, None, NA + 1)
                    e.wait_ge(row_copied, NSLICE + 1)
                    e.wait_ge(mod_copied, NSLICE)
                else:
                    main(l, st["gg"], 4, xs, first)
                    main(l, st["gg"] + 4, 24, xs)
                e.wait_ge(wrg_in, 16 * (l + 1))
                for i in range(NT):
                    if i % 2 == 0:
                        e.wait_ge(conv_step, CONVS * l + 2 * 2 * (KC + K_SHORT) + 2 * 2 * KR * (i // 2 + 1))
                    for w in range(2):
                        n = 2 * i + w
                        if n >= 4:
                            e.wait_ge(rg_sig, 2 * NT * l + n - 3)
                        e.matmul(ps[4 + n % 4][:, 0:T], wrg[:, w, i, :], xc[:, i, :], start=True, stop=True
                                 ).then_inc(rg_done, 1)
                if l == 0:
                    e.wait_ge(rg_sig, 2 * NT)
                    main(l, st["yr"] + 4, 2, xs)
                    turn(NSLICE - 1)
                    main(l, st["yr"] + 6, 2, xs)
                else:
                    main(l, st["yr"] + 4, 4, xs)
                main(l, st["ga"], 8, xs)
                main(l, st["ba"], 8, (q_hi, q_lo), lambda k: (q_ready, 2 * l + k // 4 + 1))
                main(l, st["gb"], 2, xs)
                e.wait_ge(conv_step, CONVS * (l + 1))
                e.wait_ge(pool_step, 2 * KC * (l + 1))
                stat(v, {})
                main(l, st["gb"] + 2, 3, xs)
                stat(th, {0: (ln_act, 10 * l + 2)})
                main(l, st["gb"] + 5, 3, xs)
                main(l, st["bb"], 8, (q_hi, q_lo), lambda k: (v_ready, NT * l + k + 1))
                main(l, st["wo"], 8, xs, lambda k: (m_ready, NT * l + k + 1))
                norm(2 * l + 1)
                if l == 0:
                    rows(0, NSLICE, 16 * 2, adas[1][0])

                    def four(g8, h, first, n_slice):
                        for j in range(4):
                            cs = st["gu"] + 4 * h + j
                            c = g8 + cs
                            s = cs % RING
                            e.wait_ge(lo_ready, c + 1)
                            e.wait_ge(evac_done, c - 3)
                            for k in range(NT):
                                if first and j == 0:
                                    e.wait_ge(norm_ready, NT + k + 1)
                                mm = split_mm(ps[s][:, 0:T], wtile(s, k), (xn_hi[:, k, :], xn_lo[:, k, :]),
                                              k == 0, k == NT - 1)
                            mm.then_inc(chunk_done, 1)
                            if j == 1:
                                turn(n_slice)

                    four(0, 0, True, NSLICE)
                    rows(1, NSLICE + 1, 16 * 2, adas[1][1])
                    with e.Fori(0, 5) as g:
                        for h in range(2):
                            four(g * 8 + 4, h, False, g * 2 + (NSLICE + 1 + h))
                            rows(h, g * 2 + (NSLICE + 2 + h), g * 16 + 16 * 3, adas[1][h])
                    turn(2 * NSLICE - 1)
                    e.wait_ge(evac_done, st["dn"])
                    e.wait_ge(mod_copied, 2 * NSLICE + 1)

                    def down(cs, k, start, stop):
                        s = cs % RING
                        e.wait_ge(lo_ready, k + (st["dn"] + 1))
                        e.wait_ge(tmp_used, k * 2 + (T_GU + 2))
                        for m in range(NT):
                            mm = split_mm(ps[m][:, 0:T], wtile(s, m),
                                          (h_hi[:, bass.ds(k, 1), :].rearrange("p a t -> p (a t)"),
                                           h_lo[:, bass.ds(k, 1), :].rearrange("p a t -> p (a t)")), start, stop)
                        mm.then_inc(chunk_done, 1)

                    for k in range(4):
                        down(st["dn"] + k, k, k == 0, False)
                    with e.Fori(0, 3) as g:
                        for j in range(4):
                            down(st["dn"] + 4 + j, g * 4 + (4 + j), False, False)
                    down(st["dn"] + 16, 16, False, False)
                    down(st["dn"] + 17, 17, False, False)
                    for m in range(NT):
                        for k in range(NF - 4, NF):
                            s = (st["dn"] + k) % RING
                            if m == 0:
                                e.wait_ge(lo_ready, st["dn"] + k + 1)
                                e.wait_ge(tmp_used, T_GU + 2 * k + 2)
                            mm = split_mm(ps[m][:, 0:T], wtile(s, m), (h_hi[:, k, :], h_lo[:, k, :]), False, k == NF - 1)
                            if m == NT - 1:
                                mm.then_inc(chunk_done, 1)
                            elif k == NF - 1:
                                mm.then_inc(down_done, 1)

            e.wait_ge(hn_ready, 4 * NT)
            e.wait_ge(norm_ready, 3 * NT + 1)
            for t, m in enumerate(TT):
                for k in range(NT):
                    n = _COL["wr"] + k * NE
                    mm = e.matmul(ps[0][0:m, t * NE:(t + 1) * NE], bb[:, k, t * P:t * P + m],
                                  cols[:, n:n + NE], start=k == 0, stop=k == NT - 1)
            mm.then_inc(r_pe, 1)
            for t, m in enumerate(TT):
                for i in range(NT):
                    mm = e.transpose(ps[2 + 2 * t + i // 4][0:m, (i % 4) * P:(i % 4 + 1) * P],
                                     bb[:, i, t * P:t * P + m], ident)
            mm.then_inc(r_pe, 1)
            e.wait_ge(r_dve, 2)
            sel = route[:, R_SEL:R_SEL + 24]
            for t in range(4):
                for u in range(3 if t == 0 else t):
                    w = ones[:] if t == 0 or u < t - 1 else ct("tri", P)
                    mm = e.matmul(ps[1][:, t * NE:(t + 1) * NE], w, sel[:, u * NE:(u + 1) * NE], start=u == 0,
                                  stop=u == (2 if t == 0 else t - 1))
            mm.then_inc(r_pe, 1)

            def gather(b):
                e.wait_ge(s_ready, b + 1)
                for i in range(NT):
                    for t, m in enumerate(TT):
                        for part in range(3):
                            mm = e.matmul(ps[6 + i // 4][:, (i % 4) * P:(i % 4 + 1) * P],
                                          hn_tok[0:m, part, t, i * P:(i + 1) * P], sm[0:m, t, :],
                                          start=t + part == 0, stop=t + part == 4)
                mm.then_inc(g_done, 1)

            e.wait_ge(routed, 1)
            last = e.value_load(nbi[0:1, 1:2], min_val=NE - 1, max_val=NBLK - 1)
            e.wait_ge(hn_part, 9)
            e.wait_ge(hn_last, 3)
            gather(0)

            def expert(b, more):
                def split_ready(q):
                    e.wait_ge(m_lo_dve, b * MPER + (q + 1))
                    e.wait_ge(m_lo_pool, b * MPER + (q + 1))

                def combine(i):
                    e.wait_ge(y_ready, b * 4 + (i // 2 + 1))
                    if i >= 4:
                        e.wait_ge(acc_done, b * NT + (i - 2))
                    e.matmul(ps[4 + i % 4][:, 0:T], y_hi[:, i * P:(i + 1) * P], turned[:], start=True, stop=False)
                    e.matmul(ps[4 + i % 4][:, 0:T], y_lo[:, i * P:(i + 1) * P], turned[:], start=False, stop=True
                             ).then_inc(sc_done, 1)

                e.wait_ge(xg_ready, b + 1)
                for q in range(8):
                    i, bank = q // 2, 2 * (q // 2 % 2) + q % 2
                    split_ready(q)
                    if i >= 2:
                        e.wait_ge(hs_ready, b * 4 + (i - 1))
                    for k in range(NT):
                        wh = mhi[:, q % MSPL, k * GW:(k + 1) * GW]
                        wl = mlo[:, q % MSPL, k * GW:(k + 1) * GW]
                        e.matmul(ps[bank][:, 0:GW], xg_hi[:, k, :], wh, start=k == 0, stop=False)
                        e.matmul(ps[bank][:, 0:GW], xg_hi[:, k, :], wl, start=False, stop=False)
                        mm = e.matmul(ps[bank][:, 0:GW], xg_lo[:, k, :], wh, start=False, stop=k == NT - 1)
                    mm.then_inc(m_done, 1)
                e.wait_ge(acc_done, b * NT + 1)
                e.wait_ge(wc_ready, b + 1)
                for t, m in enumerate(TT):
                    mm = e.transpose(ps[5][:, t * P:t * P + m], wc[0:m, t, :], ident[0:m, 0:m])
                mm.then_inc(wt_done, 1)
                for f in range(NFE):
                    if f % 4 == 0:
                        e.wait_ge(hs_ready, b * 4 + min(4, (f + 4) * P // GW + 1))
                    mm = e.transpose(ps[(4, 0, 1)[f // 4]][:, (f % 4) * P:(f % 4 + 1) * P],
                                     hblk[:, f * P:(f + 1) * P], ident)
                    if f % 4 == 3 or f == NFE - 1:
                        mm.then_inc(ht_done, 1)
                if more:
                    gather(b + 1)
                for j in range(4):
                    q = 8 + j
                    split_ready(q)
                    out = ps[(2 + j) % 4][:, 0:DW]
                    for f in range(NFE):
                        if j == 0 and f % 4 == 0:
                            e.wait_ge(hT_ready, b * 3 + (f // 4 + 1))
                        wh = mhi[:, q % MSPL, f * DW:(f + 1) * DW]
                        wl = mlo[:, q % MSPL, f * DW:(f + 1) * DW]
                        e.matmul(out, hT_hi[:, f, :], wh, start=f == 0, stop=False)
                        e.matmul(out, hT_hi[:, f, :], wl, start=False, stop=False)
                        mm = e.matmul(out, hT_lo[:, f, :], wh, start=False, stop=f == NFE - 1)
                    mm.then_inc(m_done, 1)
                    if j == 1:
                        e.wait_ge(wct_ready, b + 1)
                        if more:
                            e.wait_ge(xg_ready, b + 2)
                    if j >= 1:
                        combine(2 * j - 2)
                        combine(2 * j - 1)
                combine(6)
                combine(7)

            with e.Fori(0, last) as b:
                expert(b, True)
            expert(last, False)
            norm(4)

        @block.scalar
        def _(e):
            links = [0]

            def link(ins):
                links[0] += 1
                ins.then_inc(act_c, 1)
                e.wait_ge(act_c, links[0])

            def high(c_static, c):
                s = c_static % RING
                e.wait_ge(raw_landed[s], (c - c_static) * 4 + 16 * (c_static // RING + 1))
                if c_static >= RING:
                    e.wait_ge(chunk_done, c - (RING - 1))
                e.activation(whi[:, s, :], raw[:, s, :], ACT.Copy).then_inc(hi_ready, 1)

            def stage(l, c0, n, evac, t0=None, splits=True, slices=None):
                def one(c_static, c):
                    e.wait_ge(chunk_done, c + 1)
                    if t0 is not None and c_static - c0_first + t0 >= RING:
                        e.wait_ge(tmp_used, c - c0_first + (t0 - RING + 1))
                    evac(c_static - c0_first, c - c0_first, ps[c_static % RING][:, 0:T]).then_inc(evac_done, 1)
                    if splits:
                        high(c_static + RING, c + RING)

                c0_first = c0
                if t0 == 0 or not splits or n < 4:
                    for c in range(c0, c0 + min(n, 4)):
                        one(c, c)
                    c0, n = c0 + 4, n - 4
                if n > 0:
                    with e.Fori(0, n // 4) as g:
                        for j in range(4):
                            one(c0 + j, g * 4 + (c0 + j))
                            if slices is not None and j == 1:
                                mod_copy(0, g + slices)
                        if slices is not None:
                            ada_copy(g + (slices + 1))

            def tile(buf, i):
                return buf[:, bass.ds(i, 1), :].rearrange("p a t -> p (a t)")

            def ada_copy(s):
                e.wait_ge(ada_rows, s + 1)
                e.wait_ge(ada_turned, s + 1)
                e.activation(modrow[:], ps[5][:], ACT.Copy).then_inc(row_copied, 1)

            def mod_copy(l, s):
                e.wait_ge(ada_turned, s + 2)
                e.activation(mod[l][:, bass.ds((s - NSLICE * l) * 4, 4), :].rearrange("p a b -> p (a b)"),
                             ps[6][:, 0:4 * NSEQ], ACT.Copy).then_inc(mod_copied, 1)

            def square(n, i):
                if n == 4:
                    e.wait_ge(x_final, i + 1)
                elif n:
                    e.wait_ge(tmp_used, (0, T_GU, T_BASE[1], T_BASE[1] + T_GU)[n] - (NT - 1 - i))
                e.activation(ab[:, i, :], x[:, i, :], ACT.Square).then_inc(sq_ready, 1)

            def norm_std(n, i0=0):
                for i in range(i0, NT):
                    square(n, i)
                e.wait_ge(stat_done, (0, 3, 4, 7, 8)[n] + 1)
                e.activation(std[:], ps[4][:, 0:T], ACT.Sqrt, bias=eps[:], scale=1.0 / D).then_inc(std_ready, 1)

            def modulate(n):
                l, k = n // 2, n % 2
                if n == 0:
                    e.wait_ge(mod_ready, 1)
                for i in range(NT):
                    e.wait_ge(xs_ready, NT * n + i + 1)
                    e.activation(bb[:, i, 0:TP], bb[:, i, 0:TP], ACT.Identity,
                                 scale=mod[l][:, 24 * k + 8 + i, 0:1], bias=mod[l][:, 24 * k + i, 0:1]
                                 ).then_inc(hn_ready, 1)

            e.sem_inc(row_copied, 1)
            e.sem_inc(mod_copied, 1)
            e.wait_ge(x_in, 48)
            e.wait_ge(const_ready, 3)
            e.activation(csil[:, :, 0:NSEQ], cv("c", None, NT * NSEQ).rearrange("p (k b) -> p k b", b=NSEQ),
                         ACT.Silu).then_inc(csil_ready, 1)
            for l in range(DEPTH):
                link(e.activation(small[:, 0, l, :], cv("lam", l, NT), ACT.Abs))
            for l in range(DEPTH):
                e.activation(small[:, 1, l, :], small[:, 0, l, :], ACT.Exp, scale=-1.0).then_inc(csil_ready, 1)
            norm_std(0)
            for s in range(NA):
                ada_copy(s)
                mod_copy(0, s)
            for c in range(RING):
                high(c, c)

            for l in range(DEPTH):
                st = stages(l)
                tb = T_BASE[l]
                if l == 0:
                    modulate(0)
                else:
                    norm_std(2, NT - 1)
                    for c in (st["gg"], st["gg"] + 1):
                        high(c, c)
                    modulate(2)
                    for c in (st["gg"] + 2, st["gg"] + 3):
                        high(c, c)

                ev_gg = lambda j, i, p: e.activation(tmp[:, j % RING, :], p, ACT.Sigmoid if j % 2 == 0 else ACT.Copy)
                if l == 0:
                    stage(l, st["gg"], 2, ev_gg, t0=tb)
                    ada_copy(NA)
                    stage(l, st["gg"] + 2, 1, lambda j, i, p: ev_gg(2, i, p), t0=tb + 2)
                    mod_copy(0, NA)
                    stage(l, st["gg"] + 3, 1, lambda j, i, p: ev_gg(3, i, p), t0=tb + 3)
                    ada_copy(NA + 1)
                else:
                    stage(l, st["gg"], 4, ev_gg, t0=tb)
                first = lambda n: NA + 1 + n if l == 0 else None
                stage(l, st["gg"] + 4, 12, ev_gg, t0=tb + 4, slices=first(0))

                def evac_xr(j, i, p):
                    e.activation(xrp[:, bass.ds(i, 1), PR:PR + TP].rearrange("p a t -> p (a t)"), p[:, 0:TP],
                                 ACT.Copy)
                    return e.activation(sa_of(xrp, i, PR), samples(p), ACT.Copy)

                def sa_of(buf, i, hist):
                    w = hist + TS
                    row = buf[:, bass.ds(i, 1), hist + TP:hist + TP + NB * w].rearrange("p a w -> p (a w)")
                    return row.rearrange("p (b t) -> p b t", b=NB)[:, :, hist:hist + TS]

                stage(l, st["xr"], 8, evac_xr, slices=first(3))
                stage(l, st["yr"], 4, lambda j, i, p: e.activation(tile(gy, i), p, ACT.Gelu_apprx_tanh),
                      slices=first(5))

                for i in range(NT):
                    for w, (buf, b) in enumerate(((ab, "ba"), (bb, "bx"))):
                        n = 2 * i + w
                        e.wait_ge(rg_done, 2 * NT * l + n + 1)
                        e.activation(buf[:, i, :], ps[4 + n % 4][:, 0:T], ACT.Sigmoid, bias=col(b, l, i)
                                     ).then_inc(rg_sig, 1)
                e.wait_ge(st_ready, 2 * l + 1)
                e.wait_ge(rg_sig, 2 * NT * (l + 1))
                for i in range(NT):
                    e.activation(th[:, i, :], ab[:, i, :], ACT.Tanh, scale=sp8[:, l, i:i + 1])
                    ins = e.activation(ab[:, i, :], ab[:, i, :], ACT.Exp, scale=sp8[:, l, i:i + 1])
                ins.then_inc(rg_exp, 1)
                stage(l, st["yr"] + 4, 4, lambda j, i, p: e.activation(tile(gy, i + 4), p, ACT.Gelu_apprx_tanh))
                if l == 0:
                    mod_copy(0, NSLICE - 1)
                stage(l, st["ga"], 2, lambda j, i, p: e.activation(tile(sga, i), p, ACT.Sigmoid))
                e.wait_ge(rg_sq, l + 1)
                e.activation(th[:], th[:], ACT.Sqrt, scale=-1.0).then_inc(rg_root, 1)
                stage(l, st["ga"] + 2, 2, lambda j, i, p: e.activation(tile(sga, i + 2), p, ACT.Sigmoid))
                stage(l, st["ga"] + 4, 4, lambda j, i, p: e.activation(tile(sga, i + 4), p, ACT.Sigmoid))
                stage(l, st["ba"], 8, lambda j, i, p: e.activation(tile(gy, i), p, ACT.Copy))

                def gate_b(j0, n):
                    stage(l, st["gb"] + j0, n, lambda j, i, p: e.activation(tile(sgb, i + j0), p, ACT.Sigmoid))

                gate_b(0, 2)
                e.wait_ge(stat_done, 4 * l + 2)
                e.activation(mean[:], ps[4][:, 0:T], ACT.Copy, scale=1.0 / D).then_inc(ln_act, 1)
                gate_b(2, 1)
                e.wait_ge(ln_cent, (1 + NT) * l + 1)
                e.activation(th[:], v[:], ACT.Square).then_inc(ln_act, 1)
                gate_b(3, 2)
                e.wait_ge(stat_done, 4 * l + 3)
                e.activation(std[:], ps[4][:, 0:T], ACT.Sqrt, bias=eps[:], scale=1.0 / D).then_inc(std_ready, 1)
                for i in range(NT):
                    e.wait_ge(ln_cent, (1 + NT) * l + 1 + i + 1)
                    e.activation(v[:, i, :], v[:, i, :], ACT.Silu, scale=col("lng", l, i), bias=col("lnb", l, i)
                                 ).then_inc(ln_act, 1)
                gate_b(5, 3)
                stage(l, st["bb"], 8, lambda j, i, p: e.activation(tmp[:, j % RING, :], p, ACT.Identity,
                                                                   bias=col("bbb", l, i)), t0=tb + 16)
                ev_tmp = lambda j, i, p: e.activation(tmp[:, j % RING, :], p, ACT.Copy)
                stage(l, st["wo"], 4, ev_tmp, t0=tb + 24)
                for j in range(4):
                    stage(l, st["wo"] + 4 + j, 1, lambda _, i, p: ev_tmp(j, i, p), t0=tb + 28 + j, splits=l == 0)
                    square(2 * l + 1, j)
                norm_std(2 * l + 1, 4)
                modulate(2 * l + 1)
                if l == 0:
                    ada_copy(NSLICE)
                    gu = lambda j, i, p: e.activation(tmp[:, j % RING, :], p, ACT.Silu if j % 2 == 0 else ACT.Copy)

                    def four(g8, c0, s):
                        for j in range(4):
                            c = g8 + (c0 + j)
                            e.wait_ge(chunk_done, c + 1)
                            e.wait_ge(tmp_used, c + (T_GU - st["gu"] - RING + 1))
                            gu(j, None, ps[(c0 + j) % RING][:, 0:T]).then_inc(evac_done, 1)
                            high(c0 + j + RING, c + RING)
                            if j == 1:
                                mod_copy(1, s)

                    four(0, st["gu"], NSLICE)
                    ada_copy(NSLICE + 1)
                    with e.Fori(0, 5) as g:
                        for h in range(2):
                            four(g * 8, st["gu"] + 4 + 4 * h, g * 2 + (NSLICE + 1 + h))
                            ada_copy(g * 2 + (NSLICE + 2 + h))
                    mod_copy(1, 2 * NSLICE - 1)
                    with e.Fori(0, 4) as g:
                        for j in range(4):
                            high(st["dn"] + 4 + j, g * 4 + (st["dn"] + 4 + j))
                    for c in range(st["dn"] + 20, st["dn"] + NF):
                        high(c, c)
                    for m in range(NT):
                        if m < NT - 1:
                            e.wait_ge(down_done, m + 1)
                        else:
                            e.wait_ge(chunk_done, st["dn"] + NF)
                        e.wait_ge(tmp_used, T_GU + 2 * NF + m - 3)
                        e.activation(tmp[:, m % RING, :], ps[m][:, 0:T], ACT.Copy).then_inc(evac_done, 1)
                        if m >= 1:
                            square(2, m - 1)

            def mhigh(b, q):
                s = q % MPER
                e.wait_ge(m_landed[s % MRAW], b * (16 * MPER // MRAW) + 16 * (q // MRAW + 1))
                if q >= MSPL:
                    e.wait_ge(m_done, b * MPER + (q - MSPL + 1))
                e.activation(mhi[:, s % MSPL, :], mraw[:, s % MRAW, :], ACT.Copy).then_inc(m_hi, 1)

            for q in range(MSPL):
                mhigh(0, q)
            e.wait_ge(r_dve, 1)
            e.activation(route[:, R_P:R_P + 24], route[:, R_P:R_P + 24], ACT.Exp).then_inc(r_act, 1)
            e.wait_ge(r_pe, 2)
            for t, m in enumerate(TT):
                for h in range(2):
                    e.activation(hn_tok[0:m, 0, t, h * 512:(h + 1) * 512], ps[2 + 2 * t + h][0:m, :], ACT.Copy
                                 ).then_inc(hn_part, 1)
            for t, m in enumerate(TT):
                e.wait_ge(hn_rest, 2 * t + 2)
                e.activation(hn_tok[0:m, 1, t, :], rest[0:m, t, :], ACT.Copy).then_inc(hn_part, 1)
            e.wait_ge(routed, 1)
            last = e.value_load(nbi[0:1, 1:2], min_val=NE - 1, max_val=NBLK - 1)

            def gathered(n):
                e.wait_ge(g_done, n + 1)
                for h in range(2):
                    ins = e.activation(xg_hi[:, 4 * h:4 * h + 4, :].rearrange("p a s -> p (a s)"), ps[6 + h][:],
                                       ACT.Copy)
                ins.then_inc(xg_hi_ready, 1)

            gathered(0)

            def expert(b, more):
                for q in range(MPER):
                    if q < 8 and q % 2 == 0:
                        i = q // 2
                        e.wait_ge(m_done, b * MPER + (q + 1))
                        if i >= 2:
                            e.wait_ge(hs_ready, b * 4 + (i - 1))
                        e.activation(gsil[:, i % 2, :], ps[2 * (i % 2)][:, 0:GW], ACT.Silu).then_inc(gsil_ready, 1)
                    if q == 8:
                        for n, (bank, w) in enumerate(((4, 512), (0, 512), (1, 384))):
                            e.wait_ge(ht_done, b * 3 + (n + 1))
                            e.activation(hT_hi[:, 4 * n:4 * n + w // P, :].rearrange("p a s -> p (a s)"),
                                         ps[bank][:, 0:w], ACT.Copy).then_inc(hT_hi_ready, 1)
                        if more:
                            gathered(b + 1)
                    if q >= 8:
                        j = q - 8
                        e.wait_ge(m_done, b * MPER + (q + 1))
                        e.wait_ge(wct_ready, b + 1)
                        e.activation(y_hi[:, j * DW:(j + 1) * DW], ps[(2 + j) % 4][:, 0:DW], ACT.Copy,
                                     scale=wslot[:, 0:1]).then_inc(y_hi_ready, 1)
                    if q + MSPL < MPER or more:
                        mhigh(b, q + MSPL)

            with e.Fori(0, last) as b:
                expert(b, True)
            expert(last, False)
            norm_std(4)

        @block.vector
        def _(e):
            links = [0]

            def link(ins):
                links[0] += 1
                ins.then_inc(dve_c, 1)
                e.wait_ge(dve_c, links[0])

            def low(n, out, hi, src):
                return e.tensor_tensor(out, src, hi.bitcast(F32), ALU.subtract)

            def bc_tiles(ap, w):
                return ap.unsqueeze(1).broadcast_to([P, NT, w])

            def bc_seq(ap):
                return ap.unsqueeze(3).broadcast_to([P, NT, NB, TS])

            def norm(n, split):
                l, k = n // 2, n % 2
                e.wait_ge(std_ready, (1, 3, 4, 6, 7)[n])
                link(e.reciprocal(rstd[:], std[:]))
                if n == 4:
                    for i in range(NT):
                        e.scalar_tensor_tensor(out=bb[:, i, :], in0=x[:, i, :], scalar=col("fg", None, i),
                                               in1=rstd[:], op0=ALU.mult, op1=ALU.mult).then_inc(y_out, 1)
                    return
                for i in range(NT):
                    e.tensor_tensor(bb[:, i, 0:TP], x[:, i, 0:TP], rstd[:, 0:TP], ALU.mult).then_inc(xs_ready, 1)
                link(e.tensor_tensor(bb[:, :, TP:T], x[:, :, TP:T], bc_tiles(rstd[:, TP:T], T - TP), ALU.mult))
                if n == 0:
                    finish_mod(0, 0, 2 * NT)
                link(e.tensor_tensor(samples8(bb), samples8(bb), bc_seq(mod[l][:, 24 * k + 8:24 * k + 16, 1:]),
                                     ALU.mult))
                link(e.tensor_tensor(samples8(bb), samples8(bb), bc_seq(mod[l][:, 24 * k:24 * k + 8, 1:]),
                                     ALU.add))
                if not split:
                    e.sem_inc(norm_ready, 1)
                else:
                    for i in range(NT):
                        e.wait_ge(hn_ready, NT * n + i + 1)
                        link(e.tensor_copy(xn_hi[:, i, :], bb[:, i, :]))
                        low(1, xn_lo[:, i, :], xn_hi[:, i, :], bb[:, i, :]).then_inc(norm_ready, 1)

            conv_n = [0]

            def conv(l, K, tiles, srcs, dst, w, b, between=None):
                sums = 2 * len(tiles) - (sum(i >= NV for i in tiles) if K == KC else 0)
                for k in range(K):
                    if between and k in between:
                        between[k]()
                    for i in tiles:
                        pr, sa = seg(srcs, i, K - 1, k)
                        parts = [(pr, dst[:, i, 0:TP]), (sa, samples(dst[:, i, :]))]
                        if K == KC and i >= NV:
                            parts.pop()
                        for src, out in parts:
                            if k == 0:
                                ins = e.tensor_scalar(out, src, col(w, l, i), col(b, l, i), ALU.mult, ALU.add)
                            else:
                                e.wait_ge(conv_step, conv_n[0] - (sums - 1))
                                ins = e.scalar_tensor_tensor(out=out, in0=src, scalar=col(w, l, k * NT + i),
                                                             in1=out, op0=ALU.mult, op1=ALU.add)
                            ins.then_inc(conv_step, 1)
                            conv_n[0] += 1

            def finish_mod(l, a, b):
                e.wait_ge(mod_copied, NSLICE * l + b // 4 + 1)
                m = mod[l]
                link(e.tensor_tensor(m[:, a:b, :], m[:, a:b, :], cv("adab", l, 48)[:, a:b].unsqueeze(2).broadcast_to(
                    [P, b - a, NSEQ]), ALU.add))
                for k, g in ((8, "n1g"), (32, "n2g")):
                    if a <= k < b:
                        e.scalar_tensor_tensor(out=m[:, k:k + 8, :], in0=m[:, k:k + 8, :], scalar=1.0,
                                               in1=cv(g, l, NT).unsqueeze(2).broadcast_to([P, NT, NSEQ]),
                                               op0=ALU.add, op1=ALU.mult).then_inc(mod_ready, 1)
                for k in (16, 40):
                    if a <= k < b:
                        e.tensor_scalar(m[:, k:k + 8, :], m[:, k:k + 8, :], 1.0, None, ALU.add
                                        ).then_inc(mod_ready, 1)
                e.wait_ge(mod_ready, 4 * l + (1 if b <= 16 else 4))

            def residual(l, k, i, src, last):
                e.scalar_tensor_tensor(out=x[:, i, 0:TP], in0=src[:, 0:TP], scalar=mod[l][:, k + i, 0:1],
                                       in1=x[:, i, 0:TP], op0=ALU.mult, op1=ALU.add)
                link(e.tensor_tensor(samples(src), samples(src), bc_t(mod[l][:, k + i, 1:]), ALU.mult))
                e.tensor_tensor(samples(x[:, i, :]), samples(x[:, i, :]), samples(src), ALU.add
                                ).then_inc(last, 1)

            e.sem_inc(acc_done, 1)
            e.wait_ge(x_in, 48)
            e.wait_ge(csil_ready, 1 + DEPTH)
            lam2 = [small[:, k, :, :].rearrange("p l i -> p (l i)") for k in range(8)]
            link(e.tensor_scalar(lam2[2], lam2[1], 2.0, None, ALU.add))
            link(e.reciprocal(lam2[3], lam2[2]))
            link(e.tensor_tensor(lam2[4], lam2[1], lam2[3], ALU.mult))
            link(e.tensor_tensor(lam2[5], lam2[4], lam2[4], ALU.mult))
            link(e.tensor_scalar(lam2[6], lam2[5], 1.0 / 19, None, ALU.mult))
            for k in range(8, 0, -1):
                link(e.scalar_tensor_tensor(out=lam2[6], in0=lam2[6], scalar=1.0 / (2 * k + 1), in1=lam2[5],
                                            op0=ALU.add, op1=ALU.mult))
            link(e.scalar_tensor_tensor(out=lam2[6], in0=lam2[6], scalar=1.0, in1=lam2[4], op0=ALU.add,
                                        op1=ALU.mult))
            for l in range(DEPTH):
                link(e.tensor_scalar(small[:, 7, l, :], cv("lam", l, NT), -1.0, 0.0, ALU.mult, ALU.max))
            link(e.scalar_tensor_tensor(out=lam2[6], in0=lam2[6], scalar=2.0, in1=lam2[7], op0=ALU.mult,
                                        op1=ALU.add))
            link(e.tensor_scalar(sp8[:].rearrange("p l i -> p (l i)"), lam2[6], -8.0, None, ALU.mult))

            flat = lambda buf: buf[:].rearrange("p i t -> p (i t)")
            for l in range(DEPTH):
                st = stages(l)
                tb, eo = T_BASE[l], E_OFF[l]
                norm(2 * l, True)
                if l == 0:
                    e.wait_ge(pad_ready, 2)
                def make_u(i):
                    e.wait_ge(evac_done, st["gg"] - eo + 2 * i + 2)
                    s = 2 * i % RING
                    pr, sa = seg(upad, i, PC, PC)
                    e.tensor_tensor(pr, tmp[:, s, 0:TP], tmp[:, s + 1, 0:TP], ALU.mult)
                    e.tensor_tensor(sa, samples(tmp[:, s, :]), samples(tmp[:, s + 1, :]), ALU.mult
                                    ).then_inc(tmp_used, 2)

                make_u(0)
                make_u(1)
                e.wait_ge(rc_in, 16 * 2 * NT * (l + 1))
                e.wait_ge(pad_ready, 2 * (l + 1))
                e.wait_ge(tmp_used, tb + 4)
                if l == 0:
                    e.wait_ge(ada_rows, NA + 1)
                conv(l, KC, (0, 1), upad, v, "ccw", "ccb", {7 * n: (lambda i=n + 1: make_u(i)) for n in range(1, 5)})
                e.wait_ge(tmp_used, tb + 12)
                def short_conv():
                    e.wait_ge(evac_done, st["xr"] - eo + NT)
                    for pair in range(NT // 2):
                        conv(l, KR, (2 * pair, 2 * pair + 1), xrp, xc, "rgw", "rgb")
                    if l:
                        e.wait_ge(out_done, STORES * l)
                    e.tensor_copy(rclast[:, :, 0, :], xrp[:, :, TP:TP + PR])
                    e.tensor_copy(rclast[:, :, 1:, :], xrp[:, :, PR + TP:].rearrange(
                        "p i (b t) -> p i b t", b=NB)[:, :, :, TS:TS + PR]).then_inc(st_ready, 1)

                conv(l, KC, (2, 3), upad, v, "ccw", "ccb",
                     {4: lambda: make_u(6), 11: lambda: make_u(7), K_SHORT: short_conv})
                e.wait_ge(tmp_used, tb + 16)
                def decay():
                    e.wait_ge(rg_exp, l + 1)
                    link(e.tensor_tensor(flat(bb), flat(bb), flat(xc), ALU.mult))
                    link(e.tensor_tensor(flat(xc), flat(ab), flat(ab), ALU.mult))
                    e.scalar_tensor_tensor(out=flat(th), in0=flat(xc), scalar=1.0, in1=flat(th), op0=ALU.add,
                                           op1=ALU.mult).then_inc(rg_sq, 1)

                def recur():
                    e.wait_ge(rg_root, l + 1)
                    link(e.tensor_tensor(flat(bb), flat(bb), flat(th), ALU.mult))
                    first = lambda buf: samples8(buf)[:, :, :, 0]
                    h9 = hlast[:, :, 1:]
                    link(e.tensor_tensor(h9, first(ab), cv("h0", l, NT * NB).rearrange("p (i b) -> p i b", b=NB),
                                         ALU.mult))
                    link(e.tensor_tensor(first(bb), first(bb), h9, ALU.add))
                    e.memset(first(ab), 0.0).then_inc(dve_c, 1)
                    e.memset(ab[:, :, 0], 0.0).then_inc(dve_c, 1)
                    links[0] += 2
                    e.wait_ge(dve_c, links[0])
                    link(e.tensor_tensor_scan(flat(xc), flat(ab), flat(bb), 0.0, ALU.mult, ALU.add))
                    e.tensor_copy(hlast[:, :, 0], xc[:, :, TP - 1])
                    e.tensor_copy(hlast[:, :, 1:], samples8(xc)[:, :, :, TS - 1]).then_inc(st_ready, 1)
                    e.wait_ge(evac_done, st["yr"] - eo + NT)
                    for h in range(2):
                        half = lambda buf: buf[:, 4 * h:4 * h + 4, :].rearrange("p i t -> p (i t)")
                        link(e.tensor_tensor(half(gy), half(gy), half(xc), ALU.mult))
                        link(e.tensor_copy(half(q_hi), half(gy)))
                        low(1, half(q_lo), half(q_hi), half(gy)).then_inc(q_ready, 1)

                conv(l, KC, (4, 5, 6, 7), upad, v, "ccw", "ccb", {9: decay, 13: recur})
                if l == 0:
                    finish_mod(0, 2 * NT, 48)
                e.wait_ge(ln_act, 10 * l + 1)
                e.tensor_tensor(v[:], v[:], bc_tiles(mean[:], T), ALU.subtract).then_inc(ln_cent, 1)
                e.wait_ge(std_ready, 3 * l + 2)
                link(e.reciprocal(rstd[:], std[:]))
                for i in range(NT):
                    e.tensor_tensor(v[:, i, :], v[:, i, :], rstd[:], ALU.mult).then_inc(ln_cent, 1)
                for i in range(NT):
                    e.wait_ge(ln_act, 10 * l + 2 + i + 1)
                    link(e.tensor_copy(q_hi[:, i, :], v[:, i, :]))
                    low(1, q_lo[:, i, :], q_hi[:, i, :], v[:, i, :]).then_inc(v_ready, 1)
                link(e.tensor_tensor(flat(gy), flat(gy), flat(sga), ALU.mult))
                for i in range(NT):
                    e.wait_ge(evac_done, st["bb"] - eo + i + 1)
                    tm = tmp[:, i % RING, :]
                    link(e.tensor_tensor(tm, tm, sgb[:, i, :], ALU.mult))
                    e.tensor_tensor(sgb[:, i, :], tm, gy[:, i, :], ALU.add).then_inc(tmp_used, 1)
                    e.wait_ge(tmp_used, tb + 16 + i + 1)
                    link(e.tensor_copy(xn_hi[:, i, :], sgb[:, i, :]))
                    low(1, xn_lo[:, i, :], xn_hi[:, i, :], sgb[:, i, :]).then_inc(m_ready, 1)
                for i in range(NT):
                    e.wait_ge(evac_done, st["wo"] - eo + i + 1)
                    residual(l, 16, i, tmp[:, i % RING, :], tmp_used)
                norm(2 * l + 1, l == 0)
                if l == 0:
                    for f in range(NF):
                        e.wait_ge(evac_done, st["gu"] + 2 * f + 2)
                        s = 2 * f % RING
                        hf = tmp[:, s, :]
                        link(e.tensor_tensor(hf, hf, tmp[:, s + 1, :], ALU.mult))
                        link(e.tensor_copy(h_hi[:, f, :], hf))
                        low(1, h_lo[:, f, :], h_hi[:, f, :], hf).then_inc(tmp_used, 2)
                    finish_mod(1, 0, 48)
                    for i in range(NT):
                        e.wait_ge(evac_done, st["dn"] + i + 1)
                        residual(l, 40, i, tmp[:, i % RING, :], tmp_used)

            R = lambda off, n: route[:, off:off + n]
            S3 = lambda ap: ap.rearrange("p (t e) -> p t e", e=NE)
            bias = cv("br", None, NE).unsqueeze(1).broadcast_to([P, 3, NE])

            def mlow(b, q):
                s = q % MPER
                e.wait_ge(m_hi, b * MPER + (q + 1))
                low(1, mlo[:, s % MSPL, 0:MDVE], mhi[:, s % MSPL, 0:MDVE], mraw[:, s % MRAW, 0:MDVE]
                    ).then_inc(m_lo_dve, 1)

            for q in range(MSPL):
                mlow(0, q)
            link(e.memset(R(R_P, 24), 0.0))
            e.wait_ge(r_pe, 1)
            link(e.tensor_copy(R(R_P, 16), ps[0][:, 0:16]))
            link(e.tensor_copy(route[0:64, R_P + 16:R_P + 24], ps[0][0:64, 16:24]))
            pp = R(R_P, 24)
            link(e.tensor_tensor(S3(pp), S3(pp), bias, ALU.add))
            link(e.tensor_reduce(R(R_T, 3), S3(pp), AX.X, ALU.max))
            bc3 = lambda ap: ap.unsqueeze(2).broadcast_to([P, 3, NE])
            e.tensor_tensor(S3(pp), S3(pp), bc3(R(R_T, 3)), ALU.subtract).then_inc(r_dve, 1)
            e.wait_ge(r_act, 1)
            link(e.tensor_reduce(R(R_T, 3), S3(pp), AX.X, ALU.add))
            link(e.reciprocal(R(R_T + 4, 3), R(R_T, 3)))
            link(e.tensor_tensor(S3(pp), S3(pp), bc3(R(R_T + 4, 3)), ALU.mult))
            pj = S3(pp).unsqueeze(2).broadcast_to([P, 3, NE, NE])
            pe_ = S3(pp).unsqueeze(3).broadcast_to([P, 3, NE, NE])
            g4 = lambda ap: ap.rearrange("p (t e j) -> p t e j", e=NE, j=NE)
            link(e.tensor_tensor(g4(R(R_A, 192)), pj, pe_, ALU.is_gt))
            link(e.tensor_tensor(g4(R(R_B, 192)), pj, pe_, ALU.is_equal))
            before = ct("jlt", NE * NE)
            link(e.tensor_tensor(R(R_B, 192).rearrange("p (t m) -> p t m", t=3),
                                 R(R_B, 192).rearrange("p (t m) -> p t m", t=3),
                                 before.unsqueeze(1).broadcast_to([P, 3, NE * NE]), ALU.mult))
            link(e.tensor_tensor(R(R_A, 192), R(R_A, 192), R(R_B, 192), ALU.add))
            link(e.tensor_reduce(S3(R(R_C, 24)), g4(R(R_A, 192)), AX.X, ALU.add))
            sel = R(R_SEL, 24)
            link(e.tensor_scalar(sel, R(R_C, 24), 2.0, None, ALU.is_lt))
            link(e.memset(route[64:128, R_SEL + 16:R_SEL + 24], 0.0))
            e.tensor_tensor(R(R_W, 24), sel, pp, ALU.mult).then_inc(r_dve, 1)
            e.wait_ge(r_dve, 2)
            link(e.tensor_reduce(R(R_T, 3), S3(R(R_W, 24)), AX.X, ALU.add))
            link(e.tensor_scalar(R(R_T, 3), R(R_T, 3), 1e-30, None, ALU.max))
            link(e.reciprocal(R(R_T + 4, 3), R(R_T, 3)))
            link(e.tensor_tensor(S3(R(R_W, 24)), S3(R(R_W, 24)), bc3(R(R_T + 4, 3)), ALU.mult))
            for t, m in enumerate(TT):
                for h in range(2):
                    e.wait_ge(hn_part, 2 * t + h + 1)
                    e.tensor_tensor(rest[0:m, t, h * 512:(h + 1) * 512], ps[2 + 2 * t + h][0:m, :],
                                    hn_tok[0:m, 0, t, h * 512:(h + 1) * 512], ALU.subtract).then_inc(hn_rest, 1)
            e.wait_ge(r_pe, 3)
            link(e.tensor_copy(R(R_N, 32), ps[1][:, 0:32]))
            link(e.tensor_scalar(R(R_T, 8), R(R_N, 8), float(P), None, ALU.is_gt))
            link(e.tensor_scalar(R(R_T + 8, 8), R(R_N, 8), float(2 * P), 1.0, ALU.is_gt, ALU.add))
            link(e.tensor_tensor(R(R_T, 8), R(R_T, 8), R(R_T + 8, 8), ALU.add))
            link(e.tensor_tensor(R(R_A, 64).rearrange("p (e j) -> p e j", j=NE),
                                 R(R_T, 8).unsqueeze(1).broadcast_to([P, NE, NE]),
                                 before.rearrange("p (e j) -> p e j", j=NE), ALU.mult))
            link(e.tensor_reduce(R(R_BASE, 8), R(R_A, 64).rearrange("p (e j) -> p e j", j=NE), AX.X, ALU.add))
            link(e.tensor_reduce(R(R_T + 8, 1), R(R_T, 8), AX.X, ALU.add))
            link(e.tensor_scalar(R(R_T + 9, 1), R(R_T + 8, 1), -1.0, None, ALU.add))
            link(e.tensor_copy(nbi[:], R(R_T + 8, 2)))
            link(e.tensor_scalar(R(R_BASE, 8), R(R_BASE, 8), float(P), None, ALU.mult))
            slot = R(R_C, 24)
            link(e.tensor_tensor(S3(slot), S3(R(R_N + 8, 24)), R(R_BASE, 8).unsqueeze(1).broadcast_to([P, 3, NE]),
                                 ALU.add))
            link(e.scalar_tensor_tensor(out=slot, in0=slot, scalar=1.0, in1=sel, op0=ALU.add, op1=ALU.mult))
            link(e.tensor_scalar(slot, slot, -1.0, None, ALU.add))
            n3 = 3 * NBLK * NE
            b4 = lambda ap: ap.rearrange("p (t b e) -> p t b e", b=NBLK, e=NE)
            blk4 = ct("blk", NBLK).unsqueeze(1).unsqueeze(3).broadcast_to([P, 3, NBLK, NE])
            over_b = lambda ap: S3(ap).unsqueeze(2).broadcast_to([P, 3, NBLK, NE])
            link(e.tensor_tensor(b4(R(R_REL, n3)), over_b(slot), blk4, ALU.subtract))
            link(e.tensor_scalar(R(R_M, n3), R(R_REL, n3), 0.0, None, ALU.is_ge))
            link(e.scalar_tensor_tensor(out=R(R_M, n3), in0=R(R_REL, n3), scalar=float(P), in1=R(R_M, n3),
                                        op0=ALU.is_lt, op1=ALU.mult))
            link(e.scalar_tensor_tensor(out=R(R_REL, n3), in0=R(R_REL, n3), scalar=1.0, in1=R(R_M, n3),
                                        op0=ALU.add, op1=ALU.mult))
            link(e.tensor_reduce(colpos[:], b4(R(R_REL, n3)), AX.X, ALU.add))
            link(e.tensor_scalar(colpos[:], colpos[:], -1.0, None, ALU.add))
            link(e.tensor_tensor(b4(R(R_M, n3)), b4(R(R_M, n3)), over_b(R(R_W, 24)), ALU.mult))
            link(e.tensor_reduce(colw[:], b4(R(R_M, n3)), AX.X, ALU.add))
            be = R(R_REL, NBLK * NE).rearrange("p (b e) -> p b e", e=NE)
            link(e.tensor_tensor(be, R(R_BASE, 8).unsqueeze(1).broadcast_to([P, NBLK, NE]),
                                 ct("blk", NBLK).unsqueeze(2).broadcast_to([P, NBLK, NE]), ALU.is_le))
            link(e.tensor_reduce(R(R_T, NBLK), be, AX.X, ALU.add))
            link(e.tensor_scalar(R(R_T, NBLK), R(R_T, NBLK), -1.0, None, ALU.add))
            link(e.tensor_copy(ebi[:], R(R_T, NBLK)))

            def pick(b):
                for t, m in enumerate(TT):
                    ins = e.tensor_scalar(sm[0:m, t, :], ct("iota", P)[0:m, :],
                                          colpos[0:m, t, bass.ds(b, 1)], None, ALU.is_equal)
                ins.then_inc(s_ready, 1)

            def tokens(n):
                e.wait_ge(xg_hi_ready, n + 1)
                for h in range(2):
                    ins = low(1, xg_lo[:, 4 * h:4 * h + 4, :].rearrange("p a s -> p (a s)"),
                              xg_hi[:, 4 * h:4 * h + 4, :].rearrange("p a s -> p (a s)"), ps[6 + h][:])
                ins.then_inc(xg_ready, 1)

            pick(0)
            e.wait_ge(s_ready, 1)
            e.sem_inc(routed, 1)
            last = e.value_load(nbi[0:1, 1:2], min_val=NE - 1, max_val=NBLK - 1)
            tokens(0)
            e.wait_ge(acc_zero, 1)

            def expert(b, more):
                def weighted_low(j):
                    e.wait_ge(y_hi_ready, b * 4 + (j + 1))
                    e.scalar_tensor_tensor(out=y_lo[:, j * DW:(j + 1) * DW], in0=ps[(2 + j) % 4][:, 0:DW],
                                           scalar=wslot[:, 0:1], in1=y_hi[:, j * DW:(j + 1) * DW].bitcast(F32),
                                           op0=ALU.mult, op1=ALU.subtract).then_inc(y_ready, 1)

                def add(i):
                    e.wait_ge(sc_done, b * NT + (i + 2))
                    e.tensor_tensor(acc[:, i, :], acc[:, i, :], ps[4 + i % 4][:, 0:T], ALU.add
                                    ).then_inc(acc_done, 1)

                for t, m in enumerate(TT):
                    ins = e.tensor_scalar(wc[0:m, t, :], ct("iota", P)[0:m, :], colpos[0:m, t, bass.ds(b, 1)],
                                          colw[0:m, t, bass.ds(b, 1)], ALU.is_equal, ALU.mult)
                ins.then_inc(wc_ready, 1)
                if more:
                    e.wait_ge(g_done, b + 1)
                    pick(b + 1)
                for q in range(MPER):
                    if q < 8 and q % 2 == 1:
                        i = q // 2
                        e.wait_ge(m_done, b * MPER + (q + 1))
                        e.wait_ge(gsil_ready, b * 4 + (i + 1))
                        if i == 0:
                            e.wait_ge(sc_done, b * NT + 1)
                        e.tensor_tensor(hblk[:, i * GW:(i + 1) * GW], gsil[:, i % 2, :], ps[2 * (i % 2) + 1][:, 0:GW],
                                        ALU.mult).then_inc(hs_ready, 1)
                    if q == 8:
                        for n, (bank, w) in enumerate(((4, 512), (0, 512), (1, 384))):
                            e.wait_ge(hT_hi_ready, b * 3 + (n + 1))
                            hi = hT_hi[:, 4 * n:4 * n + w // P, :].rearrange("p a s -> p (a s)")
                            lo = hT_lo[:, 4 * n:4 * n + w // P, :].rearrange("p a s -> p (a s)")
                            low(1, lo, hi, ps[bank][:, 0:w]).then_inc(hT_ready, 1)
                        if more:
                            tokens(b + 1)
                        e.wait_ge(wt_done, b + 1)
                        e.tensor_reduce(wslot[:], ps[5][:, 0:T], AX.X, ALU.add)
                        e.tensor_scalar(turned[:], ps[5][:, 0:T], 0.0, None, ALU.is_gt).then_inc(wct_ready, 1)
                        mlow(b, 10)
                    if q >= 8:
                        weighted_low(q - 8)
                    for c in {6: (), 7: (9,), 10: (), 11: (13, 14)}.get(q, (q + MSPL,)):
                        if c < MPER or more:
                            mlow(b, c)
                    if q >= 9:
                        add(2 * q - 18)
                        add(2 * q - 17)
                add(6)
                add(7)

            with e.Fori(0, last) as b:
                expert(b, True)
            expert(last, False)
            for i in range(NT):
                e.wait_ge(acc_done, last * NT + (i + 2))
                residual(1, 40, i, acc[:, i, :], x_final)
            norm(4, False)


def kernel(**a):
    import numpy as np
    import concourse.bacc as bacc
    from concourse.bass_utils import run_bass_kernel_spmd

    a = {k: np.asarray(v) for k, v in a.items()}

    def tiles(w):
        k, m = w.shape
        return w.reshape(k // P, P, m // P, P).transpose(2, 1, 0, 3).reshape(m // P, P, k)

    def slices(w, n):
        k, m = w.shape
        return w.reshape(k // P, P, m // n, n).transpose(2, 1, 0, 3).reshape(m // n, P, k // P * n)

    def columns(v):
        v = np.moveaxis(v.reshape(v.shape[:-1] + (v.shape[-1] // P, P)), -1, 0)
        return v.reshape(P, -1)

    parts = []
    for l in range(DEPTH):
        w = tiles(a["w_in"][l])
        parts.append(np.stack([w[24:32], w[16:24]], 1).reshape(16, P, D))
        parts += [w[0:16], w[32:40], tiles(a["w_branch_a"][l]), w[40:48], tiles(a["w_branch_b"][l]),
                  tiles(a["w_out"][l])]
        if l == 0:
            parts.append(np.stack([tiles(a["ffn_w_gate"][0]), tiles(a["ffn_w_up"][0])], 1).reshape(2 * NF, P, D))
            parts.append(a["ffn_w_down"][0].reshape(NF, P, D))
    stream = np.concatenate(parts)
    ada = np.concatenate([slices(a["ada_w"][l], 512) for l in range(DEPTH)]).reshape(DEPTH * NSLICE, P, NT, 512)
    moe = []
    for x in range(NE):
        g, u = slices(a["moe_w_gate"][0, x], GW), slices(a["moe_w_up"][0, x], GW)
        moe += [np.stack([g, u], 1).reshape(8, P, MCH), slices(a["moe_w_down"][0, x], DW)]
    moe = np.concatenate(moe)

    pk = []
    for l in range(DEPTH):
        for n in ("norm1_g", "norm2_g", "rg_conv_w", "rg_conv_b", "rg_ba", "rg_bx", "rg_lambda", "cc_dw_w",
                  "cc_dw_b", "cc_ln_g", "cc_ln_b", "b_branch_b", "ada_b"):
            pk.append(columns(a[n][l]))
        pk.append(a["state_rglru_h"][l].reshape(NB, NT, P).transpose(2, 1, 0).reshape(P, -1))
    pk.append(columns(a["final_norm_g"]))
    c = np.concatenate([a["c_prompt"], a["c_sample"]])
    pk.append(c.reshape(NSEQ, NT, P).transpose(2, 1, 0).reshape(P, -1))
    pk.append(a["moe_router_w"][0].reshape(NT, P, NE).transpose(1, 0, 2).reshape(P, -1))
    pk.append(np.broadcast_to(a["moe_router_b"], (P, NE)))
    cols = np.concatenate(pk, 1)

    f = np.arange(P)
    sel = np.zeros((P, NSEQ), np.float32)
    for q in range(4):
        sel[32 * q:32 * q + NSEQ] = np.eye(NSEQ, dtype=np.float32)
    e8 = np.arange(NE)
    rep = lambda r: np.broadcast_to(np.asarray(r, np.float32).reshape(1, -1), (P, np.size(r)))
    cst = np.concatenate([np.eye(P, dtype=np.float32), (f[:, None] < f[None, :]).astype(np.float32), rep(f), sel,
                          rep(e8[None, :] < e8[:, None]), rep(e8), rep(P * np.arange(NBLK))], 1)

    wrg = np.zeros((DEPTH, P, 2, NT, P), np.float32)
    for w, n in enumerate(("rg_wa", "rg_wx")):
        b = a[n].reshape(DEPTH, NT, 2, 64, 64)
        for h in range(2):
            wrg[:, 64 * h:64 * h + 64, w, :, 64 * h:64 * h + 64] = b[:, :, h].transpose(0, 2, 1, 3)
    x = np.concatenate([a["x_prompt"].reshape(TP, D), a["x_sample"].reshape(NB * TS, D)])
    x = x.T.reshape(NT, P, T).transpose(1, 0, 2)
    rc = a["state_rglru_conv"].reshape(DEPTH, NB, PR, NT, P).transpose(0, 4, 3, 1, 2).reshape(DEPTH, P, NT, NB, PR)
    cc = a["state_cconv"].reshape(DEPTH, NB, PC, NT, P).transpose(0, 4, 3, 1, 2).reshape(DEPTH, P, NT, NB, PC)
    arrays = {k: np.ascontiguousarray(v) for k, v in dict(
        stream=stream, ada=ada, moe=moe, cols=cols, cst=cst, wrg=wrg, x=x, rc=rc, cc=cc).items()}

    nc = bacc.Bacc("TRN2", target_bir_lowering=False, num_devices=1)
    ins = [nc.dram_tensor("in_" + k, v.shape, F32, kind="ExternalInput").ap() for k, v in arrays.items()]
    shapes = dict(y=(P, NT, T), h=(DEPTH, P, NT, NSEQ), rc=(DEPTH, P, NT, NSEQ, PR), cc=(DEPTH, P, NT, NSEQ, PC))
    outs = [nc.dram_tensor("out_" + k, s, F32, kind="ExternalOutput").ap() for k, s in shapes.items()]
    build(nc, *ins, *outs)
    r = run_bass_kernel_spmd(nc, [{"in_" + k: v for k, v in arrays.items()}], core_ids=[0]).results[0]
    y = r["out_y"].transpose(2, 1, 0).reshape(T, D)
    h = r["out_h"].transpose(0, 3, 2, 1).reshape(DEPTH, NSEQ, D)
    rco = r["out_rc"].transpose(0, 3, 4, 2, 1).reshape(DEPTH, NSEQ, PR, D)
    cco = r["out_cc"].transpose(0, 3, 4, 2, 1).reshape(DEPTH, NSEQ, PC, D)
    return (y[:TP].reshape(1, TP, D), y[TP:].reshape(NB, TS, D), h[:, :1], rco[:, :1], cco[:, :1], h[:, 1:],
            rco[:, 1:], cco[:, 1:])
```
